# Optimizing a Trainium2 kernel written in Bass

```python
import math
import jax, jax.numpy as jnp
from jax import lax
import numpy as np

D_MODEL = 1024
BATCH = 1
SEQ = 128
DEPTH = 1
DEC_BATCH = 1
DEC_SEQ = 512
PAST_LEN = 256

GRID_W = 64
R_HEADS = 8
R_HEAD = 64
R_WIDTH = R_HEADS * R_HEAD
DECAY_LORA = 64
AAA_LORA = 64
GATE_LORA = 128
LNX_EPS = 64e-5
G_HEADS = 4
G_HEAD = 128
G_WIDTH = G_HEADS * G_HEAD
CONV_K = 3
CHUNK = 64
IN_SIZES = (R_WIDTH, R_WIDTH, R_WIDTH, DECAY_LORA, AAA_LORA, GATE_LORA,
            G_WIDTH, G_WIDTH, G_WIDTH, G_WIDTH, 2 * G_HEADS, 2 * G_HEADS)
IN_COLS = 3 * R_WIDTH + DECAY_LORA + AAA_LORA + GATE_LORA + 4 * G_WIDTH + 4 * G_HEADS
MIX_WIDTH = R_WIDTH + G_WIDTH
N_GROUPS = 4
EXPERTS_PER_GROUP = 8
N_EXPERTS = N_GROUPS * EXPERTS_PER_GROUP
TOP_K = 2
D_EXPERT = 512
MOE_BLOCK = 128
NORM_EPS = 1e-6

kernel_name = 'hybrid_rwkv7_gdn_hmoe_diffusion_step'

def _split_points(sizes):
    pts, acc = [], 0
    for s in sizes[:-1]:
        acc += s
        pts.append(acc)
    return pts

def rms_norm(x, g, eps=NORM_EPS):
    xf = x.astype(jnp.float32)
    y = xf * lax.rsqrt(jnp.mean(xf * xf, -1, keepdims=True) + eps)
    return (y * g.astype(jnp.float32)).astype(x.dtype)

def l2_normalize(x, eps=1e-6):
    xf = x.astype(jnp.float32)
    return xf * lax.rsqrt(jnp.sum(xf * xf, -1, keepdims=True) + eps)

def short_conv(x, w, n_rows):
    B, T, C = x.shape
    xs = x.reshape(B * n_rows, T // n_rows, C)
    pad = (CONV_K - 1) // 2
    y = lax.conv_general_dilated(xs, w[:, None, :].astype(x.dtype), (1,), [(pad, pad)],
                                 dimension_numbers=('NWC', 'WIO', 'NWC'), feature_group_count=C)
    return y.reshape(B, T, C)

def rwkv7_scan(r, w, k, v, a, b, s0, reverse):
    f32 = jnp.float32
    xs = tuple(jnp.moveaxis(t.astype(f32), 1, 0) for t in (r, w, k, v, a, b))

    def step(S, inp):
        r_t, w_t, k_t, v_t, a_t, b_t = inp
        sa = jnp.einsum('bhvk,bhk->bhv', S, a_t)
        S = S * w_t[:, :, None, :] + sa[..., None] * b_t[:, :, None, :] + v_t[..., None] * k_t[:, :, None, :]
        return S, jnp.einsum('bhvk,bhk->bhv', S, r_t)

    S, ys = lax.scan(step, s0.astype(f32), xs, reverse=reverse)
    return jnp.moveaxis(ys, 0, 1), S

def gated_delta_chunked(q, k, v, beta, g, s0):
    B, T, H, K = q.shape
    V = v.shape[-1]
    N = T // CHUNK
    f32 = jnp.float32

    def chunks(t):
        t = t.astype(f32).reshape(B, N, CHUNK, H, *t.shape[3:])
        return jnp.moveaxis(jnp.moveaxis(t, 1, 0), 3, 2)

    qc, kc, vc, bc, gc = chunks(q), chunks(k), chunks(v), chunks(beta), chunks(g)
    G = jnp.cumsum(gc, -1)
    idx = jnp.arange(CHUNK)
    incl = idx[:, None] >= idx[None, :]
    strict = idx[:, None] > idx[None, :]
    decay = jnp.exp(jnp.where(incl, G[..., :, None] - G[..., None, :], -jnp.inf))
    kb = kc * bc[..., None]
    M = jnp.where(strict, jnp.einsum('nbhik,nbhjk->nbhij', kb, kc) * decay, 0.0)
    A = M + jnp.eye(CHUNK, dtype=f32)

    def solve(rhs):
        return lax.linalg.triangular_solve(A, rhs, left_side=True, lower=True, unit_diagonal=True)

    u = solve(vc * bc[..., None])
    w = solve(kb * jnp.exp(G)[..., None])
    qk = jnp.einsum('nbhik,nbhjk->nbhij', qc, kc) * decay
    q_dec = qc * jnp.exp(G)[..., None]
    k_dec = kc * jnp.exp(G[..., -1:] - G)[..., None]
    g_last = jnp.exp(G[..., -1])

    def step(S, inp):
        q_n, k_n, u_n, w_n, qk_n, gl_n = inp
        v_new = u_n - jnp.einsum('bhck,bhkv->bhcv', w_n, S)
        o = jnp.einsum('bhck,bhkv->bhcv', q_n, S) + jnp.einsum('bhij,bhjv->bhiv', qk_n, v_new)
        S = S * gl_n[..., None, None] + jnp.einsum('bhck,bhcv->bhkv', k_n, v_new)
        return S, o

    S, o = lax.scan(step, s0.astype(f32), (q_dec, k_dec, u, w, qk, g_last))
    o = jnp.moveaxis(jnp.moveaxis(o, 2, 3), 0, 1).reshape(B, T, H, V)
    return o, S

def rwkv7_group(r, k, v, wl, al, gl, s0, lp):
    B, T, _ = r.shape
    f32 = jnp.float32
    heads = lambda t: t.reshape(B, T, R_HEADS, R_HEAD)
    gate = jax.nn.sigmoid(gl) @ lp['rwkv_g2']
    wl = jnp.tanh(wl)
    kk = l2_normalize(heads(k * lp['rwkv_k_k']))
    rh, vh = heads(r), heads(v)
    y_scan, bonus, finals = 0.0, 0.0, []
    for d in range(2):
        w_log = -jax.nn.softplus(-(lp['rwkv_w0'][d] + wl @ lp['rwkv_w2'][d]).astype(f32)) - 0.5
        decay = jnp.exp(-jnp.exp(w_log))
        a = jax.nn.sigmoid(lp['rwkv_a0'][d] + al @ lp['rwkv_a2'][d])
        kd = heads(k * (1.0 + (a - 1.0) * lp['rwkv_k_a']))
        yd, sd = rwkv7_scan(rh, heads(decay), kd, vh, -kk, kk * heads(a), s0[:, d], reverse=(d == 1))
        y_scan = y_scan + yd
        bonus = bonus + jnp.sum((rh * kd * lp['rwkv_r_k']).astype(f32), -1, keepdims=True) * vh.astype(f32)
        finals.append(sd.astype(r.dtype))
    mu = jnp.mean(y_scan, -1, keepdims=True)
    var = jnp.mean(jnp.square(y_scan - mu), -1, keepdims=True)
    yn = (y_scan - mu) * lax.rsqrt(var + LNX_EPS)
    yn = yn * lp['rwkv_lnx_g'].astype(f32).reshape(R_HEADS, R_HEAD) + lp['rwkv_lnx_b'].astype(f32).reshape(R_HEADS, R_HEAD)
    out = (yn + bonus).reshape(B, T, R_WIDTH) * gate.astype(f32)
    return out.astype(r.dtype), jnp.stack(finals, 1)

def gdn_group(q, k, v, z, beta_raw, alpha_raw, s0, lp, n_rows):
    B, T, _ = q.shape
    f32 = jnp.float32
    qkv = jax.nn.silu(short_conv(jnp.concatenate([q, k, v], -1), lp['gdn_conv'], n_rows))
    q, k, v = jnp.split(qkv, 3, axis=-1)
    hd = lambda t: t.reshape(B, T, G_HEADS, G_HEAD)
    q = l2_normalize(hd(q)) * (G_HEAD ** -0.5)
    k = l2_normalize(hd(k))
    v = hd(v)
    beta = jax.nn.sigmoid(beta_raw.astype(f32)).reshape(B, T, 2, G_HEADS)
    alpha = alpha_raw.astype(f32).reshape(B, T, 2, G_HEADS)
    flip = lambda t: jnp.flip(t, axis=1)
    o, finals = 0.0, []
    for d in range(2):
        g = -jnp.exp(lp['gdn_a_log'][d].astype(f32)) * jax.nn.softplus(alpha[:, :, d] + lp['gdn_dt_bias'][d].astype(f32))
        if d == 0:
            od, sd = gated_delta_chunked(q, k, v, beta[:, :, 0], g, s0[:, 0])
        else:
            od, sd = gated_delta_chunked(flip(q), flip(k), flip(v), flip(beta[:, :, 1]), flip(g), s0[:, 1])
            od = flip(od)
        o = o + od
        finals.append(sd.astype(z.dtype))
    o = rms_norm(o, lp['gdn_norm_g']) * jax.nn.silu(hd(z).astype(f32))
    return o.reshape(B, T, G_WIDTH).astype(z.dtype), jnp.stack(finals, 1)

def token_mixers(h, lp, s_rwkv0, s_gdn0, n_rows):
    proj = h @ lp['w_in']
    (r, k, v, wl, al, gl, q2, k2, v2, z2, beta_raw, alpha_raw) = jnp.split(proj, _split_points(IN_SIZES), axis=-1)
    o_r, s_r = rwkv7_group(r, k, v, wl, al, gl, s_rwkv0, lp)
    o_g, s_g = gdn_group(q2, k2, v2, z2, beta_raw, alpha_raw, s_gdn0, lp, n_rows)
    out = jnp.concatenate([o_r, o_g], -1) @ lp['w_out']
    return out, s_r, s_g

def hier_moe(h, lp):
    B, T, D = h.shape
    NT = B * T
    f32 = jnp.float32
    x = h.reshape(NT, D)
    grp_p = jax.nn.softmax((x @ lp['router_group_w']).astype(f32) + lp['router_group_b'].astype(f32), -1)
    p_grp, grp = lax.top_k(grp_p, 1)
    e_logits = ((x @ lp['router_expert_w']).astype(f32) + lp['router_expert_b'].astype(f32)).reshape(NT, N_GROUPS, EXPERTS_PER_GROUP)
    in_grp = jnp.take_along_axis(e_logits, grp[:, :, None], axis=1)[:, 0]
    p_in, idx_in = lax.top_k(jax.nn.softmax(in_grp, -1), TOP_K)
    gate = p_grp * p_in / jnp.sum(p_in, -1, keepdims=True)
    expert = grp * EXPERTS_PER_GROUP + idx_in
    A = NT * TOP_K
    flat_e = expert.reshape(A)
    flat_tok = jnp.repeat(jnp.arange(NT, dtype=jnp.int32), TOP_K)
    flat_w = gate.reshape(A)
    order = jnp.argsort(flat_e)
    se = flat_e[order]
    counts = jax.ops.segment_sum(jnp.ones((A,), jnp.int32), flat_e, num_segments=N_EXPERTS)
    padded = (counts + MOE_BLOCK - 1) // MOE_BLOCK * MOE_BLOCK
    ends = jnp.cumsum(counts)
    pends = jnp.cumsum(padded)
    rank = jnp.arange(A, dtype=jnp.int32) - (ends - counts)[se]
    dest = (pends - padded)[se] + rank
    nb = -(-A // MOE_BLOCK) + N_EXPERTS
    P = nb * MOE_BLOCK
    buf_tok = jnp.full((P,), NT, jnp.int32).at[dest].set(flat_tok[order])
    buf_w = jnp.zeros((P,), f32).at[dest].set(flat_w[order])
    blk_e = jnp.minimum(jnp.searchsorted(pends, jnp.arange(nb, dtype=jnp.int32) * MOE_BLOCK, side='right'), N_EXPERTS - 1)
    xb = jnp.concatenate([x, jnp.zeros((1, D), x.dtype)], 0)[buf_tok].reshape(nb, MOE_BLOCK, D)
    wg, wu, wd = lp['expert_gate'], lp['expert_up'], lp['expert_down']

    def expert_block(args):
        xi, e = args
        return (jax.nn.silu(xi @ wg[e]) * (xi @ wu[e])) @ wd[e]

    yb = lax.map(expert_block, (xb, blk_e)).reshape(P, D)
    out = jnp.zeros((NT + 1, D), f32).at[buf_tok].add(yb.astype(f32) * buf_w[:, None])
    return out[:NT].reshape(B, T, D).astype(h.dtype)

def block(x, cond, lp, s_rwkv0, s_gdn0, n_rows):
    mod = jax.nn.silu(cond) @ lp['ada_w'] + lp['ada_b']
    sh1, sc1, g1, sh2, sc2, g2 = jnp.split(mod[:, None, :], 6, axis=-1)
    h = rms_norm(x, lp['norm1_g']) * (1.0 + sc1) + sh1
    mix, s_r, s_g = token_mixers(h, lp, s_rwkv0, s_gdn0, n_rows)
    x = x + g1 * mix
    h = rms_norm(x, lp['norm2_g']) * (1.0 + sc2) + sh2
    x = x + g2 * hier_moe(h, lp)
    return x, s_r, s_g

def setup_inputs(seed: int = 0) -> dict:
    key = jax.random.key(seed)
    kit = iter(jax.random.split(key, 48))

    def nrm(shape, scale):
        return jax.random.normal(next(kit), shape, jnp.float32) * scale

    D, L = D_MODEL, DEPTH
    dt = jnp.exp(jax.random.uniform(next(kit), (L, 2, G_HEADS), jnp.float32, math.log(1e-3), math.log(1e-1)))
    a_log = jnp.log(jax.random.uniform(next(kit), (L, 2, G_HEADS), jnp.float32, 1.0, 16.0))
    return {
        'x_prompt': nrm((BATCH, SEQ, D), 1.0),
        'x_sample': nrm((DEC_BATCH, DEC_SEQ, D), 1.0),
        'state_rwkv': nrm((DEC_BATCH, L, 2, R_HEADS, R_HEAD, R_HEAD), 0.5),
        'state_gdn': nrm((DEC_BATCH, L, 2, G_HEADS, G_HEAD, G_HEAD), 0.1),
        'c': nrm((DEC_BATCH, D), 1.0),
        'c_ctx': nrm((D,), 1.0),
        'ada_w': nrm((L, D, 6 * D), D ** -0.5),
        'ada_b': nrm((L, 6 * D), 0.01),
        'norm1_g': 1.0 + nrm((L, D), 0.02),
        'norm2_g': 1.0 + nrm((L, D), 0.02),
        'w_in': nrm((L, D, IN_COLS), D ** -0.5),
        'w_out': nrm((L, MIX_WIDTH, D), MIX_WIDTH ** -0.5),
        'rwkv_w0': nrm((L, 2, R_WIDTH), 1.0),
        'rwkv_w2': nrm((L, 2, DECAY_LORA, R_WIDTH), 0.5 * DECAY_LORA ** -0.5),
        'rwkv_a0': nrm((L, 2, R_WIDTH), 0.1),
        'rwkv_a2': nrm((L, 2, AAA_LORA, R_WIDTH), AAA_LORA ** -0.5),
        'rwkv_g2': nrm((L, GATE_LORA, R_WIDTH), GATE_LORA ** -0.5),
        'rwkv_k_k': 0.85 + nrm((L, R_WIDTH), 0.05),
        'rwkv_k_a': 1.0 + nrm((L, R_WIDTH), 0.05),
        'rwkv_r_k': nrm((L, R_HEADS, R_HEAD), 0.1),
        'rwkv_lnx_g': 1.0 + nrm((L, R_WIDTH), 0.02),
        'rwkv_lnx_b': nrm((L, R_WIDTH), 0.01),
        'gdn_conv': nrm((L, CONV_K, 3 * G_WIDTH), CONV_K ** -0.5),
        'gdn_a_log': a_log,
        'gdn_dt_bias': dt + jnp.log(-jnp.expm1(-dt)),
        'gdn_norm_g': 1.0 + nrm((L, G_HEAD), 0.02),
        'router_group_w': nrm((L, D, N_GROUPS), D ** -0.5),
        'router_group_b': nrm((L, N_GROUPS), 0.01),
        'router_expert_w': nrm((L, D, N_EXPERTS), D ** -0.5),
        'router_expert_b': nrm((L, N_EXPERTS), 0.01),
        'expert_gate': nrm((L, N_EXPERTS, D, D_EXPERT), D ** -0.5),
        'expert_up': nrm((L, N_EXPERTS, D, D_EXPERT), D ** -0.5),
        'expert_down': nrm((L, N_EXPERTS, D_EXPERT, D), D_EXPERT ** -0.5),
        'final_norm_g': 1.0 + nrm((D,), 0.02),
    }

def reference(x_prompt, x_sample, state_rwkv, state_gdn, c, c_ctx, ada_w, ada_b, norm1_g, norm2_g,
              w_in, w_out, rwkv_w0, rwkv_w2, rwkv_a0, rwkv_a2, rwkv_g2, rwkv_k_k, rwkv_k_a, rwkv_r_k,
              rwkv_lnx_g, rwkv_lnx_b, gdn_conv, gdn_a_log, gdn_dt_bias, gdn_norm_g,
              router_group_w, router_group_b, router_expert_w, router_expert_b,
              expert_gate, expert_up, expert_down, final_norm_g):
    layers = [dict(ada_w=ada_w[l], ada_b=ada_b[l], norm1_g=norm1_g[l], norm2_g=norm2_g[l],
                   w_in=w_in[l], w_out=w_out[l], rwkv_w0=rwkv_w0[l], rwkv_w2=rwkv_w2[l],
                   rwkv_a0=rwkv_a0[l], rwkv_a2=rwkv_a2[l], rwkv_g2=rwkv_g2[l], rwkv_k_k=rwkv_k_k[l],
                   rwkv_k_a=rwkv_k_a[l], rwkv_r_k=rwkv_r_k[l], rwkv_lnx_g=rwkv_lnx_g[l],
                   rwkv_lnx_b=rwkv_lnx_b[l], gdn_conv=gdn_conv[l], gdn_a_log=gdn_a_log[l],
                   gdn_dt_bias=gdn_dt_bias[l], gdn_norm_g=gdn_norm_g[l],
                   router_group_w=router_group_w[l], router_group_b=router_group_b[l],
                   router_expert_w=router_expert_w[l], router_expert_b=router_expert_b[l],
                   expert_gate=expert_gate[l], expert_up=expert_up[l], expert_down=expert_down[l])
              for l in range(DEPTH)]

    xc = x_prompt
    bp = xc.shape[0]
    new_r, new_g = [], []
    for l in range(DEPTH):
        zr = jnp.zeros((bp, 2, R_HEADS, R_HEAD, R_HEAD), xc.dtype)
        zg = jnp.zeros((bp, 2, G_HEADS, G_HEAD, G_HEAD), xc.dtype)
        xc, s_r, s_g = block(xc, c_ctx[None, :], layers[l], zr, zg, 1)
        new_r.append(s_r)
        new_g.append(s_g)
    new_state_rwkv = jnp.stack(new_r, 1)
    new_state_gdn = jnp.stack(new_g, 1)
    y_prompt = rms_norm(xc, final_norm_g)

    n_rows = x_sample.shape[1] // GRID_W
    xl = x_sample
    for l in range(DEPTH):
        xl, _, _ = block(xl, c, layers[l], state_rwkv[:, l], state_gdn[:, l], n_rows)
    y_sample = rms_norm(xl, final_norm_g)
    return (y_prompt, y_sample, new_state_rwkv, new_state_gdn)


_drawn_inputs = setup_inputs


def setup_inputs(seed=0):
    import zlib

    import numpy as np

    out = dict(_drawn_inputs(seed))
    spreads = {}
    factors = {'state_rwkv': 8.0,
     'rwkv_lnx_g': 18.427,
     'rwkv_lnx_b': 25.048,
     'gdn_norm_g': 15.558,
     'router_group_b': 15.089,
     'router_expert_b': 13.227,
     'final_norm_g': 7.995,
     'norm2_g': 3.882,
     'rwkv_k_k': 3.419}
    for name, (base, spread) in spreads.items():
        noise = np.random.default_rng([zlib.crc32(name.encode()), seed]).standard_normal(out[name].shape)
        drawn = base * np.exp(spread * noise) if base else spread * noise
        out[name] = __import__('jax').numpy.asarray(drawn.astype(out[name].dtype))
    for name, factor in factors.items():
        out[name] = (out[name] * factor).astype(out[name].dtype)
    return out
```

```python
from contextlib import ExitStack

import numpy as np

import concourse.bass as bass
from concourse import mybir

F32 = mybir.dt.float32
I32 = mybir.dt.int32
ALU = mybir.AluOpType
ACT = mybir.ActivationFunctionType
AX = mybir.AxisListType

P = 128
D = 1024
KD = D // P
CTX, LAT = 128, 512
TOK = CTX + LAT
NT = TOK // P
HALF = TOK // 2
COLS = 512
ROW = 64
RW = 512
RH, RD = 8, 64
FT = RW // P
GH, GD = 4, 128
IN_COLS = 3856
ADA = 6 * D
ADA_BLOCKS = ADA // COLS
C_R, C_K, C_V, C_LORA, C_Q2, C_K2, C_V2, C_Z, C_BA = 0, 512, 1024, 1536, 1792, 2304, 2816, 3328, 3840
FM_R, FM_K, FM_Q2, FM_K2, FM_V2, FM_LORA = 0, 4, 8, 12, 16, 20
FM_TILES = 22
NORM_EPS = 1e-6
LNX_EPS = 64e-5
DECAY = float(np.exp(-0.5))
LEVELS = 7
NE, GROUPS, PER_GROUP = 32, 4, 8
FE = 512
BT = 64
NB = NE + (2 * TOK - NE) // BT
NB += NB % 2
SLOTS = NB * BT
BIG = 1e30

T_ID, T_ONE, T_BLK, T_MASK, T_LVL, T_EYE, T_SEL, T_HEAD, T_IOTA, T_BIOTA, T_THR, T_END = (
    0, 128, 256, 384, 1408, 3200, 3264, 3520, 3522, 3526, 3526 + NB, 3526 + NB + 10)


def shape_tables():
    t = np.zeros((P, T_END), np.float32)
    r = np.arange(P)
    j, i = r[:, None], r[None, :]
    t[:, T_ID:T_ID + P] = j == i
    t[:, T_ONE:T_ONE + P] = 1
    t[:, T_BLK:T_BLK + P] = j // RD == i // RD
    for d, (strict, incl) in enumerate(((j < i, j <= i), (j > i, j >= i))):
        for n, m in enumerate((strict, incl, strict, incl)):
            t[:, T_MASK + 512 * d + P * n:T_MASK + 512 * d + P * (n + 1)] = m
    for k in range(LEVELS):
        s = 2 ** k
        lower = (j // s == i // s + 1) & (i // s % 2 == 0)
        t[:, T_LVL + P * k:T_LVL + P * (k + 1)] = lower
        t[:, T_LVL + P * (LEVELS + k):T_LVL + P * (LEVELS + k + 1)] = lower.T
    t[:, T_EYE:T_EYE + RD] = j % RD == r[None, :RD]
    for c in range(2):
        t[c, T_SEL + P * c:T_SEL + P * (c + 1)] = 1
    for h in range(2):
        t[:, T_HEAD + h] = r // RD == h
    t[:, T_IOTA:T_IOTA + GROUPS] = r[:GROUPS]
    t[:, T_BIOTA:T_BIOTA + NB] = np.arange(NB)
    t[:, T_THR:T_THR + 10] = BT * np.arange(10)
    return t


class Steps:

    def __init__(self, sem, book, key, loop):
        self.sem, self.loop = sem, loop
        self.book = book.setdefault(key, {"per": 1})
        self.n, self.it = 0, 0

    def open(self):
        return self.sem, self.book["per"]

    def begin(self, it):
        self.it, self.n = it, 0

    def tick(self, name=None):
        self.n += 1
        if name is not None:
            self.book[name] = self.n
        self.book["per"] = max(self.book["per"], self.n)
        return self.sem, 1

    def at(self, name, it=0, back=0):
        v = self.book.get(name, 1)
        return (self.sem, (it + 1 - back) * self.book["per"] + v) if self.loop else (self.sem, v)

    def so_far(self):
        return (self.sem, (self.it + 1) * self.book["per"] + self.n) if self.loop else (self.sem, self.n)


class Stage:
    def __init__(self, ctx, nc, book, name, loop):
        mk = lambda e: Steps(ctx.enter_context(nc.semaphore(f"{name}_{e}")), book, f"{name}_{e}", loop)
        self.pe, self.act, self.dve, self.pool, self.sp = (mk(e) for e in ("pe", "act", "dve", "pool", "sp"))


def program(nc, A, O, book, dbg=None):
    ctx = ExitStack()
    with ctx:
        sb = lambda name, shape, dt=F32: ctx.enter_context(nc.sbuf_tensor(name, shape, dt))
        sem = lambda name: ctx.enter_context(nc.semaphore(name))
        flat = lambda ap: ap.rearrange("p a b -> p (a b)")
        tab = sb("tab", [P, T_END])
        x = sb("x", [P, NT, D])
        modk = sb("modk", [P, 2, 4, D])
        ring = sb("ring", [P, 2, KD, COLS])
        fm = sb("fm", [P, FM_TILES, TOK])
        hT = sb("hT", [P, KD, TOK])
        v_tm = sb("v_tm", [P, NT, RW])
        z_tm = sb("z_tm", [P, NT, RW])
        ba = sb("ba", [P, NT, 16])
        bias_row = sb("bias_row", [P, D])
        small = sb("small", [P, 64])
        par = sb("par", [P, 64])
        cw = sb("cw", [P, 12, 4])
        moda = fm[:, 0:7, :].rearrange("p a b -> p (a b)")[:, 0:4096].rearrange("p (c s n) -> p c s n", c=2, s=2)
        modrow = fm[:, 8:18, :].rearrange("p a b -> p (a b)")[0:2, 0:ADA]
        hrow = z_tm[:, 0:2, :].rearrange("p a b -> p (a b)")
        hrow2 = z_tm[:, 2:4, :].rearrange("p a b -> p (a b)")
        ps = [ctx.enter_context(nc.psum_tensor(f"ps{i}", [P, 512], F32)) for i in range(8)]

        scr = sb("scr", [P, 3, TOK])
        gs = sb("gs", [P, 2, NT, GH, 4])
        gtmp = sb("gtmp", [P, 4, NT, 8])
        bonus = sb("bonus", [P, NT, RH])
        rpar = sb("rpar", [P, FT, 8])
        hst = sb("hst", [P, 16])
        ringf = ring[:, :, :, :].rearrange("p u k n -> p (u k n)")
        hTf = hT[:, :, :].rearrange("p k n -> p (k n)")
        quad = lambda ap, n: ap.rearrange("p (s n) -> p s n", n=n)
        g_kq, g_et, g_eg, g_lt = quad(ringf[:, 0:1024], 256), quad(ringf[:, 1024:1536], P), quad(ringf[:, 1536:2048], P), quad(ringf[:, 2048:2560], P)
        g_qk, g_rhs, g_w = quad(ringf[:, 2560:3584], 256), quad(ringf[:, 3584:4608], 256), quad(ringf[:, 4608:5632], 256)
        i_x, i_xt, i_y = quad(ringf[:, 5632:6144], P), quad(ringf[:, 6144:6656], P), quad(ringf[:, 6656:7168], P)
        g_q1, g_t1 = quad(ringf[:, 7168:7680], P), quad(ringf[:, 7680:8192], P)
        g_state = hTf[:, 0:1024].rearrange("p (d n) -> p d n", d=2)
        g_gb, g_vf = quad(hTf[:, 1024:1536], P), quad(hTf[:, 1536:2048], P)
        g_sc, g_egl = hTf[:, 2048:2064].rearrange("p (s n) -> p s n", n=4), hTf[:, 2064:2068]
        y_g = hTf[:, 2560:5120].rearrange("p (t n) -> p t n", t=NT)

        r_sc = quad(ringf[:, 0:2560], 640)
        r_ar, r_bk = quad(ringf[:, 2560:3072], 256), quad(ringf[:, 3072:3584], P)
        r_rhs, r_w, r_q1 = quad(ringf[:, 3584:4096], P), quad(ringf[:, 4096:4608], P), quad(ringf[:, 4608:4864], P)
        r_t1, r_ktm, r_zn, r_zin = quad(ringf[:, 4864:4992], RD), quad(ringf[:, 4992:5248], RD), quad(ringf[:, 5248:5376], RD), quad(ringf[:, 5376:5504], RD)
        r_eu, r_cs = quad(ringf[:, 7168:7680], P), quad(ringf[:, 7680:7936], P)
        work = fm[:, FM_V2:FM_V2 + 4, :].rearrange("p a b -> p (a b)")
        r_ex, r_pq, r_kd, r_kka = quad(work[:, 0:768], P), quad(work[:, 768:1280], P), quad(work[:, 1280:1536], P), quad(work[:, 1536:1792], P)
        r_rr, r_lw, r_lora = quad(work[:, 1792:2048], P), quad(work[:, 2048:2304], P), quad(work[:, 2304:2560], P)
        lora = hTf[:, 0:1024]
        zst = hTf[:, 1024:1536]
        znat = hTf[:, 1536:2560]
        r_v = quad(ringf[:, 7936:8192], P)
        r_par, r_ht, r_h = hst[:, 0:8], hst[:, 8:10], hst[:, 10:12]
        y_r = fm[:, FM_K2:FM_K2 + 4, :].rearrange("p a b -> p (a b)")

        tl = fm[:, 0:8, :].rearrange("p a b -> p (a b)")
        o_tm, oT, h2, h2T = tl[:, 0:D], quad(tl[:, D:2 * D], P), tl[:, 2 * D:3 * D], quad(tl[:, 3 * D:4 * D], P)
        ta, tb = tl[:, 4 * D:4 * D + 512], tl[:, 4 * D + 512:5 * D]
        cst = fm[:, FM_Q2:FM_Q2 + 4, :].rearrange("p a b -> p (a b)")
        g2w, lnx_g, lnx_b, gng = cst[:, 0:512], cst[:, 512:1024], cst[:, 1024:1536], cst[:, 1536:1664]
        t_st, t_sgl, rtb = cst[:, 1664:1728], cst[:, 1728:1856], cst[:, 1856:1892]
        rw_ = work[:, 0:288].rearrange("p (k n) -> p k n", n=GROUPS + NE)
        lg, el, el2, m8, lt_ = work[:, 288:324], work[:, 324:356], work[:, 356:388], work[:, 388:396], work[:, 396:412]
        wout = ringf.rearrange("p (k n) -> p k n", n=D)
        oh = scr[:, 0, 0:2 * NT * NE].rearrange("p (k t e) -> p k t e", k=2, t=NT)
        ohs = scr[:, 1, 0:NT * NE].rearrange("p (t e) -> p t e", t=NT)
        slotm = scr[:, 1, NT * NE:2 * NT * NE].rearrange("p (t e) -> p t e", t=NT)
        gates = scr[:, 1, 2 * NT * NE:2 * NT * NE + 2 * NT].rearrange("p (t k) -> p t k", k=2)
        slot_f = scr[:, 1, 340:350].rearrange("p (t k) -> p t k", k=2)
        cnt, nblk, pend, base = scr[:, 1, 352:384], scr[:, 1, 384:416], scr[:, 1, 416:448], scr[:, 1, 448:480]
        ebf = scr[:, 1, 480:480 + NB]
        gi = sb("gi", [P, 2 * NT + NT + NB + 1 + NB + 2 + 8], I32)
        zeros = scr[:, 2, 0:256]
        slot_i, tid, eb_i = gi[:, 0:10].rearrange("p (t k) -> p t k", k=2), gi[:, 10:15], gi[:, 15:15 + NB + 1]
        tok_i, idx_u = gi[0:BT, 16 + NB:16 + 2 * NB], gi[0:BT, 16 + 2 * NB:18 + 2 * NB]
        mi8 = gi[:, 18 + 2 * NB:26 + 2 * NB]
        zi = cw[0:NB, :, :].rearrange("p a b -> p (a b)").bitcast(I32)
        e_w = [(ring[:, 0], ring[:, 1], hTf[:, 0:4096].rearrange("p (k n) -> p k n", n=D)),
               tuple(flat(fm[:, :, :])[:, 4096 * i:4096 * (i + 1)].rearrange("p (k n) -> p k n", n=(COLS, COLS, D)[i]) for i in range(3))]
        vf_, zf_ = v_tm[:, :, :].rearrange("p t n -> p (t n)"), z_tm[:, :, :].rearrange("p t n -> p (t n)")
        e_x = [vf_[0:BT, D * u:D * (u + 1)] for u in range(2)]
        e_xT = [zf_[:, 512 * u:512 * (u + 1)].rearrange("p (k n) -> p k n", n=BT) for u in range(2)]
        e_h = [zf_[:, 1024 + 256 * u:1280 + 256 * u] for u in range(2)]
        e_hT = [zf_[:, 1536 + 256 * u:1792 + 256 * u].rearrange("p (c h n) -> p c h n", c=2, h=2) for u in range(2)]
        e_y = [vf_[:, 2048:2560], zf_[:, 2048:2560]]
        h2d = nc.dram_tensor("h2_rows", (TOK, D), F32).ap()
        tokd = nc.dram_tensor("slot_token", (NB * BT, 1), I32).ap()
        yd = nc.dram_tensor("expert_rows", (NB * BT, D), F32).ap()

        ident = tab[:, T_ID:T_ID + P]
        ones = tab[:, T_ONE:T_ONE + P]
        blk64 = tab[:, T_BLK:T_BLK + P]

        tab_in, x_in, c_in, gain_in, par_in = sem("tab_in"), sem("x_in"), sem("c_in"), sem("gain_in"), sem("par_in")
        bias_in = sem("bias_in")
        ring_in = [sem("ring0_in"), sem("ring1_in")]
        ring_used = [sem("ring0_used"), sem("ring1_used")]
        out_done = sem("out_done")

        ST = lambda name, loop: Stage(ctx, nc, book, name, loop)
        s_ada, s_norm, s_fm, s_tm, s_prep = ST("ada", True), ST("norm", False), ST("fm", True), ST("tm", False), ST("prep", False)
        s_conv, s_l2, s_gdn, s_rwkv = ST("conv", True), ST("l2", True), ST("gdn", True), ST("rwkv", True)
        s_kk, s_zs = ST("kk", True), ST("zs", False)
        lora_in, rzero, rstate_in, rstate_out = sem("lora_in"), sem("rzero"), sem("rstate_in"), sem("rstate_out")
        s_tail, s_route, s_fin = ST("tail", True), ST("route", False), ST("fin", False)
        s_moe = ST("moe", True)
        wout_in, cst_in, h2_out, tz_out, tok_out, tok_in = (sem(n) for n in ("wout_in", "cst_in", "h2_out", "tz_out", "tok_out", "tok_in"))
        fin_in = sem("fin_in")
        gu_in, dn_in = [sem("gu0_in"), sem("gu1_in")], [sem("dn0_in"), sem("dn1_in")]
        rows_in, y_out = [sem("rows0_in"), sem("rows1_in")], [sem("y0_out"), sem("y1_out")]
        zeros_ready, yd_zeroed = sem("zeros_ready"), sem("yd_zeroed")
        comb_in = [sem("comb0_in"), sem("comb1_in")]
        waited = sem("waited")
        state_in, state_out, zeroed = sem("state_in"), sem("state_out"), sem("zeroed")

        def lower_mask(d, k):
            return tab[:, T_LVL + P * (LEVELS * d + k):T_LVL + P * (LEVELS * d + k + 1)].bitcast(I32).unsqueeze(1).to_broadcast([P, 2, P])

        def two(ap, n=2):
            return ap.unsqueeze(1).to_broadcast([P, n, ap.shape[-1]])

        def incl(d):
            return tab[:, T_MASK + 512 * d + P:T_MASK + 512 * d + 2 * P]

        def pair(ap, d):
            return ap[:, 2 * d:2 * d + 2, :]

        def inverse_pe(pe, S, T, it, lt):
            for d in range(2):
                pe.wait_ge(*T.dve.at(f"xt0{d}", it))
                for hh in range(2):
                    m = nc.tensor.transpose(ps[6 + d][:, P * hh:P * (hh + 1)], i_xt[:, 2 * d + hh, :], ident)
                m.then_inc(*S.tick(f"x0{d}"))
            for k in range(1, LEVELS):
                for d in range(2):
                    pe.wait_ge(*(T.act.at(f"x0{d}", it) if k == 1 else T.dve.at(f"xt{k - 1}{d}", it)))
                    for hh in range(2):
                        s_ = 2 * d + hh
                        m = nc.tensor.matmul(ps[d][:, P * hh:P * (hh + 1)], lt(s_), i_x[:, s_, :], start=True, stop=True)
                    m.then_inc(*S.tick(f"y{k}{d}"))
                for d in range(2):
                    pe.wait_ge(*T.act.at(f"y{k}{d}", it))
                    if k < LEVELS - 1:
                        for hh in range(2):
                            s_ = 2 * d + hh
                            m = nc.tensor.matmul(ps[2 + d][:, P * hh:P * (hh + 1)], i_xt[:, s_, :], i_y[:, s_, :], start=True, stop=True)
                        m.then_inc(*S.tick(f"x{k}{d}"))
                    for hh in range(2):
                        s_ = 2 * d + hh
                        m = nc.tensor.matmul(ps[4 + d][:, P * hh:P * (hh + 1)], i_y[:, s_, :], i_xt[:, s_, :], start=True, stop=True)
                    m.then_inc(*S.tick(f"xt{k}{d}"))

        def inverse_act(act, S, T, it):
            for d in range(2):
                act.wait_ge(*T.pe.at(f"x0{d}", it))
                nc.scalar.copy(pair(i_x, d), ps[6 + d][:, 0:256].rearrange("p (s n) -> p s n", n=P)).then_inc(*S.tick(f"x0{d}"))
            for k in range(1, LEVELS):
                for d in range(2):
                    act.wait_ge(*T.pe.at(f"y{k}{d}", it))
                    nc.scalar.copy(pair(i_y, d), ps[d][:, 0:256].rearrange("p (s n) -> p s n", n=P)).then_inc(*S.tick(f"y{k}{d}"))

        def inverse_dve_start(dve, S, d, lt2):
            m0 = tab[:, T_LVL + P * LEVELS * (1 - d):T_LVL + P * LEVELS * (1 - d) + P]
            nc.vector.tensor_tensor(pair(i_xt, d), lt2, two(m0), ALU.mult).then_inc(*S.tick())
            dve.wait_ge(*S.so_far())
            nc.vector.tensor_tensor(pair(i_xt, d), pair(i_xt, d), two(ident), ALU.add).then_inc(*S.tick(f"xt0{d}"))

        def inverse_dve(dve, S, T, it):
            for d in range(2):
                dve.wait_ge(*T.act.at(f"x0{d}", it))
            for k in range(1, LEVELS):
                for d in range(2):
                    if k < LEVELS - 1:
                        dve.wait_ge(*T.pe.at(f"x{k}{d}", it))
                        dve.sem_inc(waited, 1)
                        nc.vector.copy_predicated(pair(i_x, d), lower_mask(d, k), ps[2 + d][:, 0:256].rearrange("p (s n) -> p s n", n=P)).then_inc(*S.tick(f"x{k}{d}"))
                    dve.wait_ge(*T.pe.at(f"xt{k}{d}", it))
                    dve.sem_inc(waited, 1)
                    nc.vector.copy_predicated(pair(i_xt, d), lower_mask(1 - d, k), ps[4 + d][:, 0:256].rearrange("p (s n) -> p s n", n=P)).then_inc(*S.tick(f"xt{k}{d}"))

        silc = par[:, 0:16].rearrange("p (k c) -> p k c", c=2)
        craw = par[:, 16:32].rearrange("p (c k) -> p c k", c=2)
        cexp = par[:, 32:48].rearrange("p (c k) -> p c k", c=2)
        ssq, std, rstd = small[:, 0:NT], small[:, 8:8 + NT], small[:, 16:16 + NT]

        ada_d = A["ada_w"][0].rearrange("(k p) n -> p k n", p=P)
        win_d = A["w_in"][0].rearrange("(k p) n -> p k n", p=P)
        FM_USES = 4
        A_USES = ADA_BLOCKS // 2

        ctx.enter_context(nc.allow_non_contiguous_dma(reason="short per-feature parameter vectors"))
        block = ctx.enter_context(nc.Block())

        def comb(k):
            return tl[:, D * k:D * (k + 1)]


        @block.sync
        def _(sp):
            sp.dma_start(tab[:, :], A["tables"]).then_inc(tab_in, 16)
            sp.dma_start(craw[:, 0, :], A["c_ctx"].rearrange("(k p) -> p k", p=P)).then_inc(c_in, 16)
            sp.dma_start(craw[:, 1, :], A["c"][0].rearrange("(k p) -> p k", p=P)).then_inc(c_in, 16)
            for u in range(2):
                sp.dma_start(ring[:, u], ada_d[:, :, COLS * u:COLS * (u + 1)]).then_inc(ring_in[u], 16)
            sp.dma_start(modrow, A["ada_b"][0].partition_broadcast(2)).then_inc(bias_in, 16)
            sp.dma_start(x[:, 0, :], A["x_prompt"][0]).then_inc(x_in, 16)
            sp.dma_start(x[:, 1:, :], A["x_sample"][0].rearrange("(t p) d -> p t d", p=P)).then_inc(x_in, 16)
            sp.dma_start(bias_row[:, :], A["norm1_g"][0].partition_broadcast(P)).then_inc(gain_in, 16)
            for w in range(3):
                sp.dma_start(cw[:, :, w], A["gdn_conv"][0, w].rearrange("(t p) -> p t", p=P)).then_inc(par_in, 16)
            sp.dma_start(par[:, 48:56], A["gdn_a_log"][0].rearrange("d h -> (d h)").partition_broadcast(P)).then_inc(par_in, 16)
            sp.dma_start(par[:, 56:64], A["gdn_dt_bias"][0].rearrange("d h -> (d h)").partition_broadcast(P)).then_inc(par_in, 16)
            for d in range(2):
                sp.dma_start(rpar[:, :, d], A["rwkv_w0"][0, d].rearrange("(f p) -> p f", p=P)).then_inc(par_in, 16)
                sp.dma_start(rpar[:, :, 2 + d], A["rwkv_a0"][0, d].rearrange("(f p) -> p f", p=P)).then_inc(par_in, 16)
            sp.dma_start(rpar[:, :, 4], A["rwkv_k_k"][0].rearrange("(f p) -> p f", p=P)).then_inc(par_in, 16)
            sp.dma_start(rpar[:, :, 5], A["rwkv_k_a"][0].rearrange("(f p) -> p f", p=P)).then_inc(par_in, 16)
            sp.dma_start(rpar[:, :, 7], A["rwkv_r_k"][0].rearrange("(f a) k -> (a k) f", a=2)).then_inc(par_in, 16)
            with sp.Fori(1, A_USES) as j:
                for u in range(2):
                    sp.wait_ge(ring_used[u], j)
                    sp.dma_start(ring[:, u], ada_d[:, :, bass.ds(j * 2 * COLS + COLS * u, COLS)]).then_inc(ring_in[u], 16)
            with sp.Fori(0, 2) as j:
                for u in range(2):
                    sp.wait_ge(ring_used[u], j + A_USES)
                    sp.dma_start(ring[:, u], win_d[:, :, bass.ds(j * C_Q2 + COLS * u, COLS)]).then_inc(ring_in[u], 16)
            for n, (c0, nc_) in enumerate(((C_V2, 512), (C_LORA, 256), (C_V, 512), (C_Z, 512), (C_BA, 16))):
                u = n % 2
                sp.wait_ge(ring_used[u], A_USES + 2 + n // 2)
                sp.dma_start(ring[:, u, :, 0:nc_], win_d[:, :, c0:c0 + nc_]).then_inc(ring_in[u], 16)
            sp.wait_ge(zeros_ready, 1)
            sp.dma_start(yd.rearrange('(p a) (b n) -> p (a b) n', p=P, n=256), zeros.unsqueeze(1).to_broadcast([P, NB * BT * D // (P * 256), 256])).then_inc(yd_zeroed, 16)
            g_dram = lambda ap: ap.rearrange("d h k v -> k d h v")
            g_sb = g_state.rearrange("p d (h v) -> p d h v", h=GH)
            sp.wait_ge(*s_gdn.dve.at("state", 1))
            sp.dma_start(g_dram(O["new_gdn"][0, 0]), g_sb).then_inc(state_out, 16)
            sp.wait_ge(state_out, 16)
            for d in range(2):
                sp.dma_start(g_sb[:, d], A["state_gdn"][0, 0, d].rearrange("h k v -> k h v")).then_inc(state_in, 16)
            sp.wait_ge(*s_gdn.dve.at("state", 2 * NT - 1))
            for d in range(2):
                sp.dma_start(lora[0:64, RW * d:RW * (d + 1)], A["rwkv_w2"][0, d]).then_inc(lora_in, 16)
                sp.dma_start(lora[64:128, RW * d:RW * (d + 1)], A["rwkv_a2"][0, d]).then_inc(lora_in, 16)
            z_dram = lambda ap: ap.rearrange("d h v k -> v (d h) k")
            z_sb = znat[0:RD, :].rearrange("v (n k) -> v n k", k=RD)
            sp.wait_ge(*s_zs.act.at("znat"))
            sp.dma_start(z_dram(O["new_rwkv"][0, 0]), z_sb).then_inc(rstate_out, 16)
            sp.wait_ge(rstate_out, 16)
            sp.dma_start(z_sb, z_dram(A["state_rwkv"][0, 0])).then_inc(rstate_in, 16)
            sp.wait_ge(*s_rwkv.dve.at("last", NT * FT - 1))
            sp.dma_start(wout, A["w_out"][0].rearrange("(k p) n -> p k n", p=P)).then_inc(wout_in, 16)
            sp.dma_start(g2w, A["rwkv_g2"][0]).then_inc(cst_in, 16)
            sp.dma_start(lnx_g, A["rwkv_lnx_g"][0].partition_broadcast(P)).then_inc(cst_in, 16)
            sp.dma_start(lnx_b, A["rwkv_lnx_b"][0].partition_broadcast(P)).then_inc(cst_in, 16)
            sp.dma_start(gng, A["gdn_norm_g"][0].partition_broadcast(P)).then_inc(cst_in, 16)
            sp.dma_start(rw_[:, :, 0:GROUPS], A["router_group_w"][0].rearrange("(k p) n -> p k n", p=P)).then_inc(cst_in, 16)
            sp.dma_start(rw_[:, :, GROUPS:], A["router_expert_w"][0].rearrange("(k p) n -> p k n", p=P)).then_inc(cst_in, 16)
            sp.dma_start(rtb[:, 0:GROUPS], A["router_group_b"][0].partition_broadcast(P)).then_inc(cst_in, 16)
            sp.dma_start(rtb[:, GROUPS:], A["router_expert_b"][0].partition_broadcast(P)).then_inc(cst_in, 16)
            sp.dma_start(bias_row[:, :], A["norm2_g"][0].partition_broadcast(P)).then_inc(cst_in, 16)
            sp.wait_ge(*s_route.pool.at("zi"))
            sp.dma_start(tokd.rearrange("(b s) o -> b (s o)", b=NB)[:, 0:48], zi[:, 0:48]).then_inc(tz_out, 16)
            sp.dma_start(tokd.rearrange("(b s) o -> b (s o)", b=NB)[:, 48:64], zi[:, 0:16]).then_inc(tz_out, 16)
            for it0, it1 in ((0, 1), (1, NT)):
                with sp.Fori(it0, it1) as t:
                    sp.wait_ge(*s_tail.dve.at("h2", t))
                    sp.dma_start(h2d[bass.ds(t * P, P), :], h2).then_inc(h2_out, 16)
            sp.wait_ge(tok_out, 16 * 2 * NT)
            sp.dma_start(tok_i, tokd.rearrange("(b s) o -> s (b o)", s=BT)).then_inc(tok_in, 16)
            sp.wait_ge(*s_route.dve.at("eb"))
            n_blocks = sp.value_load(eb_i[0:1, NB:NB + 1], min_val=0, max_val=NB)
            eg = A["expert_gate"].rearrange("l e (k p) n -> p (l e k) n", p=P)
            eu = A["expert_up"].rearrange("l e (k p) n -> p (l e k) n", p=P)
            ed = A["expert_down"].rearrange("l e (k p) n -> p (l e k) n", p=P)
            sp.sem_inc(*s_moe.sp.open())
            with sp.Fori(0, NB // 2) as j:
                for u in range(2):
                    with sp.If(j * 2 + u < n_blocks):
                        e = sp.value_load(eb_i[0:1, bass.ds(j * 2 + u, 1)], min_val=0, max_val=NE - 1)
                        sp.wait_ge(*s_moe.pe.at(f"up{u}", j, 1))
                        sp.dma_start(e_w[u][0], eg[:, bass.ds(e * KD, KD), :]).then_inc(gu_in[u], 16)
                        sp.dma_start(e_w[u][1], eu[:, bass.ds(e * KD, KD), :]).then_inc(gu_in[u], 16)
                        sp.wait_ge(*s_moe.pe.at(f"down{u}", j, 1))
                        sp.dma_start(e_w[u][2], ed[:, bass.ds(e * 4, 4), :]).then_inc(dn_in[u], 16)
                    sp.end_ifs()
            sp.wait_ge(*s_route.dve.at("eb"))
            sp.dma_start(bias_row[:, :], A["final_norm_g"].partition_broadcast(P)).then_inc(fin_in, 16)
            for t in range(NT):
                sp.wait_ge(*s_fin.dve.at(f"out{t}"))
                dst = O["y_prompt"][0] if t == 0 else O["y_sample"][0, P * (t - 1):P * t, :]
                sp.dma_start(dst, x[:, t, :]).then_inc(out_done, 16)
            sp.wait_ge(out_done, 16 * NT)

        @block.tensor
        def _(pe):
            S = s_ada.pe
            pe.sem_inc(*S.open())
            pe.wait_ge(tab_in, 16)
            pe.wait_ge(*s_norm.dve.at("silc"))
            with pe.Fori(0, A_USES) as j:
                S.begin(j)
                for u in range(2):
                    pe.wait_ge(ring_in[u], j * 16 + 16)
                    pe.wait_ge(*s_ada.dve.at(f"row{u}", j, 1))
                    for k in range(KD):
                        m = nc.tensor.matmul(ps[u][0:2, :], silc[:, k, :], ring[:, u, k, :], start=k == 0, stop=k == KD - 1)
                    m.then_inc(ring_used[u], 1)
                for u in range(2):
                    pe.wait_ge(*s_ada.dve.at(f"row{u}", j))
                    pe.wait_ge(*s_ada.act.at(f"bc{u}1", j, 1))
                    for c in range(2):
                        nc.tensor.matmul(ps[2 + 2 * u + c][:, :], tab[0:2, T_SEL + P * c:T_SEL + P * (c + 1)],
                                         modrow[:, bass.ds(j * 2 * COLS + COLS * u, COLS)], start=True, stop=True
                                         ).then_inc(*S.tick(f"bc{u}{c}"))
            S = s_norm.pe
            pe.wait_ge(*s_ada.act.at("bc11", A_USES - 1))
            for t in range(NT):
                pe.wait_ge(*s_norm.dve.at(f"h{t}"))
                for b in range(2):
                    if t:
                        pe.wait_ge(*s_norm.act.at(f"hT{t - 1}{b}"))
                    for k in range(4):
                        m = nc.tensor.transpose(ps[b][:, P * k:P * (k + 1)], (hrow if t % 2 == 0 else hrow2)[:, P * (4 * b + k):P * (4 * b + k + 1)], ident)
                    m.then_inc(*S.tick(f"hT{t}{b}"))
            S = s_fm.pe
            pe.sem_inc(*S.open())
            pe.wait_ge(*s_norm.act.at(f"hT{NT - 1}1"))

            def fm_tile(job, u, ct):
                for g in range(2):
                    for k in range(KD):
                        m = nc.tensor.matmul(ps[2 * (job % 2) + g][:, 0:HALF], ring[:, u, k, P * ct:P * (ct + 1)],
                                             hT[:, k, HALF * g:HALF * (g + 1)], start=k == 0, stop=k == KD - 1)
                return m

            with pe.Fori(0, 2) as j:
                S.begin(j)
                for job in range(8):
                    u, ct = divmod(job, 4)
                    if ct == 0:
                        pe.wait_ge(ring_in[u], j * 16 + 16 * (A_USES + 1))
                    pe.wait_ge(*s_fm.act.at(f"a{(job - 2) % 8}", j, 1 if job < 2 else 0))
                    pe.wait_ge(*s_fm.dve.at(f"d{(job - 2) % 8}", j, 1 if job < 2 else 0))
                    m = fm_tile(job, u, ct)
                    m.then_inc(*S.tick(f"p{job}"))
                    if ct == 3:
                        pe.wait_ge(*S.so_far())
                        pe.sem_inc(ring_used[u], 1)
            S = s_tm.pe
            for job in range(6):
                u, ct = divmod(job, 4)
                if ct == 0:
                    pe.wait_ge(ring_in[u], 16 * (A_USES + 3))
                if job < 2:
                    pe.wait_ge(*s_fm.act.at(f"a{6 + job}", 1))
                    pe.wait_ge(*s_fm.dve.at(f"d{6 + job}", 1))
                else:
                    pe.wait_ge(*s_tm.act.at(f"a{job - 2}"))
                    pe.wait_ge(*s_tm.dve.at(f"d{job - 2}"))
                fm_tile(job, u, ct).then_inc(*S.tick(f"p{job}"))
                if job in (3, 5):
                    pe.wait_ge(*S.so_far())
                    pe.sem_inc(ring_used[u], 1)
            for n, (w, nc_) in enumerate((("v", 512), ("z", 512), ("ba", 16))):
                u = n % 2
                pe.wait_ge(ring_in[u], 16 * (A_USES + 4 + n // 2))
                for t in range(NT):
                    q = n * NT + t
                    if q >= 4:
                        pe.wait_ge(*s_tm.act.at(f"t{q - 4}"))
                    for k in range(KD):
                        m = nc.tensor.matmul(ps[4 + q % 4][:, 0:nc_], hT[:, k, P * t:P * (t + 1)], ring[:, u, k, 0:nc_],
                                             start=k == 0, stop=k == KD - 1)
                    m.then_inc(*S.tick(f"t{q}"))
                pe.wait_ge(*S.so_far())
                pe.sem_inc(ring_used[u], 1)
            S = s_prep.pe
            pe.wait_ge(*s_prep.dve.at("g"))
            pe.wait_ge(*s_tm.act.at(f"t{3 * NT - 1}"))
            for d in range(2):
                m = nc.tensor.matmul(ps[7][:, 32 * d:32 * d + 20], incl(d), gtmp[:, 2, :, 4 * d:4 * d + 4], start=True, stop=True)
            m.then_inc(*S.tick("G"))
            S = s_l2.pe
            pe.sem_inc(*S.open())
            def l2_pe(it, weight):
                S.begin(it)
                pe.wait_ge(*s_l2.act.at("sq", it))
                pe.wait_ge(*s_l2.dve.at("eps", it, 1))
                for g in range(2):
                    m = nc.tensor.matmul(ps[g][:, 0:HALF], weight, scr[:, 0, HALF * g:HALF * (g + 1)], start=True, stop=True)
                m.then_inc(*S.tick("ss"))
            with pe.Fori(0, 8) as j:
                l2_pe(j, ones)
            pe.wait_ge(*s_prep.act.at("negeg"))
            pe.wait_ge(*s_l2.dve.at("eps", 7))
            S = s_gdn.pe
            pe.sem_inc(*S.open())

            def gdn_pe(it, hp, tiles):
                S.begin(it)
                pe.wait_ge(*s_gdn.pool.at("copies", it))
                pe.wait_ge(*s_gdn.dve.at("state", it, 1))
                for s_ in range(4):
                    m = nc.tensor.matmul(ps[0][:, P * s_:P * (s_ + 1)], g_gb[:, s_, :], incl(s_ // 2), start=True, stop=True)
                m.then_inc(*S.tick("grow"))
                for s_ in range(4):
                    m = nc.tensor.matmul(ps[1 + s_ // 2][:, 256 * (s_ % 2):256 * (s_ % 2 + 1)], g_kq[:, s_, 0:P], g_kq[:, s_, :], start=True, stop=True)
                m.then_inc(*S.tick("scores"))
                for s_ in range(4):
                    m = nc.tensor.transpose(ps[3][:, P * s_:P * (s_ + 1)], g_kq[:, s_, 0:P], ident)
                m.then_inc(*S.tick("ktm"))
                for s_ in range(4):
                    m = nc.tensor.transpose(ps[4][:, P * s_:P * (s_ + 1)], g_vf[:, s_, :], ident)
                m.then_inc(*S.tick("vtm"))
                pe.wait_ge(*s_gdn.dve.at("qk", it))
                pe.wait_ge(*s_gdn.act.at("vtm", it))
                pe.wait_ge(*s_gdn.act.at("eg", it))
                inverse_pe(pe, S, s_gdn, it, lambda s_: g_lt[:, s_, :])
                for d in range(2):
                    pe.wait_ge(*s_gdn.dve.at(f"xt{LEVELS - 1}{d}", it))
                    for hh in range(2):
                        m = nc.tensor.matmul(ps[6 + d][:, 256 * hh:256 * (hh + 1)], i_xt[:, 2 * d + hh, :], g_rhs[:, 2 * d + hh, :], start=True, stop=True)
                    m.then_inc(*S.tick(f"w{d}"))
                for d in range(2):
                    pe.wait_ge(*s_gdn.act.at(f"w{d}", it))
                    for hh in range(2):
                        m = nc.tensor.matmul(ps[d][:, 256 * hh:256 * (hh + 1)], g_w[:, 2 * d + hh, 0:P], g_qk[:, 2 * d + hh, :], start=True, stop=True)
                    m.then_inc(*S.tick(f"c{d}"))
                pe.wait_ge(*s_gdn.dve.at("t1", it))
                for s_ in range(4):
                    st = g_state[:, s_ // 2, bass.ds(hp * 256 + P * (s_ % 2), P)]
                    nc.tensor.matmul(ps[2][:, P * s_:P * (s_ + 1)], g_qk[:, s_, 0:P], g_w[:, s_, P:2 * P], start=True, stop=False)
                    m = nc.tensor.matmul(ps[2][:, P * s_:P * (s_ + 1)], g_q1[:, s_, :], st, start=False, stop=True)
                m.then_inc(*S.tick("y"))
                for s_ in range(4):
                    st = g_state[:, s_ // 2, bass.ds(hp * 256 + P * (s_ % 2), P)]
                    nc.tensor.matmul(ps[3][:, P * s_:P * (s_ + 1)], g_qk[:, s_, P:2 * P], g_w[:, s_, P:2 * P], start=True, stop=False)
                    m = nc.tensor.matmul(ps[3][:, P * s_:P * (s_ + 1)], g_t1[:, s_, :], st, start=False, stop=True)
                m.then_inc(*S.tick("t2"))

            pe.wait_ge(zeroed, 3)
            with pe.Fori(0, 2) as hp:
                gdn_pe(hp, hp, (0, 0))
            pe.wait_ge(state_in, 32)
            with pe.Fori(1, NT) as n:
                with pe.Fori(0, 2) as hp:
                    gdn_pe(n * 2 + hp, hp, (n, NT - n))
            S = s_kk.pe
            pe.sem_inc(*S.open())
            with pe.Fori(0, FT) as j:
                S.begin(j)
                pe.wait_ge(*s_kk.act.at("sq", j))
                pe.wait_ge(*s_kk.dve.at("eps", j, 1))
                for g in range(2):
                    m = nc.tensor.matmul(ps[g][:, 0:HALF], blk64, scr[:, 0, HALF * g:HALF * (g + 1)], start=True, stop=True)
                m.then_inc(*S.tick("ss"))
            S = s_rwkv.pe
            pe.sem_inc(*S.open())
            pe.wait_ge(*s_kk.dve.at("eps", FT - 1))
            pe.wait_ge(rzero, 2)

            def rwkv_pe(it, ft, tiles):
                S.begin(it)
                pe.wait_ge(*s_rwkv.pool.at("copies", it))
                pe.wait_ge(*s_rwkv.dve.at("last", it, 1))
                for d in range(2):
                    nc.tensor.matmul(ps[0][:, P * d:P * (d + 1)], r_lora[0:64, d, :], r_lw[0:64, d, :], start=True, stop=True)
                    m = nc.tensor.matmul(ps[1][:, P * d:P * (d + 1)], r_lora[64:128, d, :], r_lw[64:128, d, :], start=True, stop=True)
                m.then_inc(*S.tick("u"))
                pe.wait_ge(*s_rwkv.pool.at("rr", it))
                for d in range(2):
                    m = nc.tensor.matmul(ps[7][:, 256 + 2 * d:258 + 2 * d], r_rr[:, d, :], tab[:, T_HEAD:T_HEAD + 2], start=True, stop=True)
                pe.wait_ge(*s_rwkv.dve.at("bk", it))
                for d in range(2):
                    for half in range(2):
                        for hh in range(2):
                            rows = slice(RD * hh, RD * (hh + 1))
                            m = nc.tensor.matmul(ps[2 + 2 * d + hh][:, 256 * half:256 * (half + 1)], r_bk[rows, 2 * half + d, :], r_ar[rows, d, :], start=True, stop=True)
                    m.then_inc(*S.tick(f"scores{d}"))
                for n in range(4):
                    m = nc.tensor.transpose(ps[6][:, P * n:P * (n + 1)], r_bk[:, n, :], ident)
                m.then_inc(*S.tick("bktm"))
                for d in range(2):
                    m = nc.tensor.transpose(ps[7][:, P * d:P * (d + 1)], r_ar[:, d, 0:P], ident)
                m.then_inc(*S.tick("atm"))
                pe.wait_ge(*s_rwkv.act.at("tm", it))
                pe.wait_ge(*s_rwkv.dve.at("bonus", it))
                for s_ in range(4):
                    v = r_v[:, s_ // 2, RD * (s_ % 2):RD * (s_ % 2 + 1)]
                    m = nc.tensor.matmul(ps[0][:, RD * s_:RD * (s_ + 1)], r_sc[:, s_, 320:448], v, start=True, stop=True)
                m.then_inc(*S.tick("akv"))
                pe.wait_ge(*s_rwkv.act.at("akv", it))
                inverse_pe(pe, S, s_rwkv, it, lambda s_: r_sc[:, s_, 0:P])
                for d in range(2):
                    pe.wait_ge(*s_rwkv.dve.at(f"xt{LEVELS - 1}{d}", it))
                    for hh in range(2):
                        s_ = 2 * d + hh
                        m = nc.tensor.matmul(ps[6 + d][:, P * hh:P * (hh + 1)], i_xt[:, s_, :], r_rhs[:, s_, :], start=True, stop=True)
                    m.then_inc(*S.tick(f"w{d}"))
                for d in range(2):
                    pe.wait_ge(*s_rwkv.act.at(f"w{d}", it))
                    for hh in range(2):
                        m = nc.tensor.matmul(ps[d][RD * hh:RD * (hh + 1), 0:192], r_w[:, 2 * d + hh, 0:RD], r_sc[:, 2 * d + hh, P:P + 192], start=True, stop=True)
                    m.then_inc(*S.tick(f"c{d}"))
                pe.wait_ge(*s_rwkv.dve.at("t1", it))
                for d in range(2):
                    for hh in range(2):
                        s_ = 2 * d + hh
                        v = r_v[:, d, RD * hh:RD * (hh + 1)]
                        rows = slice(RD * hh, RD * (hh + 1))
                        yo = ps[(2, 5)[hh]][:, RD * d:RD * (d + 1)]
                        nc.tensor.matmul(yo, r_sc[:, s_, P:2 * P], r_w[:, s_, RD:P], start=True, stop=False)
                        nc.tensor.matmul(yo, r_sc[:, s_, 448:576], v, start=False, stop=False)
                        m = nc.tensor.matmul(yo, r_q1[rows, d, :], r_zin[rows, d, :], start=False, stop=True)
                m.then_inc(*S.tick("y"))
                for d in range(2):
                    for hh in range(2):
                        s_ = 2 * d + hh
                        v = r_v[:, d, RD * hh:RD * (hh + 1)]
                        rows = slice(RD * hh, RD * (hh + 1))
                        zo = ps[3 + hh][rows, RD * d:RD * (d + 1)]
                        nc.tensor.matmul(zo, r_sc[:, s_, 256:320], r_w[:, s_, RD:P], start=True, stop=False)
                        nc.tensor.matmul(zo, r_ktm[:, s_, :], v, start=False, stop=False)
                        m = nc.tensor.matmul(zo, r_t1[rows, d, :], r_zin[rows, d, :], start=False, stop=True)
                m.then_inc(*S.tick("t2"))

            with pe.Fori(0, FT) as ft:
                rwkv_pe(ft, ft, (0, 0))
            Z = s_zs.pe
            pe.wait_ge(*s_rwkv.dve.at("last", FT - 1))
            for n in range(8):
                m = nc.tensor.transpose(ps[n // 4][0:RD, P * (n % 4):P * (n % 4 + 1)], zst[:, RD * n:RD * (n + 1)], ident)
            m.then_inc(*Z.tick("out"))
            pe.wait_ge(rstate_in, 16)
            pe.wait_ge(*s_zs.act.at("znat"))
            for n in range(8):
                m = nc.tensor.transpose(ps[0][:, RD * n:RD * (n + 1)], znat[0:RD, P * n:P * (n + 1)], ident[0:RD, 0:RD])
            m.then_inc(*Z.tick("in"))
            pe.wait_ge(*s_zs.act.at("zst"))
            with pe.Fori(1, NT) as n:
                with pe.Fori(0, FT) as ft:
                    rwkv_pe(n * FT + ft, ft, (n, NT - n))
            S = s_tail.pe
            pe.sem_inc(*S.open())
            pe.wait_ge(wout_in, 16)
            pe.wait_ge(cst_in, 16 * 9)

            def tail_pe(it):
                S.begin(it)
                pe.wait_ge(*s_tail.dve.at("sgl", it))
                nc.tensor.matmul(ps[0][:, :], t_sgl, g2w, start=True, stop=True).then_inc(*S.tick("gate"))
                pe.wait_ge(*s_tail.dve.at("o", it))
                for b in range(2):
                    for k in range(4):
                        m = nc.tensor.transpose(ps[1 + b][:, P * k:P * (k + 1)], o_tm[:, P * (4 * b + k):P * (4 * b + k + 1)], ident)
                    m.then_inc(*S.tick(f"oT{b}"))
                pe.wait_ge(*s_tail.act.at("oT1", it))
                for b in range(2):
                    for k in range(KD):
                        m = nc.tensor.matmul(ps[3 + b][:, :], oT[:, k, :], wout[:, k, 512 * b:512 * (b + 1)], start=k == 0, stop=k == KD - 1)
                    m.then_inc(*S.tick(f"mix{b}"))
                pe.wait_ge(*s_tail.dve.at("h2", it))
                for b in range(2):
                    for k in range(4):
                        m = nc.tensor.transpose(ps[5 + b][:, P * k:P * (k + 1)], h2[:, P * (4 * b + k):P * (4 * b + k + 1)], ident)
                    m.then_inc(*S.tick(f"h2T{b}"))
                pe.wait_ge(*s_tail.act.at("h2T1", it))
                for k in range(KD):
                    m = nc.tensor.matmul(ps[7][:, 0:GROUPS + NE], h2T[:, k, :], rw_[:, k, :], start=k == 0, stop=k == KD - 1)
                m.then_inc(*S.tick("logits"))

            tail_pe(0)
            with pe.Fori(1, NT) as t:
                tail_pe(t)
            S = s_route.pe
            pe.wait_ge(*s_tail.dve.at("last", NT - 1))
            for t in range(NT):
                for q in range(t + 1):
                    m = nc.tensor.matmul(ps[0][:, NE * t:NE * (t + 1)], tab[:, T_MASK:T_MASK + P] if q == t else ones, ohs[:, q, :], start=q == 0, stop=q == t)
            for q in range(NT):
                m = nc.tensor.matmul(ps[0][:, NE * NT:NE * (NT + 1)], ones, ohs[:, q, :], start=q == 0, stop=q == NT - 1)
            m.then_inc(*S.tick("rank"))
            pe.wait_ge(*s_route.dve.at("eb"))
            n_blocks = pe.value_load(eb_i[0:1, NB:NB + 1], min_val=0, max_val=NB)
            S = s_moe.pe
            pe.sem_inc(*S.open())
            with pe.Fori(0, NB // 2) as j:
                S.begin(j)
                for u in range(2):
                    with pe.If(j * 2 + u < n_blocks):
                        wg, wu, wd = e_w[u]
                        pe.wait_ge(rows_in[u], j * 16 + 16)
                        pe.wait_ge(*s_moe.act.at(f"xT{u}", j, 1))
                        pe.sem_inc(waited, 1)
                        for k in range(KD):
                            m = nc.tensor.transpose(ps[u][:, BT * k:BT * (k + 1)], e_x[u][:, P * k:P * (k + 1)], ident[0:BT, 0:BT])
                        m.then_inc(*S.tick(f"xT{u}"))
                        pe.wait_ge(*s_moe.act.at(f"xT{u}", j))
                        pe.wait_ge(gu_in[u], j * 32 + 32)
                        pe.wait_ge(*s_moe.dve.at(f"h{1 - u}", j, 1 - u))
                        for w_, bank in ((wg, 2), (wu, 3)):
                            for k in range(KD):
                                for h in range(2):
                                    m = nc.tensor.matmul(ps[bank][BT * h:BT * (h + 1), 0:256], e_xT[u][:, k, :], w_[:, k, 256 * h:256 * (h + 1)], start=k == 0, stop=k == KD - 1)
                            m.then_inc(*S.tick(f"{'gate' if bank == 2 else 'up'}{u}"))
                        pe.wait_ge(*s_moe.dve.at(f"h{u}", j))
                        for c in range(2):
                            m = nc.tensor.transpose(ps[4][:, P * c:P * (c + 1)], e_h[u][:, P * c:P * (c + 1)], ident)
                        m.then_inc(*S.tick(f"hT{u}"))
                        pe.wait_ge(*s_moe.dve.at(f"hT{u}", j))
                        pe.wait_ge(dn_in[u], j * 16 + 16)
                        pe.wait_ge(*s_moe.act.at(f"y{1 - u}", j, 1 - u))
                        for n in range(4):
                            for h in range(2):
                                m = nc.tensor.matmul(ps[5][BT * h:BT * (h + 1), :], e_hT[u][:, n % 2, n // 2, :], wd[:, n, 512 * h:512 * (h + 1)], start=n == 0, stop=n == 3)
                        m.then_inc(*S.tick(f"down{u}"))
                    pe.end_ifs()

        @block.gpsimd
        def _(pool):
            nc.gpsimd.memset(zeros, 0.0).then_inc(zeros_ready, 1)
            nc.gpsimd.memset(bonus[:, :, :], 0.0).then_inc(zeroed, 1)
            pool.wait_ge(*s_tm.pe.at(f"t{3 * NT - 1}"))
            nc.gpsimd.memset(hTf[:, 0:1024], 0.0).then_inc(zeroed, 1)
            nc.gpsimd.memset(hTf[:, 2560:5120], 0.0).then_inc(zeroed, 1)
            S = s_gdn.pool
            pool.sem_inc(*S.open())
            pool.wait_ge(*s_l2.dve.at("out", 7))

            def gdn_pool(it, hp, tiles):
                S.begin(it)
                pool.wait_ge(*S.so_far())
                pool.wait_ge(*s_gdn.pe.at("t2", it, 1))
                pool.wait_ge(*s_gdn.dve.at("q1", it, 1))
                pool.sem_inc(waited, 1)
                for d in range(2):
                    col = tiles[d] * P
                    for base, dst in ((FM_K2, g_kq[:, 2 * d:2 * d + 2, 0:P]), (FM_Q2, g_kq[:, 2 * d:2 * d + 2, P:2 * P]), (FM_V2, pair(g_vf, d))):
                        for hh in range(2):
                            nc.gpsimd.tensor_copy(dst[:, hh], fmf[:, bass.ds((base + hh) * TOK + hp * (2 * TOK) + col, P)]).then_inc(*S.tick())
                    for hh in range(2):
                        nc.gpsimd.tensor_copy(g_gb[:, 2 * d + hh, :], gtf[:, bass.ds((2 * NT) * 8 + tiles[d] * 8 + hp * 2 + 4 * d + hh, 1)].to_broadcast([P, P])).then_inc(*S.tick())
                S.book[f"copies"] = S.n
                pool.wait_ge(*s_gdn.act.at("eg", it))
                pool.sem_inc(waited, 1)
                for d in range(2):
                    last = P - 1 if d == 0 else 0
                    nc.gpsimd.tensor_copy(g_egl[:, 2 * d:2 * d + 2], pair(g_eg, d)[:, :, last]).then_inc(*S.tick())
                pool.wait_ge(*S.so_far())
                nc.gpsimd.tensor_tensor(g_eg, g_eg, g_kq[:, :, P:2 * P], ALU.mult).then_inc(*S.tick("qd"))

            fmf, gtf = flat(fm[:, :, :]), gtmp[:, :, :, :].rearrange("p a b c -> p (a b c)")
            with pool.Fori(0, 2) as hp:
                gdn_pool(hp, hp, (0, 0))
            with pool.Fori(1, NT) as n:
                with pool.Fori(0, 2) as hp:
                    gdn_pool(n * 2 + hp, hp, (n, NT - n))
            pool.wait_ge(*s_gdn.dve.at("state", 2 * NT - 1))
            pool.wait_ge(*s_gdn.pe.at("t2", 2 * NT - 1))
            nc.gpsimd.memset(y_r, 0.0).then_inc(rzero, 1)
            nc.gpsimd.memset(zst, 0.0).then_inc(rzero, 1)
            S = s_rwkv.pool
            pool.sem_inc(*S.open())
            pool.wait_ge(lora_in, 64)
            pool.wait_ge(*s_kk.dve.at("out", FT - 1))

            def rwkv_pool(it, ft, tiles):
                S.begin(it)
                pool.wait_ge(*S.so_far())
                pool.wait_ge(*s_rwkv.pe.at("t2", it, 1))
                pool.wait_ge(*s_rwkv.dve.at("last", it, 1))
                pool.sem_inc(waited, 1)
                nc.gpsimd.tensor_copy(r_par, rpar[:, :, :].rearrange("p f n -> p (f n)")[:, bass.ds(ft * 8, 8)]).then_inc(*S.tick())
                for d in range(2):
                    nc.gpsimd.tensor_copy(r_lora[:, d, :], lora[:, bass.ds(ft * P + RW * d, P)]).then_inc(*S.tick())
                    nc.gpsimd.tensor_copy(r_lw[:, d, :], fmf[:, bass.ds(tiles[d] * P + FM_LORA * TOK, P)]).then_inc(*S.tick())
                    nc.gpsimd.tensor_copy(r_v[:, d, :], v_tm[:, :, :].rearrange("p t n -> p (t n)")[:, bass.ds(tiles[d] * RW + ft * P, P)]).then_inc(*S.tick("copies"))
                pool.wait_ge(*s_rwkv.dve.at("gates", it))
                pool.wait_ge(*S.so_far())
                pool.sem_inc(waited, 1)
                nc.gpsimd.tensor_scalar(r_kd, r_eu[:, 2:4, :], r_par[:, 5:6], r_par[:, 6:7], ALU.mult, ALU.add).then_inc(*S.tick())
                for d in range(2):
                    nc.gpsimd.tensor_tensor(r_kka[:, d, :], r_eu[:, 2 + d, :], fmf[:, bass.ds(ft * TOK + tiles[d] * P + FM_Q2 * TOK, P)], ALU.mult).then_inc(*S.tick("kka"))
                pool.wait_ge(*S.so_far())
                for d in range(2):
                    nc.gpsimd.tensor_tensor(r_kd[:, d, :], r_kd[:, d, :], fmf[:, bass.ds(ft * TOK + tiles[d] * P + FM_K * TOK, P)], ALU.mult).then_inc(*S.tick("kd"))
                pool.wait_ge(*S.so_far())
                pool.sem_inc(waited, 1)
                nc.gpsimd.tensor_scalar(r_rr, r_kd, r_par[:, 7:8], 1.0, ALU.mult, ALU.mult).then_inc(*S.tick())
                pool.wait_ge(*S.so_far())
                for d in range(2):
                    nc.gpsimd.tensor_tensor(r_rr[:, d, :], r_rr[:, d, :], fmf[:, bass.ds(ft * TOK + tiles[d] * P + FM_R * TOK, P)], ALU.mult).then_inc(*S.tick("rr"))

            with pool.Fori(0, FT) as ft:
                rwkv_pool(ft, ft, (0, 0))
            with pool.Fori(1, NT) as n:
                with pool.Fori(0, FT) as ft:
                    rwkv_pool(n * FT + ft, ft, (n, NT - n))
            S = s_route.pool
            pool.wait_ge(*s_conv.dve.at("out", 11))
            nc.gpsimd.memset(zi, 0).then_inc(*S.tick("zi"))
            nc.gpsimd.iota(tid, pattern=[[P, NT]], base=0, channel_multiplier=1).then_inc(*S.tick("tid"))
            pool.wait_ge(tz_out, 32)
            pool.wait_ge(*S.so_far())
            pool.wait_ge(*s_route.dve.at("slots"))
            for t in range(NT):
                for k in range(2):
                    nc.gpsimd.indirect_dma_start(out=tokd, out_offset=bass.IndirectOffsetOnAxis(ap=slot_i[:, t, k:k + 1], axis=0),
                                                 in_=tid[:, t:t + 1], in_offset=None).then_inc(tok_out, 16)
            pool.wait_ge(tok_in, 16)
            pool.wait_ge(h2_out, 16 * NT)
            pool.wait_ge(*s_route.dve.at("eb"))
            n_blocks = pool.value_load(eb_i[0:1, NB:NB + 1], min_val=0, max_val=NB)
            S = s_moe.pool
            pool.sem_inc(*S.open())
            with pool.Fori(0, NB // 2) as j:
                S.begin(j)
                for u in range(2):
                    with pool.If(j * 2 + u < n_blocks):
                        pool.wait_ge(*s_moe.pe.at(f"xT{u}", j, 1))
                        pool.sem_inc(waited, 1)
                        nc.gpsimd.tensor_copy(idx_u[:, u:u + 1], tok_i[:, bass.ds(j * 2 + u, 1)]).then_inc(*S.tick(f"idx{u}"))
                        pool.wait_ge(*S.so_far())
                        pool.sem_inc(waited, 1)
                        nc.gpsimd.indirect_dma_start(out=e_x[u], out_offset=None, in_=h2d,
                                                     in_offset=bass.IndirectOffsetOnAxis(ap=idx_u[:, u:u + 1], axis=0)).then_inc(rows_in[u], 16)
                    pool.end_ifs()
            pool.wait_ge(yd_zeroed, 16)
            for u in range(2):
                n_u = pool.snap((n_blocks + (1 - u)) // 2)
                pool.wait_ge(y_out[u], n_u * 32 + 32)
                pool.sem_inc(waited, 1)
            for t in range(NT):
                for k in range(2):
                    if t >= 1:
                        pool.wait_ge(*s_fin.dve.at(f"sum{t - 1}"))
                    nc.gpsimd.indirect_dma_start(out=comb(k), out_offset=None, in_=yd,
                                                 in_offset=bass.IndirectOffsetOnAxis(ap=slot_i[:, t, k:k + 1], axis=0)).then_inc(comb_in[k], 16)

        @block.scalar
        def _(act):
            S = s_norm.act
            act.wait_ge(c_in, 32)
            nc.scalar.activation(cexp, craw, ACT.Exp, scale=-1.0).then_inc(*S.tick("cexp"))
            act.wait_ge(x_in, 32)
            for t in range(NT):
                nc.scalar.activation(flat(hT[:, :, :])[:, D * t:D * (t + 1)], x[:, t, :], ACT.Square, accum_out=ssq[:, t:t + 1]).then_inc(*S.tick(f"ssq{t}"))
            S = s_ada.act
            act.sem_inc(*S.open())
            for j0, j1, home in ((0, 2, moda), (2, A_USES, modk)):
                with act.Fori(j0, j1) as j:
                    S.begin(j)
                    for u in range(2):
                        for c in range(2):
                            act.wait_ge(*s_ada.pe.at(f"bc{u}{c}", j))
                            dst = home[:, c].rearrange("p s n -> p (s n)")[:, bass.ds((j - j0) * 2 * COLS + COLS * u, COLS)]
                            nc.scalar.copy(dst, ps[2 + 2 * u + c][:, :]).then_inc(*S.tick(f"bc{u}{c}"))
            S = s_norm.act
            act.wait_ge(*s_norm.dve.at("var"))
            nc.scalar.activation(std, std, ACT.Sqrt).then_inc(*S.tick("std"))
            for t in range(NT):
                for b in range(2):
                    act.wait_ge(*s_norm.pe.at(f"hT{t}{b}"))
                    nc.scalar.copy(hT[:, 4 * b:4 * b + 4, P * t:P * (t + 1)], ps[b][:, :].rearrange("p (k n) -> p k n", k=4)
                                   ).then_inc(*S.tick(f"hT{t}{b}"))
            S = s_fm.act
            act.sem_inc(*S.open())
            with act.Fori(0, 2) as j:
                S.begin(j)
                for job in range(8):
                    act.wait_ge(*s_fm.pe.at(f"p{job}", j))
                    nc.scalar.copy(flat(fm[:, :, :])[:, bass.ds(j * 8 * TOK + job * TOK, HALF)], ps[2 * (job % 2)][:, 0:HALF]).then_inc(*S.tick(f"a{job}"))
            S = s_tm.act
            for job in range(6):
                act.wait_ge(*s_tm.pe.at(f"p{job}"))
                nc.scalar.copy(fm[:, FM_V2 + job, 0:HALF], ps[2 * (job % 2)][:, 0:HALF]).then_inc(*S.tick(f"a{job}"))
            for n, dst in enumerate((v_tm, z_tm, ba)):
                for t in range(NT):
                    q = n * NT + t
                    act.wait_ge(*s_tm.pe.at(f"t{q}"))
                    nc.scalar.copy(dst[:, t, :], ps[4 + q % 4][:, 0:dst[:, t, :].shape[-1]]).then_inc(*S.tick(f"t{q}"))
            S = s_conv.act
            act.sem_inc(*S.open())
            with act.Fori(0, 12) as j:
                S.begin(j)
                act.wait_ge(*s_conv.dve.at("cv", j))
                nc.scalar.activation(scr[:, 1, :], scr[:, 0, :], ACT.Exp, scale=-1.0).then_inc(*S.tick("e"))
            S = s_prep.act
            act.wait_ge(*s_tm.act.so_far())
            nc.scalar.activation(gtmp[:, 0], ba[:, :, 0:8], ACT.Exp, scale=-1.0).then_inc(*S.tick("ebeta"))
            act.wait_ge(*s_prep.dve.at("xa"))
            nc.scalar.activation(gtmp[:, 1], gtmp[:, 2], ACT.Abs).then_inc(*S.tick())
            act.wait_ge(*S.so_far())
            nc.scalar.activation(gtmp[:, 1], gtmp[:, 1], ACT.Exp, scale=-1.0).then_inc(*S.tick())
            act.wait_ge(*S.so_far())
            nc.scalar.activation(gtmp[:, 1], gtmp[:, 1], ACT.Ln, bias=1.0).then_inc(*S.tick("ln"))
            act.wait_ge(par_in, 16 * 12)
            nc.scalar.activation(par[:, 48:56], par[:, 48:56], ACT.Exp).then_inc(*S.tick("alog"))
            nc.scalar.activation(fm[0:64, FM_LORA, :], fm[0:64, FM_LORA, :], ACT.Tanh).then_inc(*S.tick("tanh"))
            S = s_prep.act
            act.wait_ge(*s_prep.pe.at("G"))
            Gp = ps[7][:, 0:64].rearrange("p (d n) -> p d n", d=2)[:, :, 0:20].rearrange("p d (t h) -> p d t h", t=NT)
            for d in range(2):
                nc.scalar.copy(gs[:, d, :, :, 0], Gp[:, d]).then_inc(*S.tick())
                nc.scalar.activation(gs[:, d, :, :, 1], Gp[:, d], ACT.Exp).then_inc(*S.tick("eg0" if d == 0 else "negeg"))
            S = s_l2.act
            act.sem_inc(*S.open())
            def l2_act(it, src):
                S.begin(it)
                act.wait_ge(*S.so_far())
                act.wait_ge(*s_l2.dve.at("out", it, 1))
                act.wait_ge(*s_l2.pe.at("ss", it, 1))
                nc.scalar.activation(scr[:, 0, :], src, ACT.Square).then_inc(*S.tick("sq"))
                act.wait_ge(*s_l2.dve.at("eps", it))
                nc.scalar.activation(scr[:, 1, :], scr[:, 1, :], ACT.Sqrt).then_inc(*S.tick("sd"))
            act.wait_ge(*s_conv.dve.at("out", 11))
            with act.Fori(0, 8) as j:
                l2_act(j, flat(fm[:, :, :])[:, bass.ds(j * TOK + FM_Q2 * TOK, TOK)])
            S = s_gdn.act
            act.sem_inc(*S.open())

            def gdn_act(it, hp, tiles):
                S.begin(it)
                act.wait_ge(*S.so_far())
                act.wait_ge(*s_gdn.pool.at("qd", it, 1))
                act.wait_ge(*s_gdn.pe.at("t2", it, 1))
                act.wait_ge(*s_gdn.dve.at("dif", it))
                nc.scalar.activation(g_et, g_et, ACT.Exp).then_inc(*S.tick("et"))
                nc.scalar.activation(g_eg, ps[0][:, :].rearrange("p (s n) -> p s n", n=P), ACT.Exp).then_inc(*S.tick("eg"))
                act.wait_ge(*s_gdn.pe.at("ktm", it))
                for s_ in range(4):
                    nc.scalar.mul(g_rhs[:, s_, 0:P], ps[3][:, P * s_:P * (s_ + 1)], g_sc[:, s_, 1:2]).then_inc(*S.tick())
                act.wait_ge(*s_gdn.dve.at("etm", it))
                for s_ in range(4):
                    last = P - 1 if s_ < 2 else 0
                    nc.scalar.mul(g_qk[:, s_, P:2 * P], ps[3][:, P * s_:P * (s_ + 1)], g_et[:, s_, last:last + 1]).then_inc(*S.tick())
                act.wait_ge(*s_gdn.pe.at("vtm", it))
                nc.scalar.copy(g_rhs[:, :, P:2 * P], ps[4][:, :].rearrange("p (s n) -> p s n", n=P)).then_inc(*S.tick("vtm"))
                inverse_act(act, S, s_gdn, it)
                for d in range(2):
                    act.wait_ge(*s_gdn.pe.at(f"w{d}", it))
                    for hh in range(2):
                        s_ = 2 * d + hh
                        nc.scalar.mul(g_w[:, s_, :], ps[6 + d][:, 256 * hh:256 * (hh + 1)], g_sc[:, s_, 3:4]).then_inc(*S.tick(f"w{d}"))

            with act.Fori(0, 2) as hp:
                gdn_act(hp, hp, (0, 0))
            with act.Fori(1, NT) as n:
                with act.Fori(0, 2) as hp:
                    gdn_act(n * 2 + hp, hp, (n, NT - n))
            S = s_kk.act
            act.sem_inc(*S.open())
            with act.Fori(0, FT) as j:
                S.begin(j)
                act.wait_ge(*S.so_far())
                act.wait_ge(*s_kk.pe.at("ss", j, 1))
                act.wait_ge(*s_kk.dve.at("raw", j))
                nc.scalar.activation(scr[:, 0, :], scr[:, 2, :], ACT.Square).then_inc(*S.tick("sq"))
                act.wait_ge(*s_kk.dve.at("eps", j))
                nc.scalar.activation(scr[:, 1, :], scr[:, 1, :], ACT.Sqrt).then_inc(*S.tick("sd"))
            S = s_rwkv.act
            act.sem_inc(*S.open())

            def rwkv_act(it, ft, tiles):
                S.begin(it)
                act.wait_ge(*S.so_far())
                act.wait_ge(*s_rwkv.dve.at("last", it, 1))
                act.wait_ge(*s_rwkv.pool.at("rr", it, 1))
                act.wait_ge(*s_rwkv.pool.at("copies", it))
                act.wait_ge(*s_rwkv.pe.at("u", it))
                for kind in range(2):
                    for d in range(2):
                        n = 2 * kind + d
                        nc.scalar.activation(r_eu[:, n, :], ps[kind][:, P * d:P * (d + 1)], ACT.Exp, scale=-1.0, bias=r_par[:, n:n + 1]).then_inc(*S.tick("eu"))
                act.wait_ge(*s_rwkv.dve.at("pq", it))
                for n, (src, sign) in enumerate(((2, -1), (1, 1), (0, -1), (3, 1), (0, 1), (3, -1))):
                    nc.scalar.activation(r_ex[:, n, :], r_pq[:, src, :], ACT.Exp, scale=sign * DECAY).then_inc(*S.tick(f"ex{n}"))
                nc.scalar.activation(r_h, r_ht, ACT.Exp, scale=-DECAY).then_inc(*S.tick("h"))
                act.wait_ge(*s_rwkv.pe.at("bktm", it))
                act.wait_ge(*s_rwkv.pe.at("t2", it, 1))
                for d in range(2):
                    nc.scalar.copy(r_sc[:, 2 * d:2 * d + 2, 256:320], ps[6][:, P * d:P * (d + 1)].rearrange("p (s n) -> p s n", s=2)).then_inc(*S.tick())
                nc.scalar.copy(r_ktm, ps[6][:, 256:512].rearrange("p (s n) -> p s n", n=RD)).then_inc(*S.tick())
                act.wait_ge(*s_rwkv.pe.at("atm", it))
                nc.scalar.copy(r_rhs[:, :, 0:RD], ps[7][:, 0:256].rearrange("p (s n) -> p s n", n=RD)).then_inc(*S.tick("tm"))
                act.wait_ge(*s_rwkv.pe.at("akv", it))
                nc.scalar.copy(r_rhs[:, :, RD:P], ps[0][:, 0:256].rearrange("p (s n) -> p s n", n=RD)).then_inc(*S.tick("akv"))
                inverse_act(act, S, s_rwkv, it)
                for d in range(2):
                    act.wait_ge(*s_rwkv.pe.at(f"w{d}", it))
                    nc.scalar.copy(pair(r_w, d), ps[6 + d][:, 0:256].rearrange("p (s n) -> p s n", s=2)).then_inc(*S.tick(f"w{d}"))

            act.wait_ge(par_in, 16 * 12)
            with act.Fori(0, FT) as ft:
                rwkv_act(ft, ft, (0, 0))
            Z = s_zs.act
            act.wait_ge(*s_zs.pe.at("out"))
            for b in range(2):
                nc.scalar.copy(znat[0:RD, 512 * b:512 * (b + 1)], ps[b][0:RD, :]).then_inc(*Z.tick("znat"))
            act.wait_ge(*s_zs.pe.at("in"))
            nc.scalar.copy(zst, ps[0][:, :]).then_inc(*Z.tick("zst"))
            with act.Fori(1, NT) as n:
                with act.Fori(0, FT) as ft:
                    rwkv_act(n * FT + ft, ft, (n, NT - n))
            act.wait_ge(yd_zeroed, 16)
            S = s_tail.act
            act.sem_inc(*S.open())
            nc.scalar.activation(fm[:, FM_LORA + 1, :], fm[:, FM_LORA + 1, :], ACT.Sigmoid).then_inc(*s_route.act.tick("sgl"))

            def tail_act(it):
                S.begin(it)
                act.wait_ge(*S.so_far())
                act.wait_ge(*s_tail.dve.at("last", it, 1))
                yrt = y_r[:, bass.ds(it * RW, RW)]
                act.wait_ge(*s_tail.dve.at("yc", it))
                nc.scalar.activation(tb, ta, ACT.Square).then_inc(*S.tick("ysq"))
                act.wait_ge(*s_tail.dve.at("var", it))
                nc.scalar.activation(t_st[:, 16:28], t_st[:, 16:28], ACT.Sqrt).then_inc(*S.tick("sd"))
                act.wait_ge(*s_tail.dve.at("gn", it))
                nc.scalar.activation(ta, zf[:, bass.ds(it * GH * GD, GH * GD)], ACT.Silu).then_inc(*S.tick("sz"))
                for b in range(2):
                    act.wait_ge(*s_tail.pe.at(f"oT{b}", it))
                    nc.scalar.copy(oT[:, 4 * b:4 * b + 4, :], ps[1 + b][:, :].rearrange("p (k n) -> p k n", n=P)).then_inc(*S.tick(f"oT{b}"))
                act.wait_ge(*s_tail.dve.at("x2", it))
                nc.scalar.activation(o_tm, xf[:, bass.ds(it * D, D)], ACT.Square, accum_out=t_st[:, 32:33]).then_inc(*S.tick("ssq"))
                act.wait_ge(*s_tail.dve.at("var2", it))
                nc.scalar.activation(t_st[:, 33:34], t_st[:, 33:34], ACT.Sqrt).then_inc(*S.tick("sd2"))
                for b in range(2):
                    act.wait_ge(*s_tail.pe.at(f"h2T{b}", it))
                    nc.scalar.copy(h2T[:, 4 * b:4 * b + 4, :], ps[5 + b][:, :].rearrange("p (k n) -> p k n", n=P)).then_inc(*S.tick(f"h2T{b}"))
                act.wait_ge(*s_tail.dve.at("gmax", it))
                nc.scalar.activation(lt_[:, 0:4], lg[:, 0:4], ACT.Exp, bias=lt_[:, 4:5], accum_out=lt_[:, 5:6]).then_inc(*S.tick("gsum"))
                act.wait_ge(*s_tail.dve.at("e2", it))
                nc.scalar.activation(lt_[:, 6:7], lt_[:, 6:7], ACT.Exp).then_inc(*S.tick("e2"))

            xf, zf = x[:, :, :].rearrange("p t n -> p (t n)"), z_tm[:, :, :].rearrange("p t n -> p (t n)")
            tail_act(0)
            with act.Fori(1, NT) as t:
                tail_act(t)
            act.wait_ge(*s_route.dve.at("eb"))
            n_blocks = act.value_load(eb_i[0:1, NB:NB + 1], min_val=0, max_val=NB)
            S = s_moe.act
            act.sem_inc(*S.open())
            for u in range(2):
                act.sem_inc(y_out[u], 32)
            with act.Fori(0, NB // 2) as j:
                S.begin(j)
                for u in range(2):
                    with act.If(j * 2 + u < n_blocks):
                        act.wait_ge(*s_moe.pe.at(f"xT{u}", j))
                        act.wait_ge(*s_moe.pe.at(f"down{u}", j, 1))
                        nc.scalar.copy(e_xT[u], ps[u][:, :].rearrange("p (k n) -> p k n", n=BT)).then_inc(*S.tick(f"xT{u}"))
                        act.wait_ge(*s_moe.pe.at(f"gate{u}", j))
                        nc.scalar.activation(e_h[u], ps[2][:, 0:256], ACT.Silu).then_inc(*S.tick(f"silu{u}"))
                        act.wait_ge(*s_moe.pe.at(f"down{u}", j))
                        act.wait_ge(y_out[u], j * 32 + 32)
                        nc.scalar.copy(e_y[u], ps[5][:, :]).then_inc(*S.tick(f"y{u}"))
                        act.wait_ge(*S.so_far())
                        for h in range(2):
                            act.dma_start(yd[bass.ds((j * 2 + u) * BT, BT), 512 * h:512 * (h + 1)], e_y[u][BT * h:BT * (h + 1), :]).then_inc(y_out[u], 16)
                    act.end_ifs()
            S = s_fin.act
            for t in range(NT):
                act.wait_ge(*s_fin.dve.at(f"x{t}"))
                nc.scalar.activation(comb(0), x[:, t, :], ACT.Square, accum_out=ssq[:, t:t + 1]).then_inc(*S.tick(f"ssq{t}"))
                act.wait_ge(*s_fin.dve.at(f"var{t}"))
                nc.scalar.activation(std[:, t:t + 1], std[:, t:t + 1], ACT.Sqrt).then_inc(*S.tick(f"sd{t}"))

        @block.vector
        def _(dve):
            S = s_norm.dve
            dve.wait_ge(*s_norm.act.at("cexp"))
            nc.vector.tensor_scalar(cexp, cexp, 1.0, None, ALU.add).then_inc(*S.tick())
            dve.wait_ge(*S.so_far())
            nc.vector.reciprocal(cexp, cexp).then_inc(*S.tick())
            dve.wait_ge(*S.so_far())
            nc.vector.tensor_tensor(silc.rearrange("p k c -> p c k"), craw, cexp, ALU.mult).then_inc(*S.tick("silc"))
            dve.wait_ge(*s_norm.act.at(f"ssq{NT - 1}"))
            nc.vector.tensor_scalar(std, ssq, 1.0 / D, NORM_EPS, ALU.mult, ALU.add).then_inc(*S.tick("var"))
            S = s_ada.dve
            dve.sem_inc(*S.open())
            dve.wait_ge(bias_in, 16)
            with dve.Fori(0, A_USES) as j:
                S.begin(j)
                for u in range(2):
                    dve.wait_ge(ring_used[u], j + 1)
                    row = modrow[:, bass.ds(j * 2 * COLS + COLS * u, COLS)]
                    nc.vector.tensor_tensor(row, row, ps[u][0:2, :], ALU.add).then_inc(*S.tick(f"row{u}"))
            S = s_norm.dve
            dve.wait_ge(*s_norm.act.at("std"))
            nc.vector.reciprocal(rstd, std).then_inc(*S.tick())
            dve.wait_ge(*s_ada.act.at("bc11", A_USES - 1))
            dve.wait_ge(gain_in, 16)
            for c in range(2):
                nc.vector.scalar_tensor_tensor(moda[:, c, 1, :], moda[:, c, 1, :], 1.0, bias_row[:, :], ALU.add, ALU.mult).then_inc(*S.tick())
            dve.wait_ge(*S.so_far())
            for t in range(NT):
                c = min(t, 1)
                if t >= 2:
                    dve.wait_ge(*s_norm.pe.at(f"hT{t - 2}1"))
                hr = hrow if t % 2 == 0 else hrow2
                nc.vector.scalar_tensor_tensor(hr, x[:, t, :], rstd[:, t:t + 1], moda[:, c, 1, :], ALU.mult, ALU.mult).then_inc(*S.tick())
                dve.wait_ge(*S.so_far())
                nc.vector.tensor_tensor(hr, hr, moda[:, c, 0, :], ALU.add).then_inc(*S.tick(f"h{t}"))
            S = s_fm.dve
            dve.sem_inc(*S.open())
            with dve.Fori(0, 2) as j:
                S.begin(j)
                for job in range(8):
                    dve.wait_ge(*s_fm.pe.at(f"p{job}", j))
                    nc.vector.tensor_copy(flat(fm[:, :, :])[:, bass.ds(j * 8 * TOK + job * TOK + HALF, HALF)], ps[2 * (job % 2) + 1][:, 0:HALF]).then_inc(*S.tick(f"d{job}"))
            S = s_tm.dve
            for job in range(6):
                dve.wait_ge(*s_tm.pe.at(f"p{job}"))
                nc.vector.tensor_copy(fm[:, FM_V2 + job, HALF:TOK], ps[2 * (job % 2) + 1][:, 0:HALF]).then_inc(*S.tick(f"d{job}"))
            fmd = flat(fm[:, :, :])
            S = s_conv.dve
            dve.sem_inc(*S.open())
            dve.wait_ge(par_in, 16 * 12)
            cwf = cw[:, :, :].rearrange("p a b -> p (a b)")
            dve.wait_ge(*s_tm.act.at("a3"))
            dve.wait_ge(*s_tm.dve.at("d5"))
            with dve.Fori(0, 12) as j:
                S.begin(j)
                src = flat(fm[:, :, :])[:, bass.ds(j * TOK + FM_Q2 * TOK, TOK)]
                rows = src.rearrange("p (r c) -> p r c", c=ROW)
                cv = scr[:, 0, :]
                cvr = cv.rearrange("p (r c) -> p r c", c=ROW)
                taps = hst[:, 0:3]
                dve.wait_ge(*S.so_far())
                nc.vector.tensor_copy(taps, cwf[:, bass.ds(j * 4, 3)]).then_inc(*S.tick())
                dve.wait_ge(*S.so_far())
                nc.vector.tensor_scalar(cv, src, taps[:, 1:2], None, ALU.mult).then_inc(*S.tick())
                dve.wait_ge(*S.so_far())
                nc.vector.scalar_tensor_tensor(cvr[:, :, 1:], rows[:, :, :-1], taps[:, 0:1], cvr[:, :, 1:], ALU.mult, ALU.add).then_inc(*S.tick())
                dve.wait_ge(*S.so_far())
                nc.vector.scalar_tensor_tensor(cvr[:, :, :-1], rows[:, :, 1:], taps[:, 2:3], cvr[:, :, :-1], ALU.mult, ALU.add).then_inc(*S.tick())
                dve.wait_ge(*S.so_far())
                nc.vector.scalar_tensor_tensor(cv[:, ROW:ROW + 1], rows[:, 0, ROW - 1:ROW], taps[:, 0:1], cv[:, ROW:ROW + 1], ALU.mult, ALU.add).then_inc(*S.tick())
                nc.vector.scalar_tensor_tensor(cv[:, ROW - 1:ROW], rows[:, 1, 0:1], taps[:, 2:3], cv[:, ROW - 1:ROW], ALU.mult, ALU.add).then_inc(*S.tick("cv"))
                dve.wait_ge(*s_conv.act.at("e", j))
                nc.vector.tensor_scalar(scr[:, 1, :], scr[:, 1, :], 1.0, None, ALU.add).then_inc(*S.tick())
                dve.wait_ge(*S.so_far())
                nc.vector.reciprocal(scr[:, 1, :], scr[:, 1, :]).then_inc(*S.tick())
                dve.wait_ge(*S.so_far())
                nc.vector.tensor_tensor(src, cv, scr[:, 1, :], ALU.mult).then_inc(*S.tick("out"))
            S = s_prep.dve
            dve.wait_ge(*s_tm.act.at(f"t{3 * NT - 1}"))
            dtb = par[:, 56:64].unsqueeze(1).to_broadcast([P, NT, 8])
            nc.vector.tensor_tensor(gtmp[:, 2], ba[:, :, 8:16], dtb, ALU.add).then_inc(*S.tick("xa"))
            dve.wait_ge(*s_prep.act.at("ebeta"))
            nc.vector.tensor_scalar(gtmp[:, 0], gtmp[:, 0], 1.0, None, ALU.add).then_inc(*S.tick())
            dve.wait_ge(*s_prep.act.at("ln"))
            nc.vector.tensor_scalar(gtmp[:, 2], gtmp[:, 2], 0.0, None, ALU.max).then_inc(*S.tick())
            dve.wait_ge(*S.so_far())
            nc.vector.tensor_tensor(gtmp[:, 2], gtmp[:, 2], gtmp[:, 1], ALU.add).then_inc(*S.tick())
            nc.vector.reciprocal(gtmp[:, 3], gtmp[:, 0]).then_inc(*S.tick())
            dve.wait_ge(*s_prep.act.at("alog"))
            dve.wait_ge(*S.so_far())
            nc.vector.scalar_tensor_tensor(gtmp[:, 2], gtmp[:, 2], -1.0, par[:, 48:56].unsqueeze(1).to_broadcast([P, NT, 8]), ALU.mult, ALU.mult).then_inc(*S.tick("g"))
            for d in range(2):
                nc.vector.tensor_scalar(gs[:, d, :, :, 2], gtmp[:, 3, :, 4 * d:4 * d + 4], -1.0, None, ALU.mult).then_inc(*S.tick())
                nc.vector.tensor_copy(gs[:, d, :, :, 3], gtmp[:, 3, :, 4 * d:4 * d + 4]).then_inc(*S.tick())
            dve.wait_ge(*s_prep.act.at("negeg"))
            for d in range(2):
                nc.vector.tensor_scalar(gs[:, d, :, :, 1], gs[:, d, :, :, 1], -1.0, None, ALU.mult).then_inc(*S.tick("gs"))
            S = s_l2.dve
            dve.sem_inc(*S.open())

            def l2_dve(it, src, dst, scale):
                S.begin(it)
                dve.wait_ge(*S.so_far())
                dve.wait_ge(*s_l2.pe.at("ss", it))
                for g in range(2):
                    nc.vector.tensor_scalar(scr[:, 1, HALF * g:HALF * (g + 1)], ps[g][:, 0:HALF], 1e-6, scale, ALU.add, ALU.mult).then_inc(*S.tick("eps"))
                dve.wait_ge(*s_l2.act.at("sd", it))
                nc.vector.reciprocal(scr[:, 1, :], scr[:, 1, :]).then_inc(*S.tick())
                dve.wait_ge(*S.so_far())
                nc.vector.tensor_tensor(dst, src, scr[:, 1, :], ALU.mult).then_inc(*S.tick("out"))

            for g0 in range(2):
                with dve.Fori(4 * g0, 4 * g0 + 4) as j:
                    src = flat(fm[:, :, :])[:, bass.ds(j * TOK + FM_Q2 * TOK, TOK)]
                    l2_dve(j, src, src, float(GD) if g0 == 0 else 1.0)
            S = s_gdn.dve
            dve.sem_inc(*S.open())
            dve.wait_ge(*s_prep.dve.at("gs"))
            gsf = gs[:, :, :, :, :].rearrange("p d t h n -> p (d t h n)")

            def gdn_dve(it, hp, tiles):
                S.begin(it)
                dve.wait_ge(*S.so_far())
                dve.wait_ge(*s_gdn.act.at("w1", it, 1))
                for d in range(2):
                    nc.vector.tensor_copy(g_sc[:, 2 * d:2 * d + 2, :].rearrange("p s n -> p (s n)"),
                                          gsf[:, bass.ds((tiles[d] + NT * d) * (4 * GH) + hp * 8, 8)]).then_inc(*S.tick())
                dve.wait_ge(*S.so_far())
                dve.wait_ge(*s_gdn.pe.at("grow", it))
                for s_ in range(4):
                    nc.vector.tensor_scalar(g_et[:, s_, :], ps[0][:, P * s_:P * (s_ + 1)], g_sc[:, s_, 0:1], 0.0, ALU.subtract, ALU.min).then_inc(*S.tick("dif"))
                dve.wait_ge(*s_gdn.act.at("et", it))
                for d in range(2):
                    nc.vector.tensor_tensor(pair(g_et, d), pair(g_et, d), two(incl(d)), ALU.mult).then_inc(*S.tick("etm"))
                dve.wait_ge(*S.so_far())
                dve.wait_ge(*s_gdn.pe.at("scores", it))
                for s_ in range(4):
                    nc.vector.scalar_tensor_tensor(g_lt[:, s_, :], ps[1 + s_ // 2][:, 256 * (s_ % 2):256 * (s_ % 2) + P], g_sc[:, s_, 2:3], g_et[:, s_, :], ALU.mult, ALU.mult).then_inc(*S.tick())
                for d in range(2):
                    nc.vector.tensor_tensor(g_qk[:, 2 * d:2 * d + 2, 0:P], ps[1 + d][:, :].rearrange("p (s n) -> p s n", s=2)[:, :, P:2 * P], pair(g_et, d), ALU.mult).then_inc(*S.tick("qk"))
                dve.wait_ge(*S.so_far())
                for d in range(2):
                    inverse_dve_start(dve, S, d, pair(g_lt, d))
                inverse_dve(dve, S, s_gdn, it)
                dve.wait_ge(*s_gdn.pool.at("qd", it))
                for d in range(2):
                    dve.wait_ge(*s_gdn.pe.at(f"c{d}", it))
                    cp = ps[d][:, :].rearrange("p (s n) -> p s n", s=2)
                    nc.vector.tensor_tensor(pair(g_q1, d), cp[:, :, 0:P], pair(g_eg, d), ALU.add).then_inc(*S.tick("q1"))
                    for hh in range(2):
                        s_ = 2 * d + hh
                        nc.vector.scalar_tensor_tensor(g_t1[:, s_, :], ident, g_egl[:, s_:s_ + 1], cp[:, hh, P:2 * P], ALU.mult, ALU.add).then_inc(*S.tick("t1"))
                dve.wait_ge(*s_gdn.pe.at("y", it))
                for d in range(2):
                    yv = y_gf[:, bass.ds(tiles[d] * 512 + hp * 256, 256)]
                    nc.vector.tensor_tensor(yv, yv, ps[2][:, 256 * d:256 * (d + 1)], ALU.add).then_inc(*S.tick())
                    dve.wait_ge(*S.so_far())
                dve.wait_ge(*s_gdn.pe.at("t2", it))
                for d in range(2):
                    nc.vector.tensor_copy(g_state[:, d, bass.ds(hp * 256, 256)], ps[3][:, 256 * d:256 * (d + 1)]).then_inc(*S.tick("state"))

            y_gf = hTf[:, 2560:5120]
            dve.wait_ge(zeroed, 3)
            with dve.Fori(0, 2) as hp:
                gdn_dve(hp, hp, (0, 0))
            dve.wait_ge(state_in, 32)
            with dve.Fori(1, NT) as n:
                with dve.Fori(0, 2) as hp:
                    gdn_dve(n * 2 + hp, hp, (n, NT - n))
            dve.wait_ge(yd_zeroed, 16)
            S = s_kk.dve
            dve.sem_inc(*S.open())
            dve.wait_ge(*s_gdn.pe.at("t2", 2 * NT - 1))
            dve.wait_ge(*s_gdn.pool.at("qd", 2 * NT - 1))
            dve.wait_ge(*s_l2.dve.at("out", 7))
            nc.vector.tensor_scalar(rpar[:, :, 6], rpar[:, :, 5], -1.0, 1.0, ALU.mult, ALU.add).then_inc(waited, 1)
            nc.vector.tensor_scalar(rpar[:, :, 0:4], rpar[:, :, 0:4], -1.0, None, ALU.mult).then_inc(waited, 1)
            rparf = rpar[:, :, :].rearrange("p f n -> p (f n)")
            with dve.Fori(0, FT) as j:
                S.begin(j)
                dve.wait_ge(*S.so_far())
                dve.sem_inc(waited, 1)
                nc.vector.tensor_copy(r_ht[:, 0:1], rparf[:, bass.ds(j * 8 + 4, 1)]).then_inc(*S.tick())
                dve.wait_ge(*S.so_far())
                nc.vector.tensor_scalar(scr[:, 2, :], fmd[:, bass.ds(j * TOK + FM_K * TOK, TOK)], r_ht[:, 0:1], None, ALU.mult).then_inc(*S.tick("raw"))
                dve.wait_ge(*s_kk.pe.at("ss", j))
                for g in range(2):
                    nc.vector.tensor_scalar(scr[:, 1, HALF * g:HALF * (g + 1)], ps[g][:, 0:HALF], 1e-6, None, ALU.add).then_inc(*S.tick("eps"))
                dve.wait_ge(*s_kk.act.at("sd", j))
                nc.vector.reciprocal(scr[:, 1, :], scr[:, 1, :]).then_inc(*S.tick())
                dve.wait_ge(*S.so_far())
                nc.vector.tensor_tensor(fmd[:, bass.ds(j * TOK + FM_Q2 * TOK, TOK)], scr[:, 2, :], scr[:, 1, :], ALU.mult).then_inc(*S.tick("out"))
            S = s_rwkv.dve
            dve.sem_inc(*S.open())
            dve.wait_ge(rzero, 2)
            bonusf = bonus[:, :, :].rearrange("p t h -> p (t h)")

            def rwkv_dve(it, ft, tiles):
                S.begin(it)
                dve.wait_ge(*S.so_far())
                dve.wait_ge(*s_rwkv.act.at("eu", it))
                nc.vector.tensor_scalar(r_eu, r_eu, 1.0, None, ALU.add).then_inc(*S.tick())
                dve.wait_ge(*S.so_far())
                nc.vector.reciprocal(r_eu, r_eu).then_inc(*S.tick("gates"))
                dve.wait_ge(*S.so_far())
                for d in range(2):
                    nc.vector.tensor_tensor_scan(r_cs[:, d, :], ones, r_eu[:, d, :], 0.0, ALU.mult, ALU.add).then_inc(*S.tick())
                dve.wait_ge(*S.so_far())
                nc.vector.tensor_scalar(r_ht, r_cs[:, :, P - 1], 0.5, None, ALU.mult).then_inc(*S.tick())
                dve.wait_ge(*S.so_far())
                for d in range(2):
                    nc.vector.tensor_scalar(r_pq[:, d, :], r_cs[:, d, :], r_ht[:, d:d + 1], None, ALU.subtract).then_inc(*S.tick())
                dve.wait_ge(*S.so_far())
                nc.vector.tensor_tensor(r_pq[:, 2:4, :], r_pq[:, 0:2, :], r_eu[:, 0:2, :], ALU.subtract).then_inc(*S.tick("pq"))
                dve.wait_ge(*s_rwkv.pe.at("t2", it, 1))
                dve.wait_ge(*s_rwkv.act.at("ex3", it))
                for d in range(2):
                    kkn = fmd[:, bass.ds(ft * TOK + tiles[d] * P + FM_Q2 * TOK, P)]
                    rr_ = fmd[:, bass.ds(ft * TOK + tiles[d] * P + FM_R * TOK, P)]
                    nc.vector.tensor_tensor(r_ar[:, d, 0:P], kkn, r_ex[:, d, :], ALU.mult).then_inc(*S.tick())
                    nc.vector.tensor_tensor(r_ar[:, d, P:2 * P], rr_, r_ex[:, 2 + d, :], ALU.mult).then_inc(*S.tick())
                dve.wait_ge(*s_rwkv.act.at("h", it))
                dve.wait_ge(*s_rwkv.pool.at("kd", it))
                nc.vector.scalar_tensor_tensor(r_bk[:, 0:2, :], r_kka, -1.0, r_ex[:, 4:6, :], ALU.mult, ALU.mult).then_inc(*S.tick())
                nc.vector.tensor_tensor(r_bk[:, 2:4, :], r_kd, r_ex[:, 4:6, :], ALU.mult).then_inc(*S.tick("bk"))
                for d in range(2):
                    dve.wait_ge(*s_rwkv.pe.at(f"scores{d}", it))
                    for hh in range(2):
                        s_ = 2 * d + hh
                        nc.vector.tensor_tensor(r_sc[:, s_, :].rearrange("p (a b) -> p a b", b=320)[:, :, 0:256], ps[2 + s_][:, :].rearrange("p (a b) -> p a b", a=2),
                                                tab[:, T_MASK + 512 * d:T_MASK + 512 * (d + 1)].rearrange("p (a b) -> p a b", a=2), ALU.mult).then_inc(*S.tick("sc"))
                    dve.wait_ge(*S.so_far())
                    inverse_dve_start(dve, S, d, r_sc[:, 2 * d:2 * d + 2, 0:P])
                dve.wait_ge(*s_rwkv.act.at("tm", it))
                for d in range(2):
                    bv = bonusf[:, bass.ds(tiles[d] * RH + ft * 2, 2)]
                    nc.vector.tensor_tensor(bv, bv, ps[7][:, 256 + 2 * d:258 + 2 * d], ALU.add).then_inc(*S.tick("bonus"))
                    nc.vector.tensor_scalar(r_zin[:, d, :], zst[:, bass.ds(ft * RD + 256 * d, RD)], r_h[:, d:d + 1], None, ALU.mult).then_inc(*S.tick())
                    dve.wait_ge(*S.so_far())
                inverse_dve(dve, S, s_rwkv, it)
                for d in range(2):
                    dve.wait_ge(*s_rwkv.pe.at(f"c{d}", it))
                    nc.vector.tensor_tensor(r_q1[:, d, :], ps[d][:, 0:P], r_ar[:, d, P:2 * P], ALU.add).then_inc(*S.tick())
                    nc.vector.tensor_tensor(r_t1[:, d, :], ps[d][:, P:P + RD], tab[:, T_EYE:T_EYE + RD], ALU.add).then_inc(*S.tick("t1"))
                dve.wait_ge(*s_rwkv.pe.at("y", it))
                for d in range(2):
                    for hh in range(2):
                        yv = y_r[:, bass.ds(tiles[d] * RW + ft * P + RD * hh, RD)]
                        nc.vector.tensor_tensor(yv, yv, ps[(2, 5)[hh]][:, RD * d:RD * (d + 1)], ALU.add).then_inc(*S.tick())
                    dve.wait_ge(*S.so_far())
                dve.wait_ge(*s_rwkv.pe.at("t2", it))
                for hh in range(2):
                    rows = slice(RD * hh, RD * (hh + 1))
                    for d in range(2):
                        nc.vector.tensor_scalar(r_zn[rows, d, :], ps[3 + hh][rows, RD * d:RD * (d + 1)], r_h[rows, d:d + 1], None, ALU.mult).then_inc(*S.tick())
                dve.wait_ge(*S.so_far())
                dve.sem_inc(waited, 1)
                for d in range(2):
                    nc.vector.tensor_copy(zst[:, bass.ds(ft * RD + 256 * d, RD)], r_zn[:, d, :]).then_inc(*S.tick("last"))

            with dve.Fori(0, FT) as ft:
                rwkv_dve(ft, ft, (0, 0))
            dve.wait_ge(*s_zs.act.at("zst"))
            with dve.Fori(1, NT) as n:
                with dve.Fori(0, FT) as ft:
                    rwkv_dve(n * FT + ft, ft, (n, NT - n))
            S = s_tail.dve
            dve.sem_inc(*S.open())
            dve.wait_ge(cst_in, 16 * 9)
            dve.wait_ge(*s_route.act.at("sgl"))
            for c in range(2):
                nc.vector.scalar_tensor_tensor(modk[:, c, 2, :], modk[:, c, 2, :], 1.0, bias_row[:, :], ALU.add, ALU.mult).then_inc(*s_route.dve.tick("gain2"))
            dve.wait_ge(*s_route.dve.so_far())
            xd, zd, vd = x[:, :, :].rearrange("p t n -> p (t n)"), z_tm[:, :, :].rearrange("p t n -> p (t n)"), v_tm[:, :, :].rearrange("p t n -> p (t n)")
            b3 = lambda ap, n: ap.unsqueeze(2).to_broadcast([P, ap.shape[-1], n])
            ohd, ohsd, gad = scr[:, 0, :], scr[:, 1, 0:NT * NE], scr[:, 1, 2 * NT * NE:2 * NT * NE + 2 * NT]

            def tail_dve(it, c):
                S.begin(it)
                dve.wait_ge(*S.so_far())
                dve.sem_inc(waited, 1)

                def then(ins, name=None):
                    ins.then_inc(*S.tick(name))
                    dve.wait_ge(*S.so_far())
                then(nc.vector.tensor_copy(t_sgl, fmd[:, bass.ds(it * P + (FM_LORA + 1) * TOK, P)]), "sgl")
                y3 = y_r[:, bass.ds(it * RW, RW)].rearrange("p (h n) -> p h n", n=RD)
                ta3, tb3 = ta.rearrange("p (h n) -> p h n", n=RD), tb.rearrange("p (h n) -> p h n", n=RD)
                then(nc.vector.tensor_reduce(t_st[:, 0:8], y3, AX.X, ALU.add))
                then(nc.vector.tensor_scalar(t_st[:, 0:8], t_st[:, 0:8], 1.0 / RD, None, ALU.mult))
                then(nc.vector.tensor_tensor(ta3, y3, b3(t_st[:, 0:8], RD), ALU.subtract), "yc")
                dve.wait_ge(*s_tail.act.at("ysq", it))
                then(nc.vector.tensor_reduce(t_st[:, 8:16], tb3, AX.X, ALU.add))
                then(nc.vector.tensor_scalar(t_st[:, 16:24], t_st[:, 8:16], 1.0 / RD, LNX_EPS, ALU.mult, ALU.add))
                yg = y_gf[:, bass.ds(it * 512, 512)]
                then(nc.vector.tensor_tensor(tb, yg, yg, ALU.mult))
                then(nc.vector.tensor_reduce(t_st[:, 8:12], tb.rearrange("p (h n) -> p h n", n=GD), AX.X, ALU.add))
                then(nc.vector.tensor_scalar(t_st[:, 24:28], t_st[:, 8:12], 1.0 / GD, NORM_EPS, ALU.mult, ALU.add), "var")
                dve.wait_ge(*s_tail.act.at("sd", it))
                then(nc.vector.reciprocal(t_st[:, 16:28], t_st[:, 16:28]))
                then(nc.vector.tensor_tensor(ta3, ta3, b3(t_st[:, 16:24], RD), ALU.mult))
                then(nc.vector.tensor_tensor(ta, ta, lnx_g, ALU.mult))
                then(nc.vector.tensor_tensor(ta, ta, lnx_b, ALU.add))
                then(nc.vector.tensor_copy(t_st[:, 8:16], bonusf[:, bass.ds(it * RH, RH)]))
                then(nc.vector.tensor_tensor(tb3, vd[:, bass.ds(it * RW, RW)].rearrange("p (h n) -> p h n", n=RD), b3(t_st[:, 8:16], RD), ALU.mult))
                then(nc.vector.tensor_tensor(ta, ta, tb, ALU.add))
                dve.wait_ge(*s_tail.pe.at("gate", it))
                then(nc.vector.tensor_tensor(o_tm[:, 0:RW], ta, ps[0][:, :], ALU.mult), "gn")
                then(nc.vector.tensor_tensor(tb.rearrange("p (h n) -> p h n", n=GD), yg.rearrange("p (h n) -> p h n", n=GD), b3(t_st[:, 24:28], GD), ALU.mult))
                then(nc.vector.tensor_tensor(tb.rearrange("p (h n) -> p h n", n=GD), tb.rearrange("p (h n) -> p h n", n=GD), gng.unsqueeze(1).to_broadcast([P, GH, GD]), ALU.mult))
                dve.wait_ge(*s_tail.act.at("sz", it))
                then(nc.vector.tensor_tensor(o_tm[:, RW:D], tb, ta, ALU.mult), "o")
                for b in range(2):
                    dve.wait_ge(*s_tail.pe.at(f"mix{b}", it))
                    then(nc.vector.tensor_tensor(ta, ps[3 + b][:, :], modk[:, c, 0, 512 * b:512 * (b + 1)], ALU.mult))
                    xb = xd[:, bass.ds(it * D + 512 * b, 512)]
                    then(nc.vector.tensor_tensor(xb, xb, ta, ALU.add), "x2")
                dve.wait_ge(*s_tail.act.at("ssq", it))
                then(nc.vector.tensor_scalar(t_st[:, 33:34], t_st[:, 32:33], 1.0 / D, NORM_EPS, ALU.mult, ALU.add), "var2")
                dve.wait_ge(*s_tail.act.at("sd2", it))
                then(nc.vector.reciprocal(t_st[:, 34:35], t_st[:, 33:34]))
                if c:
                    dve.wait_ge(h2_out, it * 16)
                then(nc.vector.scalar_tensor_tensor(h2, xd[:, bass.ds(it * D, D)], t_st[:, 34:35], modk[:, c, 2, :], ALU.mult, ALU.mult))
                then(nc.vector.tensor_tensor(h2, h2, modk[:, c, 1, :], ALU.add), "h2")
                dve.wait_ge(*s_tail.pe.at("logits", it))
                then(nc.vector.memset(lg[:, 0:8], -BIG))
                then(nc.vector.tensor_tensor(lg[:, 0:4], ps[7][:, 0:GROUPS], rtb[:, 0:GROUPS], ALU.add))
                then(nc.vector.tensor_tensor(el, ps[7][:, GROUPS:GROUPS + NE], rtb[:, GROUPS:], ALU.add))
                dve.sem_inc(waited, 1)
                then(nc.vector.max(m8, lg[:, 0:8]))
                dve.sem_inc(waited, 1)
                then(nc.vector.max_index(mi8.bitcast(mybir.dt.uint32), m8, lg[:, 0:8]))
                then(nc.vector.tensor_scalar(lt_[:, 4:5], m8[:, 0:1], -1.0, None, ALU.mult), "gmax")
                then(nc.vector.tensor_copy(lt_[:, 7:8], mi8[:, 0:1]))
                then(nc.vector.tensor_scalar(lt_[:, 8:12], tab[:, T_IOTA:T_IOTA + GROUPS], lt_[:, 7:8], None, ALU.is_equal))
                then(nc.vector.tensor_scalar(lt_[:, 12:16], lt_[:, 8:12], BIG, -BIG, ALU.mult, ALU.add))
                el3, el23 = el.rearrange("p (g n) -> p g n", n=PER_GROUP), el2.rearrange("p (g n) -> p g n", n=PER_GROUP)
                then(nc.vector.tensor_tensor(el23, el3, b3(lt_[:, 8:12], PER_GROUP), ALU.mult))
                then(nc.vector.tensor_tensor(el23, el23, b3(lt_[:, 12:16], PER_GROUP), ALU.add))
                dve.sem_inc(waited, 1)
                then(nc.vector.max(m8, el2))
                dve.sem_inc(waited, 1)
                then(nc.vector.max_index(mi8.bitcast(mybir.dt.uint32), m8, el2))
                dve.wait_ge(*s_tail.act.at("gsum", it))
                then(nc.vector.tensor_tensor(lt_[:, 6:7], m8[:, 1:2], m8[:, 0:1], ALU.subtract), "e2")
                then(nc.vector.tensor_copy(lt_[:, 8:10], mi8[:, 0:2]))
                for k in range(2):
                    then(nc.vector.tensor_scalar(ohd[:, bass.ds(it * NE + NT * NE * k, NE)], tab[:, T_BIOTA:T_BIOTA + NE], lt_[:, 8 + k:9 + k], None, ALU.is_equal))
                then(nc.vector.tensor_tensor(ohsd[:, bass.ds(it * NE, NE)], ohd[:, bass.ds(it * NE, NE)], ohd[:, bass.ds(it * NE + NT * NE, NE)], ALU.add))
                dve.wait_ge(*s_tail.act.at("e2", it))
                then(nc.vector.tensor_scalar(lt_[:, 10:11], lt_[:, 6:7], 1.0, lt_[:, 5:6], ALU.add, ALU.mult))
                then(nc.vector.reciprocal(lt_[:, 10:11], lt_[:, 10:11]))
                then(nc.vector.tensor_tensor(lt_[:, 11:12], lt_[:, 10:11], lt_[:, 6:7], ALU.mult))
                dve.sem_inc(waited, 1)
                then(nc.vector.tensor_copy(gad[:, bass.ds(it * 2, 2)], lt_[:, 10:12]), "last")

            tail_dve(0, 0)
            with dve.Fori(1, NT) as t:
                tail_dve(t, 1)
            S = s_route.dve

            def then(ins, name=None):
                ins.then_inc(*S.tick(name))
                dve.wait_ge(*S.so_far())
            dve.wait_ge(*s_route.pe.at("rank"))
            then(nc.vector.tensor_copy(cnt, ps[0][:, NE * NT:NE * (NT + 1)]))
            big = oT.rearrange("p k n -> p (k n)")[:, 0:NE * 10].rearrange("p (e m) -> p e m", m=10)
            then(nc.vector.tensor_tensor(big, b3(cnt, 10), tab[:, T_THR:T_THR + 10].unsqueeze(1).to_broadcast([P, NE, 10]), ALU.is_gt))
            then(nc.vector.tensor_reduce(nblk, big, AX.X, ALU.add))
            then(nc.vector.tensor_tensor_scan(pend, ones[:, 0:NE], nblk, 0.0, ALU.mult, ALU.add))
            then(nc.vector.tensor_tensor(base, pend, nblk, ALU.subtract))
            then(nc.vector.tensor_scalar(base, base, float(BT), None, ALU.mult))
            then(nc.vector.tensor_tensor(slotm, ps[0][:, 0:NE * NT].rearrange("p (t e) -> p t e", e=NE), base.unsqueeze(1).to_broadcast([P, NT, NE]), ALU.add))
            for k in range(2):
                then(nc.vector.tensor_tensor(oh[:, k], oh[:, k], slotm, ALU.mult))
                then(nc.vector.tensor_reduce(slot_f[:, :, k], oh[:, k], AX.X, ALU.add))
            then(nc.vector.tensor_copy(slot_i, slot_f), "slots")
            big2 = tl[:, 0:NB * NE].rearrange("p (b e) -> p b e", e=NE)
            then(nc.vector.tensor_tensor(big2, pend.unsqueeze(1).to_broadcast([P, NB, NE]), b3(tab[:, T_BIOTA:T_BIOTA + NB], NE), ALU.is_le))
            then(nc.vector.tensor_reduce(ebf, big2, AX.X, ALU.add))
            then(nc.vector.tensor_scalar(ebf, ebf, float(NE - 1), None, ALU.min))
            then(nc.vector.tensor_copy(eb_i[:, NB:NB + 1], pend[:, NE - 1:NE]))
            then(nc.vector.tensor_copy(eb_i[:, 0:NB], ebf), "eb")
            n_blocks = dve.value_load(eb_i[0:1, NB:NB + 1], min_val=0, max_val=NB)
            S = s_moe.dve
            dve.sem_inc(*S.open())
            with dve.Fori(0, NB // 2) as j:
                S.begin(j)
                for u in range(2):
                    with dve.If(j * 2 + u < n_blocks):
                        dve.wait_ge(*s_moe.act.at(f"silu{u}", j))
                        dve.wait_ge(*s_moe.pe.at(f"up{u}", j))
                        nc.vector.tensor_tensor(e_h[u], e_h[u], ps[3][:, 0:256], ALU.mult).then_inc(*S.tick(f"h{u}"))
                        dve.wait_ge(*s_moe.pe.at(f"hT{u}", j))
                        dve.sem_inc(waited, 1)
                        nc.vector.tensor_copy(e_hT[u], ps[4][:, 0:256].rearrange("p (c h n) -> p c h n", c=2, h=2)).then_inc(*S.tick(f"hT{u}"))
                    dve.end_ifs()
            S = s_fin.dve
            dve.wait_ge(fin_in, 16)
            for t in range(NT):
                c = min(t, 1)
                for k in range(2):
                    dve.wait_ge(comb_in[k], 16 * (t + 1))
                then(nc.vector.tensor_scalar(comb(0), comb(0), gates[:, t, 0:1], None, ALU.mult))
                then(nc.vector.scalar_tensor_tensor(comb(2), comb(1), gates[:, t, 1:2], comb(0), ALU.mult, ALU.add))
                then(nc.vector.tensor_tensor(comb(2), comb(2), modk[:, c, 3, :], ALU.mult))
                then(nc.vector.tensor_tensor(x[:, t, :], x[:, t, :], comb(2), ALU.add), f"x{t}")
                dve.wait_ge(*s_fin.act.at(f"ssq{t}"))
                then(nc.vector.tensor_scalar(std[:, t:t + 1], ssq[:, t:t + 1], 1.0 / D, NORM_EPS, ALU.mult, ALU.add), f"var{t}")
                S.book[f"sum{t}"] = S.n
                dve.wait_ge(*s_fin.act.at(f"sd{t}"))
                then(nc.vector.reciprocal(rstd[:, t:t + 1], std[:, t:t + 1]))
                then(nc.vector.scalar_tensor_tensor(x[:, t, :], x[:, t, :], rstd[:, t:t + 1], bias_row[:, :], ALU.mult, ALU.mult), f"out{t}")


INS = ['x_prompt', 'x_sample', 'state_rwkv', 'state_gdn', 'c', 'c_ctx', 'ada_w', 'ada_b', 'norm1_g', 'norm2_g',
       'w_in', 'w_out', 'rwkv_w0', 'rwkv_w2', 'rwkv_a0', 'rwkv_a2', 'rwkv_g2', 'rwkv_k_k', 'rwkv_k_a', 'rwkv_r_k',
       'rwkv_lnx_g', 'rwkv_lnx_b', 'gdn_conv', 'gdn_a_log', 'gdn_dt_bias', 'gdn_norm_g', 'router_group_w',
       'router_group_b', 'router_expert_w', 'router_expert_b', 'expert_gate', 'expert_up', 'expert_down', 'final_norm_g']
OUTS = [('y_prompt', (1, CTX, D)), ('y_sample', (1, LAT, D)), ('new_rwkv', (1, 1, 2, RH, RD, RD)), ('new_gdn', (1, 1, 2, GH, GD, GD))]


def kernel(**inputs):
    import concourse.bacc as bacc
    from concourse.bass_utils import run_bass_kernel_spmd

    arrays = {f"in_{n}": np.ascontiguousarray(inputs[n]) for n in INS}
    arrays["in_tables"] = shape_tables()
    book = {}
    for _ in range(2):
        nc = bacc.Bacc("TRN2", target_bir_lowering=False, num_devices=1)
        A = {n[3:]: nc.dram_tensor(n, a.shape, mybir.dt.from_np(a.dtype), kind="ExternalInput").ap() for n, a in arrays.items()}
        O = {n: nc.dram_tensor(f"out_{n}", shape, F32, kind="ExternalOutput").ap() for n, shape in OUTS}
        program(nc, A, O, book)
    got = run_bass_kernel_spmd(nc, [arrays], core_ids=[0]).results[0]
    return tuple(got[f"out_{n}"] for n, _ in OUTS)
```

```python
from contextlib import ExitStack

import numpy as np

import concourse.bass as bass
from concourse import mybir

F32 = mybir.dt.float32
I32 = mybir.dt.int32
ALU = mybir.AluOpType
ACT = mybir.ActivationFunctionType
AX = mybir.AxisListType

P = 128
D = 1024
KD = D // P
CTX, LAT = 128, 512
TOK = CTX + LAT
NT = TOK // P
HALF = TOK // 2
COLS = 512
ROW = 64
RW = 512
RH, RD = 8, 64
FT = RW // P
GH, GD = 4, 128
IN_COLS = 3856
ADA = 6 * D
ADA_BLOCKS = ADA // COLS
C_R, C_K, C_V, C_LORA, C_Q2, C_K2, C_V2, C_Z, C_BA = 0, 512, 1024, 1536, 1792, 2304, 2816, 3328, 3840
FM_R, FM_K, FM_Q2, FM_K2, FM_V2, FM_LORA = 0, 4, 8, 12, 16, 20
FM_TILES = 22
NORM_EPS = 1e-6
LNX_EPS = 64e-5
DECAY = float(np.exp(-0.5))
LEVELS = 7
NE, GROUPS, PER_GROUP = 32, 4, 8
FE = 512
BT = 64
NB = NE + (2 * TOK - NE) // BT
NB += NB % 2
SLOTS = NB * BT
BIG = 1e30

T_ID, T_ONE, T_BLK, T_MASK, T_LVL, T_EYE, T_SEL, T_HEAD, T_IOTA, T_BIOTA, T_THR, T_END = (
    0, 128, 256, 384, 1408, 3200, 3264, 3520, 3522, 3526, 3526 + NB, 3526 + NB + 10)


def shape_tables():
    t = np.zeros((P, T_END), np.float32)
    r = np.arange(P)
    j, i = r[:, None], r[None, :]
    t[:, T_ID:T_ID + P] = j == i
    t[:, T_ONE:T_ONE + P] = 1
    t[:, T_BLK:T_BLK + P] = j // RD == i // RD
    for d, (strict, incl) in enumerate(((j < i, j <= i), (j > i, j >= i))):
        for n, m in enumerate((strict, incl, strict, incl)):
            t[:, T_MASK + 512 * d + P * n:T_MASK + 512 * d + P * (n + 1)] = m
    for k in range(LEVELS):
        s = 2 ** k
        lower = (j // s == i // s + 1) & (i // s % 2 == 0)
        t[:, T_LVL + P * k:T_LVL + P * (k + 1)] = lower
        t[:, T_LVL + P * (LEVELS + k):T_LVL + P * (LEVELS + k + 1)] = lower.T
    t[:, T_EYE:T_EYE + RD] = j % RD == r[None, :RD]
    for c in range(2):
        t[c, T_SEL + P * c:T_SEL + P * (c + 1)] = 1
    for h in range(2):
        t[:, T_HEAD + h] = r // RD == h
    t[:, T_IOTA:T_IOTA + GROUPS] = r[:GROUPS]
    t[:, T_BIOTA:T_BIOTA + NB] = np.arange(NB)
    t[:, T_THR:T_THR + 10] = BT * np.arange(10)
    return t


class Steps:

    def __init__(self, sem, book, key, loop):
        self.sem, self.loop = sem, loop
        self.book = book.setdefault(key, {"per": 1})
        self.n, self.it = 0, 0

    def open(self):
        return self.sem, self.book["per"]

    def begin(self, it):
        self.it, self.n = it, 0

    def tick(self, name=None):
        self.n += 1
        if name is not None:
            self.book[name] = self.n
        self.book["per"] = max(self.book["per"], self.n)
        return self.sem, 1

    def at(self, name, it=0, back=0):
        v = self.book.get(name, 1)
        return (self.sem, (it + 1 - back) * self.book["per"] + v) if self.loop else (self.sem, v)

    def so_far(self):
        return (self.sem, (self.it + 1) * self.book["per"] + self.n) if self.loop else (self.sem, self.n)


class Stage:
    def __init__(self, ctx, nc, book, name, loop):
        mk = lambda e: Steps(ctx.enter_context(nc.semaphore(f"{name}_{e}")), book, f"{name}_{e}", loop)
        self.pe, self.act, self.dve, self.pool, self.sp = (mk(e) for e in ("pe", "act", "dve", "pool", "sp"))


def program(nc, A, O, book, dbg=None):
    ctx = ExitStack()
    with ctx:
        sb = lambda name, shape, dt=F32: ctx.enter_context(nc.sbuf_tensor(name, shape, dt))
        sem = lambda name: ctx.enter_context(nc.semaphore(name))
        flat = lambda ap: ap.rearrange("p a b -> p (a b)")
        tab = sb("tab", [P, T_END])
        x = sb("x", [P, NT, D])
        modk = sb("modk", [P, 2, 4, D])
        ring = sb("ring", [P, 2, KD, COLS])
        fm = sb("fm", [P, FM_TILES, TOK])
        hT = sb("hT", [P, KD, TOK])
        v_tm = sb("v_tm", [P, NT, RW])
        z_tm = sb("z_tm", [P, NT, RW])
        ba = sb("ba", [P, NT, 16])
        bias_row = sb("bias_row", [P, D])
        small = sb("small", [P, 64])
        par = sb("par", [P, 64])
        cw = sb("cw", [P, 12, 4])
        moda = fm[:, 0:7, :].rearrange("p a b -> p (a b)")[:, 0:4096].rearrange("p (c s n) -> p c s n", c=2, s=2)
        modrow = fm[:, 8:18, :].rearrange("p a b -> p (a b)")[0:2, 0:ADA]
        hrow = z_tm[:, 0:2, :].rearrange("p a b -> p (a b)")
        hrow2 = z_tm[:, 2:4, :].rearrange("p a b -> p (a b)")
        ps = [ctx.enter_context(nc.psum_tensor(f"ps{i}", [P, 512], F32)) for i in range(8)]

        scr = sb("scr", [P, 3, TOK])
        gs = sb("gs", [P, 2, NT, GH, 4])
        gtmp = sb("gtmp", [P, 4, NT, 8])
        bonus = sb("bonus", [P, NT, RH])
        rpar = sb("rpar", [P, FT, 8])
        hst = sb("hst", [P, 16])
        ringf = ring[:, :, :, :].rearrange("p u k n -> p (u k n)")
        hTf = hT[:, :, :].rearrange("p k n -> p (k n)")
        quad = lambda ap, n: ap.rearrange("p (s n) -> p s n", n=n)
        g_kq, g_et, g_eg, g_lt = quad(ringf[:, 0:1024], 256), quad(ringf[:, 1024:1536], P), quad(ringf[:, 1536:2048], P), quad(ringf[:, 2048:2560], P)
        g_qk, g_rhs, g_w = quad(ringf[:, 2560:3584], 256), quad(ringf[:, 3584:4608], 256), quad(ringf[:, 4608:5632], 256)
        i_x, i_xt, i_y = quad(ringf[:, 5632:6144], P), quad(ringf[:, 6144:6656], P), quad(ringf[:, 6656:7168], P)
        g_q1, g_t1 = quad(ringf[:, 7168:7680], P), quad(ringf[:, 7680:8192], P)
        g_state = hTf[:, 0:1024].rearrange("p (d n) -> p d n", d=2)
        g_gb, g_vf = quad(hTf[:, 1024:1536], P), quad(hTf[:, 1536:2048], P)
        g_sc, g_egl = hTf[:, 2048:2064].rearrange("p (s n) -> p s n", n=4), hTf[:, 2064:2068]
        y_g = hTf[:, 2560:5120].rearrange("p (t n) -> p t n", t=NT)

        r_sc = quad(ringf[:, 0:2560], 640)
        r_ar, r_bk = quad(ringf[:, 2560:3072], 256), quad(ringf[:, 3072:3584], P)
        r_rhs, r_w, r_q1 = quad(ringf[:, 3584:4096], P), quad(ringf[:, 4096:4608], P), quad(ringf[:, 4608:4864], P)
        r_t1, r_ktm, r_zn, r_zin = quad(ringf[:, 4864:4992], RD), quad(ringf[:, 4992:5248], RD), quad(ringf[:, 5248:5376], RD), quad(ringf[:, 5376:5504], RD)
        r_eu, r_cs = quad(ringf[:, 7168:7680], P), quad(ringf[:, 7680:7936], P)
        work = fm[:, FM_V2:FM_V2 + 4, :].rearrange("p a b -> p (a b)")
        r_ex, r_pq, r_kd, r_kka = quad(work[:, 0:768], P), quad(work[:, 768:1280], P), quad(work[:, 1280:1536], P), quad(work[:, 1536:1792], P)
        r_rr, r_lw, r_lora = quad(work[:, 1792:2048], P), quad(work[:, 2048:2304], P), quad(work[:, 2304:2560], P)
        lora = hTf[:, 0:1024]
        zst = hTf[:, 1024:1536]
        znat = hTf[:, 1536:2560]
        r_v = quad(ringf[:, 7936:8192], P)
        r_par, r_ht, r_h, r_hc = hst[:, 0:8], hst[:, 8:10], hst[:, 10:12], hst[:, 12:14]
        kk_root = ringf[:, 2560:5120].rearrange("p (f n) -> p f n", f=FT)
        r_keep = quad(bias_row[:, 0:256], P)
        y_r = fm[:, FM_K2:FM_K2 + 4, :].rearrange("p a b -> p (a b)")

        tl = fm[:, 0:8, :].rearrange("p a b -> p (a b)")
        o_tm, oT, h2, h2T = tl[:, 0:D], quad(tl[:, D:2 * D], P), tl[:, 2 * D:3 * D], quad(tl[:, 3 * D:4 * D], P)
        ta, tb = tl[:, 4 * D:4 * D + 512], tl[:, 4 * D + 512:5 * D]
        cst = fm[:, FM_Q2:FM_Q2 + 4, :].rearrange("p a b -> p (a b)")
        g2w, lnx_g, lnx_b, gng = cst[:, 0:512], cst[:, 512:1024], cst[:, 1024:1536], cst[:, 1536:1664]
        t_st, t_sgl, rtb = cst[:, 1664:1728], cst[:, 1728:1856], cst[:, 1856:1892]
        rw_ = work[:, 0:288].rearrange("p (k n) -> p k n", n=GROUPS + NE)
        lg, el, el2, m8, lt_ = work[:, 288:324], work[:, 324:356], work[:, 356:388], work[:, 388:396], work[:, 396:412]
        wout = ringf.rearrange("p (k n) -> p k n", n=D)
        oh = scr[:, 0, 0:2 * NT * NE].rearrange("p (k t e) -> p k t e", k=2, t=NT)
        ohs = scr[:, 1, 0:NT * NE].rearrange("p (t e) -> p t e", t=NT)
        slotm = scr[:, 1, NT * NE:2 * NT * NE].rearrange("p (t e) -> p t e", t=NT)
        gates = scr[:, 1, 2 * NT * NE:2 * NT * NE + 2 * NT].rearrange("p (t k) -> p t k", k=2)
        slot_f = scr[:, 1, 340:350].rearrange("p (t k) -> p t k", k=2)
        cnt, nblk, pend, base = scr[:, 1, 352:384], scr[:, 1, 384:416], scr[:, 1, 416:448], scr[:, 1, 448:480]
        ebf = scr[:, 1, 480:480 + NB]
        gi = sb("gi", [P, 2 * NT + NT + NB + 1 + NB + 2 + 8], I32)
        zeros = scr[:, 2, 0:256]
        slot_i, tid, eb_i = gi[:, 0:10].rearrange("p (t k) -> p t k", k=2), gi[:, 10:15], gi[:, 15:15 + NB + 1]
        tok_i, idx_u = gi[0:BT, 16 + NB:16 + 2 * NB], gi[0:BT, 16 + 2 * NB:18 + 2 * NB]
        mi8 = gi[:, 18 + 2 * NB:26 + 2 * NB]
        zi = cw[0:NB, :, :].rearrange("p a b -> p (a b)").bitcast(I32)
        e_w = [(ring[:, 0], ring[:, 1], hTf[:, 0:4096].rearrange("p (k n) -> p k n", n=D)),
               tuple(flat(fm[:, :, :])[:, 4096 * i:4096 * (i + 1)].rearrange("p (k n) -> p k n", n=(COLS, COLS, D)[i]) for i in range(3))]
        vf_, zf_ = v_tm[:, :, :].rearrange("p t n -> p (t n)"), z_tm[:, :, :].rearrange("p t n -> p (t n)")
        e_x = [vf_[0:BT, D * u:D * (u + 1)] for u in range(2)]
        e_xT = [zf_[:, 512 * u:512 * (u + 1)].rearrange("p (k n) -> p k n", n=BT) for u in range(2)]
        e_h = [zf_[:, 1024 + 256 * u:1280 + 256 * u] for u in range(2)]
        e_hT = [zf_[:, 1536 + 256 * u:1792 + 256 * u].rearrange("p (c h n) -> p c h n", c=2, h=2) for u in range(2)]
        e_y = [vf_[:, 2048:2560], zf_[:, 2048:2560]]
        h2d = nc.dram_tensor("h2_rows", (TOK, D), F32).ap()
        tokd = nc.dram_tensor("slot_token", (NB * BT, 1), I32).ap()
        yd = nc.dram_tensor("expert_rows", (NB * BT, D), F32).ap()

        ident = tab[:, T_ID:T_ID + P]
        ones = tab[:, T_ONE:T_ONE + P]
        blk64 = tab[:, T_BLK:T_BLK + P]

        tab_in, x_in, c_in, gain_in, par_in = sem("tab_in"), sem("x_in"), sem("c_in"), sem("gain_in"), sem("par_in")
        bias_in = sem("bias_in")
        ring_in = [sem("ring0_in"), sem("ring1_in")]
        ring_used = [sem("ring0_used"), sem("ring1_used")]
        out_done = sem("out_done")

        ST = lambda name, loop: Stage(ctx, nc, book, name, loop)
        s_ada, s_norm, s_fm, s_tm, s_prep = ST("ada", True), ST("norm", False), ST("fm", True), ST("tm", False), ST("prep", False)
        s_conv, s_l2, s_gdn, s_rwkv = ST("conv", True), ST("l2", True), ST("gdn", True), ST("rwkv", True)
        s_gp = ST("gdn_prep", True)
        s_kk, s_zs, s_rp = ST("kk", False), ST("zs", False), ST("rwkv_prep", True)
        lora_in, rzero, rstate_in, rstate_out = sem("lora_in"), sem("rzero"), sem("rstate_in"), sem("rstate_out")
        s_mix, s_tail, s_route, s_fin = ST("mix", True), ST("tail", True), ST("route", False), ST("fin", False)
        s_moe = ST("moe", True)
        wout_in, cst_in, h2_out, tz_out, tok_out, tok_in = (sem(n) for n in ("wout_in", "cst_in", "h2_out", "tz_out", "tok_out", "tok_in"))
        fin_in = sem("fin_in")
        gu_in, dn_in = [sem("gu0_in"), sem("gu1_in")], [sem("dn0_in"), sem("dn1_in")]
        rows_in, y_out = [sem("rows0_in"), sem("rows1_in")], [sem("y0_out"), sem("y1_out")]
        eps_ready = sem("eps_ready")
        zeros_ready, yd_zeroed = sem("zeros_ready"), sem("yd_zeroed")
        comb_in = [sem("comb0_in"), sem("comb1_in")]
        waited = sem("waited")
        state_in, state_out, zeroed = sem("state_in"), sem("state_out"), sem("zeroed")

        def lower_mask(d, k):
            return tab[:, T_LVL + P * (LEVELS * d + k):T_LVL + P * (LEVELS * d + k + 1)].bitcast(I32).unsqueeze(1).to_broadcast([P, 2, P])

        def two(ap, n=2):
            return ap.unsqueeze(1).to_broadcast([P, n, ap.shape[-1]])

        def incl(d):
            return tab[:, T_MASK + 512 * d + P:T_MASK + 512 * d + 2 * P]

        def pair(ap, d):
            return ap[:, 2 * d:2 * d + 2, :]

        def next_of(eng, it, tiles, per=FT):
            total = NT * per
            j = eng.snap(it + 1 - (it + 1 + 32 - total) // 32, min_val=0, max_val=total - 1)
            n = eng.snap(j // per, min_val=0, max_val=NT - 1)
            ft = eng.snap(j % per, min_val=0, max_val=per - 1)
            back = n * (NT - 1) if isinstance(tiles[0], int) else NT - n
            return ft, (n, back)

        def keep_clock(bank, n):
            for _ in range(n):
                nc.tensor.matmul(ps[bank][:, 0:P], ident, ident, start=True, stop=True)

        def inverse_pe(pe, S, T, it, lt, beside={}):
            for d in range(2):
                pe.wait_ge(*T.dve.at(f"xt0{d}", it))
                for hh in range(2):
                    m = nc.tensor.transpose(ps[6 + d][:, P * hh:P * (hh + 1)], i_xt[:, 2 * d + hh, :], ident)
                m.then_inc(*S.tick(f"x0{d}"))
            if 0 in beside:
                beside[0]()
            for k in range(1, LEVELS):
                for d in range(2):
                    pe.wait_ge(*(T.act.at(f"x0{d}", it) if k == 1 else T.dve.at(f"xt{k - 1}{d}", it)))
                    for hh in range(2):
                        s_ = 2 * d + hh
                        m = nc.tensor.matmul(ps[d][:, P * hh:P * (hh + 1)], lt(s_), i_x[:, s_, :], start=True, stop=True)
                    m.then_inc(*S.tick(f"y{k}{d}"))
                for d in range(2):
                    pe.wait_ge(*T.act.at(f"y{k}{d}", it))
                    if k < LEVELS - 1:
                        for hh in range(2):
                            s_ = 2 * d + hh
                            m = nc.tensor.matmul(ps[2 + d][:, P * hh:P * (hh + 1)], i_xt[:, s_, :], i_y[:, s_, :], start=True, stop=True)
                        m.then_inc(*S.tick(f"x{k}{d}"))
                    for hh in range(2):
                        s_ = 2 * d + hh
                        m = nc.tensor.matmul(ps[4 + d][:, P * hh:P * (hh + 1)], i_y[:, s_, :], i_xt[:, s_, :], start=True, stop=True)
                    m.then_inc(*S.tick(f"xt{k}{d}"))
                if k in beside:
                    beside[k]()

        def inverse_act(act, S, T, it, beside={}):
            for d in range(2):
                act.wait_ge(*T.pe.at(f"x0{d}", it))
                nc.scalar.copy(pair(i_x, d), ps[6 + d][:, 0:256].rearrange("p (s n) -> p s n", n=P)).then_inc(*S.tick(f"x0{d}"))
            for k in range(1, LEVELS):
                for d in range(2):
                    act.wait_ge(*T.pe.at(f"y{k}{d}", it))
                    nc.scalar.copy(pair(i_y, d), ps[d][:, 0:256].rearrange("p (s n) -> p s n", n=P)).then_inc(*S.tick(f"y{k}{d}"))
                if k in beside:
                    beside[k]()

        def inverse_dve_start(dve, S, d, lt2):
            m0 = tab[:, T_LVL + P * LEVELS * (1 - d):T_LVL + P * LEVELS * (1 - d) + P]
            nc.vector.tensor_tensor(pair(i_xt, d), lt2, two(m0), ALU.mult).then_inc(*S.tick())
            dve.wait_ge(*S.so_far())
            nc.vector.tensor_tensor(pair(i_xt, d), pair(i_xt, d), two(ident), ALU.add).then_inc(*S.tick(f"xt0{d}"))

        def inverse_dve(dve, S, T, it, beside={}):
            for d in range(2):
                dve.wait_ge(*T.act.at(f"x0{d}", it))
            for k in range(1, LEVELS):
                for d in range(2):
                    if k < LEVELS - 1:
                        dve.wait_ge(*T.pe.at(f"x{k}{d}", it))
                        dve.sem_inc(waited, 1)
                        nc.vector.copy_predicated(pair(i_x, d), lower_mask(d, k), ps[2 + d][:, 0:256].rearrange("p (s n) -> p s n", n=P)).then_inc(*S.tick(f"x{k}{d}"))
                    dve.wait_ge(*T.pe.at(f"xt{k}{d}", it))
                    dve.sem_inc(waited, 1)
                    nc.vector.copy_predicated(pair(i_xt, d), lower_mask(1 - d, k), ps[4 + d][:, 0:256].rearrange("p (s n) -> p s n", n=P)).then_inc(*S.tick(f"xt{k}{d}"))
                if k in beside:
                    beside[k]()

        silc = par[:, 0:16].rearrange("p (k c) -> p k c", c=2)
        craw = par[:, 16:32].rearrange("p (c k) -> p c k", c=2)
        cexp = par[:, 32:48].rearrange("p (c k) -> p c k", c=2)
        ssq, std, rstd = small[:, 0:NT], small[:, 8:8 + NT], small[:, 16:16 + NT]
        l2_eps = small[:, 24:25]

        ada_d = A["ada_w"][0].rearrange("(k p) n -> p k n", p=P)
        win_d = A["w_in"][0].rearrange("(k p) n -> p k n", p=P)
        FM_USES = 4
        A_USES = ADA_BLOCKS // 2

        ctx.enter_context(nc.allow_non_contiguous_dma(reason="short per-feature parameter vectors"))
        block = ctx.enter_context(nc.Block())

        def comb(k):
            return tl[:, D * k:D * (k + 1)]


        @block.sync
        def _(sp):
            sp.dma_start(craw[:, 0, :], A["c_ctx"].rearrange("(k p) -> p k", p=P)).then_inc(c_in, 16)
            sp.dma_start(craw[:, 1, :], A["c"][0].rearrange("(k p) -> p k", p=P)).then_inc(c_in, 16)
            for u in range(2):
                sp.dma_start(ring[:, u], ada_d[:, :, COLS * u:COLS * (u + 1)]).then_inc(ring_in[u], 16)
            sp.dma_start(modrow, A["ada_b"][0].partition_broadcast(2)).then_inc(bias_in, 16)
            sp.dma_start(tab[:, :], A["tables"]).then_inc(tab_in, 16)
            sp.wait_ge(ring_in[0], 16)
            sp.dma_start(x[:, 0, :], A["x_prompt"][0]).then_inc(x_in, 16)
            sp.dma_start(x[:, 1:, :], A["x_sample"][0].rearrange("(t p) d -> p t d", p=P)).then_inc(x_in, 16)
            sp.dma_start(bias_row[:, :], A["norm1_g"][0].partition_broadcast(P)).then_inc(gain_in, 16)
            for w in range(3):
                sp.dma_start(cw[:, :, w], A["gdn_conv"][0, w].rearrange("(t p) -> p t", p=P)).then_inc(par_in, 16)
            sp.dma_start(par[:, 48:56], A["gdn_a_log"][0].rearrange("d h -> (d h)").partition_broadcast(P)).then_inc(par_in, 16)
            sp.dma_start(par[:, 56:64], A["gdn_dt_bias"][0].rearrange("d h -> (d h)").partition_broadcast(P)).then_inc(par_in, 16)
            for d in range(2):
                sp.dma_start(rpar[:, :, d], A["rwkv_w0"][0, d].rearrange("(f p) -> p f", p=P)).then_inc(par_in, 16)
                sp.dma_start(rpar[:, :, 2 + d], A["rwkv_a0"][0, d].rearrange("(f p) -> p f", p=P)).then_inc(par_in, 16)
            sp.dma_start(rpar[:, :, 4], A["rwkv_k_k"][0].rearrange("(f p) -> p f", p=P)).then_inc(par_in, 16)
            sp.dma_start(rpar[:, :, 5], A["rwkv_k_a"][0].rearrange("(f p) -> p f", p=P)).then_inc(par_in, 16)
            sp.dma_start(rpar[:, :, 7], A["rwkv_r_k"][0].rearrange("(f a) k -> (a k) f", a=2)).then_inc(par_in, 16)
            with sp.Fori(1, A_USES) as j:
                for u in range(2):
                    sp.wait_ge(ring_used[u], j)
                    sp.dma_start(ring[:, u], ada_d[:, :, bass.ds(j * 2 * COLS + COLS * u, COLS)]).then_inc(ring_in[u], 16)
            with sp.Fori(0, 2) as j:
                for u in range(2):
                    sp.wait_ge(ring_used[u], j + A_USES)
                    sp.dma_start(ring[:, u], win_d[:, :, bass.ds(j * C_Q2 + COLS * u, COLS)]).then_inc(ring_in[u], 16)
            for n, (c0, nc_) in enumerate(((C_V2, 512), (C_LORA, 256), (C_BA, 16), (C_V, 512), (C_Z, 512))):
                u = n % 2
                sp.wait_ge(ring_used[u], A_USES + 2 + n // 2)
                sp.dma_start(ring[:, u, :, 0:nc_], win_d[:, :, c0:c0 + nc_]).then_inc(ring_in[u], 16)
            sp.wait_ge(zeros_ready, 1)
            sp.dma_start(yd.rearrange('(p a) (b n) -> p (a b) n', p=P, n=256), zeros.unsqueeze(1).to_broadcast([P, NB * BT * D // (P * 256), 256])).then_inc(yd_zeroed, 16)
            g_dram = lambda ap: ap.rearrange("d h k v -> k d h v")
            g_sb = g_state.rearrange("p d (h v) -> p d h v", h=GH)
            sp.wait_ge(*s_gdn.dve.at("state", 1))
            sp.dma_start(g_dram(O["new_gdn"][0, 0]), g_sb).then_inc(state_out, 16)
            sp.wait_ge(state_out, 16)
            for d in range(2):
                sp.dma_start(g_sb[:, d], A["state_gdn"][0, 0, d].rearrange("h k v -> k h v")).then_inc(state_in, 16)
            sp.wait_ge(*s_gdn.dve.at("state", 2 * NT - 1))
            for d in range(2):
                sp.dma_start(lora[0:64, RW * d:RW * (d + 1)], A["rwkv_w2"][0, d]).then_inc(lora_in, 16)
                sp.dma_start(lora[64:128, RW * d:RW * (d + 1)], A["rwkv_a2"][0, d]).then_inc(lora_in, 16)
            z_dram = lambda ap: ap.rearrange("d h v k -> v (d h) k")
            z_sb = znat[0:RD, :].rearrange("v (n k) -> v n k", k=RD)
            sp.wait_ge(*s_zs.act.at("znat"))
            sp.dma_start(z_dram(O["new_rwkv"][0, 0]), z_sb).then_inc(rstate_out, 16)
            sp.wait_ge(rstate_out, 16)
            sp.dma_start(z_sb, z_dram(A["state_rwkv"][0, 0])).then_inc(rstate_in, 16)
            sp.wait_ge(*s_rwkv.dve.at("last", NT * FT - 1))
            sp.wait_ge(*s_rp.dve.at("bk", NT * FT))
            sp.wait_ge(*s_rp.pool.at("rr", NT * FT))
            sp.dma_start(g2w, A["rwkv_g2"][0]).then_inc(cst_in, 16)
            sp.dma_start(lnx_g, A["rwkv_lnx_g"][0].partition_broadcast(P)).then_inc(cst_in, 16)
            sp.dma_start(lnx_b, A["rwkv_lnx_b"][0].partition_broadcast(P)).then_inc(cst_in, 16)
            sp.dma_start(gng, A["gdn_norm_g"][0].partition_broadcast(P)).then_inc(cst_in, 16)
            sp.dma_start(rw_[:, :, 0:GROUPS], A["router_group_w"][0].rearrange("(k p) n -> p k n", p=P)).then_inc(cst_in, 16)
            sp.dma_start(rw_[:, :, GROUPS:], A["router_expert_w"][0].rearrange("(k p) n -> p k n", p=P)).then_inc(cst_in, 16)
            sp.dma_start(rtb[:, 0:GROUPS], A["router_group_b"][0].partition_broadcast(P)).then_inc(cst_in, 16)
            sp.dma_start(rtb[:, GROUPS:], A["router_expert_b"][0].partition_broadcast(P)).then_inc(cst_in, 16)
            sp.dma_start(bias_row[:, :], A["norm2_g"][0].partition_broadcast(P)).then_inc(cst_in, 16)
            sp.dma_start(wout, A["w_out"][0].rearrange("(k p) n -> p k n", p=P)).then_inc(wout_in, 16)
            sp.wait_ge(*s_route.pool.at("zi"))
            sp.dma_start(tokd.rearrange("(b s) o -> b (s o)", b=NB)[:, 0:48], zi[:, 0:48]).then_inc(tz_out, 16)
            sp.dma_start(tokd.rearrange("(b s) o -> b (s o)", b=NB)[:, 48:64], zi[:, 0:16]).then_inc(tz_out, 16)
            for it0, it1 in ((0, 1), (1, NT)):
                with sp.Fori(it0, it1) as t:
                    sp.wait_ge(*s_tail.dve.at("h2", t))
                    sp.dma_start(h2d[bass.ds(t * P, P), :], h2).then_inc(h2_out, 16)
            sp.wait_ge(*s_route.dve.at("eb"))
            n_blocks = sp.value_load(eb_i[0:1, NB:NB + 1], min_val=0, max_val=NB)
            eg = A["expert_gate"].rearrange("l e (k p) n -> p (l e k) n", p=P)
            eu = A["expert_up"].rearrange("l e (k p) n -> p (l e k) n", p=P)
            ed = A["expert_down"].rearrange("l e (k p) n -> p (l e k) n", p=P)
            sp.sem_inc(*s_moe.sp.open())
            with sp.Fori(0, NB // 2) as j:
                for u in range(2):
                    with sp.If(j * 2 + u < n_blocks):
                        e = sp.value_load(eb_i[0:1, bass.ds(j * 2 + u, 1)], min_val=0, max_val=NE - 1)
                        sp.wait_ge(*s_moe.pe.at(f"up{u}", j, 1))
                        if u == 1:
                            sp.wait_ge(rows_in[0], j * 16 + 16)
                        sp.dma_start(e_w[u][0], eg[:, bass.ds(e * KD, KD), :]).then_inc(gu_in[u], 16)
                        sp.dma_start(e_w[u][1], eu[:, bass.ds(e * KD, KD), :]).then_inc(gu_in[u], 16)
                        sp.wait_ge(*s_moe.pe.at(f"down{u}", j, 1))
                        sp.dma_start(e_w[u][2], ed[:, bass.ds(e * 4, 4), :]).then_inc(dn_in[u], 16)
                    sp.end_ifs()
            sp.wait_ge(*s_route.dve.at("eb"))
            sp.dma_start(bias_row[:, :], A["final_norm_g"].partition_broadcast(P)).then_inc(fin_in, 16)
            for t in range(NT):
                sp.wait_ge(*s_fin.dve.at(f"out{t}"))
                dst = O["y_prompt"][0] if t == 0 else O["y_sample"][0, P * (t - 1):P * t, :]
                sp.dma_start(dst, x[:, t, :]).then_inc(out_done, 16)
            sp.wait_ge(out_done, 16 * NT)

        @block.tensor
        def _(pe):
            S = s_ada.pe
            pe.sem_inc(*S.open())
            pe.wait_ge(*s_norm.dve.at("silc"))
            with pe.Fori(0, A_USES) as j:
                S.begin(j)
                for u in range(2):
                    pe.wait_ge(ring_in[u], j * 16 + 16)
                    pe.wait_ge(*s_ada.dve.at(f"row{u}", j, 1))
                    for k in range(KD):
                        m = nc.tensor.matmul(ps[u][0:2, :], silc[:, k, :], ring[:, u, k, :], start=k == 0, stop=k == KD - 1)
                    m.then_inc(ring_used[u], 1)
                pe.wait_ge(tab_in, 16)
                for u in range(2):
                    pe.wait_ge(*s_ada.dve.at(f"row{u}", j))
                    pe.wait_ge(*s_ada.act.at(f"bc{u}1", j, 1))
                    for c in range(2):
                        nc.tensor.matmul(ps[2 + 2 * u + c][:, :], tab[0:2, T_SEL + P * c:T_SEL + P * (c + 1)],
                                         modrow[:, bass.ds(j * 2 * COLS + COLS * u, COLS)], start=True, stop=True
                                         ).then_inc(*S.tick(f"bc{u}{c}"))
            S = s_norm.pe
            pe.wait_ge(*s_ada.act.at("bc11", A_USES - 1))
            for t in range(NT):
                pe.wait_ge(*s_norm.dve.at(f"h{t}"))
                for b in range(2):
                    if t:
                        pe.wait_ge(*s_norm.act.at(f"hT{t - 1}{b}"))
                    for k in range(4):
                        m = nc.tensor.transpose(ps[b][:, P * k:P * (k + 1)], (hrow if t % 2 == 0 else hrow2)[:, P * (4 * b + k):P * (4 * b + k + 1)], ident)
                    m.then_inc(*S.tick(f"hT{t}{b}"))
            S = s_fm.pe
            pe.sem_inc(*S.open())
            pe.wait_ge(*s_norm.act.at(f"hT{NT - 1}1"))

            def fm_tile(job, u, ct):
                for g in range(2):
                    for k in range(KD):
                        m = nc.tensor.matmul(ps[2 * (job % 2) + g][:, 0:HALF], ring[:, u, k, P * ct:P * (ct + 1)],
                                             hT[:, k, HALF * g:HALF * (g + 1)], start=k == 0, stop=k == KD - 1)
                return m

            with pe.Fori(0, 2) as j:
                S.begin(j)
                for job in range(8):
                    u, ct = divmod(job, 4)
                    if ct == 0:
                        pe.wait_ge(ring_in[u], j * 16 + 16 * (A_USES + 1))
                    pe.wait_ge(*s_fm.act.at(f"a{(job - 2) % 8}", j, 1 if job < 2 else 0))
                    pe.wait_ge(*s_fm.dve.at(f"d{(job - 2) % 8}", j, 1 if job < 2 else 0))
                    m = fm_tile(job, u, ct)
                    m.then_inc(*S.tick(f"p{job}"))
                    if ct == 3:
                        pe.wait_ge(*S.so_far())
                        pe.sem_inc(ring_used[u], 1)
            S = s_tm.pe
            for job in range(6):
                u, ct = divmod(job, 4)
                if ct == 0:
                    pe.wait_ge(ring_in[u], 16 * (A_USES + 3))
                if job < 2:
                    pe.wait_ge(*s_fm.act.at(f"a{6 + job}", 1))
                    pe.wait_ge(*s_fm.dve.at(f"d{6 + job}", 1))
                else:
                    pe.wait_ge(*s_tm.act.at(f"c{job - 2}"))
                fm_tile(job, u, ct).then_inc(*S.tick(f"p{job}"))
                if job in (3, 5):
                    pe.wait_ge(*S.so_far())
                    pe.sem_inc(ring_used[u], 1)
            pe.sem_inc(*s_l2.pe.open())

            def l2_pe(it):
                s_l2.pe.begin(it)
                pe.wait_ge(*s_l2.act.at("sq", it))
                pe.wait_ge(*s_l2.act.at("ln", it, 1))
                for g in range(2):
                    m = nc.tensor.matmul(ps[g][:, 0:HALF], ones, scr[:, 0, HALF * g:HALF * (g + 1)], start=True, stop=True)
                m.then_inc(*s_l2.pe.tick("ss"))

            for n, nc_ in enumerate((16, 512, 512)):
                u = n % 2
                pe.wait_ge(ring_in[u], 16 * (A_USES + 4 + n // 2))
                for t in range(NT):
                    q = n * NT + t
                    if q >= 4:
                        pe.wait_ge(*s_tm.act.at(f"t{q - 4}"))
                    for k in range(KD):
                        m = nc.tensor.matmul(ps[4 + q % 4][:, 0:nc_], hT[:, k, P * t:P * (t + 1)], ring[:, u, k, 0:nc_],
                                             start=k == 0, stop=k == KD - 1)
                    m.then_inc(*S.tick(f"t{q}"))
                    if 0 <= q - 6 < 8:
                        l2_pe(q - 6)
                pe.wait_ge(*S.so_far())
                pe.sem_inc(ring_used[u], 1)
            S = s_prep.pe
            pe.wait_ge(*s_prep.dve.at("g"))
            pe.wait_ge(*s_tm.act.at(f"t{3 * NT - 1}"))
            for d in range(2):
                m = nc.tensor.matmul(ps[7][:, 32 * d:32 * d + 20], incl(d), gtmp[:, 2, :, 4 * d:4 * d + 4], start=True, stop=True)
            m.then_inc(*S.tick("G"))
            pe.wait_ge(*s_prep.act.at("negeg"))
            pe.wait_ge(*s_l2.act.at("ln", 7))
            S = s_gdn.pe
            pe.sem_inc(*S.open())

            def gdn_pe(it, hp, tiles):
                S.begin(it)
                pe.wait_ge(*s_gp.pool.at("copies", it))
                pe.wait_ge(*s_gdn.dve.at("state", it, 1))
                for s_ in range(4):
                    m = nc.tensor.matmul(ps[0][:, P * s_:P * (s_ + 1)], g_gb[:, s_, :], incl(s_ // 2), start=True, stop=True)
                m.then_inc(*S.tick("grow"))
                for s_ in range(4):
                    m = nc.tensor.matmul(ps[1 + s_ // 2][:, 256 * (s_ % 2):256 * (s_ % 2 + 1)], g_kq[:, s_, 0:P], g_kq[:, s_, :], start=True, stop=True)
                m.then_inc(*S.tick("scores"))
                for s_ in range(4):
                    m = nc.tensor.transpose(ps[3][:, P * s_:P * (s_ + 1)], g_kq[:, s_, 0:P], ident)
                m.then_inc(*S.tick("ktm"))
                for s_ in range(4):
                    m = nc.tensor.transpose(ps[4][:, P * s_:P * (s_ + 1)], g_vf[:, s_, :], ident)
                m.then_inc(*S.tick("vtm"))
                keep_clock(5, 10)
                pe.wait_ge(*s_gdn.dve.at("qk", it))
                pe.wait_ge(*s_gdn.act.at("vtm", it))
                pe.wait_ge(*s_gdn.act.at("eg", it))
                inverse_pe(pe, S, s_gdn, it, lambda s_: g_lt[:, s_, :])
                for d in range(2):
                    pe.wait_ge(*s_gdn.dve.at(f"xt{LEVELS - 1}{d}", it))
                    for hh in range(2):
                        m = nc.tensor.matmul(ps[6 + d][:, 256 * hh:256 * (hh + 1)], i_xt[:, 2 * d + hh, :], g_rhs[:, 2 * d + hh, :], start=True, stop=True)
                    m.then_inc(*S.tick(f"w{d}"))
                for d in range(2):
                    pe.wait_ge(*s_gdn.act.at(f"w{d}", it))
                    for hh in range(2):
                        m = nc.tensor.matmul(ps[d][:, 256 * hh:256 * (hh + 1)], g_w[:, 2 * d + hh, 0:P], g_qk[:, 2 * d + hh, :], start=True, stop=True)
                    m.then_inc(*S.tick(f"c{d}"))
                pe.wait_ge(*s_gdn.dve.at("t1", it))
                for s_ in range(4):
                    st = g_state[:, s_ // 2, bass.ds(hp * 256 + P * (s_ % 2), P)]
                    nc.tensor.matmul(ps[2][:, P * s_:P * (s_ + 1)], g_qk[:, s_, 0:P], g_w[:, s_, P:2 * P], start=True, stop=False)
                    m = nc.tensor.matmul(ps[2][:, P * s_:P * (s_ + 1)], g_q1[:, s_, :], st, start=False, stop=True)
                m.then_inc(*S.tick("y"))
                for s_ in range(4):
                    st = g_state[:, s_ // 2, bass.ds(hp * 256 + P * (s_ % 2), P)]
                    nc.tensor.matmul(ps[3][:, P * s_:P * (s_ + 1)], g_qk[:, s_, P:2 * P], g_w[:, s_, P:2 * P], start=True, stop=False)
                    m = nc.tensor.matmul(ps[3][:, P * s_:P * (s_ + 1)], g_t1[:, s_, :], st, start=False, stop=True)
                m.then_inc(*S.tick("t2"))
                keep_clock(6, 4)

            pe.wait_ge(zeroed, 3)
            with pe.Fori(0, 2) as hp:
                gdn_pe(hp, hp, (0, 0))
            pe.wait_ge(state_in, 32)
            with pe.Fori(1, NT) as n:
                with pe.Fori(0, 2) as hp:
                    gdn_pe(n * 2 + hp, hp, (n, NT - n))
            for j in range(FT):
                pe.wait_ge(*s_kk.act.at(f"sq{j}"))
                if j >= 2:
                    pe.wait_ge(*s_kk.act.at(f"ln{j - 2}"))
                for g in range(2):
                    m = nc.tensor.matmul(ps[2 * (j % 2) + g][:, 0:HALF], blk64, scr[:, j % 2, HALF * g:HALF * (g + 1)], start=True, stop=True)
                m.then_inc(*s_kk.pe.tick(f"ss{j}"))
            S = s_rwkv.pe
            pe.sem_inc(*S.open())
            pe.wait_ge(*s_kk.act.at(f"ln{FT - 1}"))
            pe.wait_ge(rzero, 2)

            pe.sem_inc(*s_rp.pe.open())

            def prep_pe(it):
                s_rp.pe.begin(it)
                pe.wait_ge(*s_rp.pool.at("copies", it))
                for d in range(2):
                    nc.tensor.matmul(ps[6][:, P * d:P * (d + 1)], r_lora[0:64, d, :], r_lw[0:64, d, :], start=True, stop=True)
                    m = nc.tensor.matmul(ps[7][:, P * d:P * (d + 1)], r_lora[64:128, d, :], r_lw[64:128, d, :], start=True, stop=True)
                m.then_inc(*s_rp.pe.tick("u"))

            prep_pe(0)
            pe.wait_ge(*s_rp.act.at("eu", 0))

            def rwkv_pe(it, ft, tiles):
                S.begin(it)
                pe.wait_ge(*s_rwkv.dve.at("last", it, 1))
                pe.wait_ge(*s_rp.pool.at("rr", it))
                for d in range(2):
                    m = nc.tensor.matmul(ps[1][:, 256 + 2 * d:258 + 2 * d], r_rr[:, d, :], tab[:, T_HEAD:T_HEAD + 2], start=True, stop=True)
                pe.wait_ge(*s_rp.dve.at("bk", it))
                for d in range(2):
                    for half in range(2):
                        for hh in range(2):
                            rows = slice(RD * hh, RD * (hh + 1))
                            m = nc.tensor.matmul(ps[2 + 2 * d + hh][:, 256 * half:256 * (half + 1)], r_bk[rows, 2 * half + d, :], r_ar[rows, d, :], start=True, stop=True)
                    m.then_inc(*S.tick(f"scores{d}"))
                for n in range(4):
                    m = nc.tensor.transpose(ps[6][:, P * n:P * (n + 1)], r_bk[:, n, :], ident)
                m.then_inc(*S.tick("bktm"))
                for d in range(2):
                    m = nc.tensor.transpose(ps[7][:, P * d:P * (d + 1)], r_ar[:, d, 0:P], ident)
                m.then_inc(*S.tick("atm"))
                keep_clock(0, 5)
                pe.wait_ge(*s_rwkv.act.at("tm", it))

                def values():
                    pe.wait_ge(*s_rwkv.pool.at("v", it))
                    for s_ in range(4):
                        v = r_v[:, s_ // 2, RD * (s_ % 2):RD * (s_ % 2 + 1)]
                        m = nc.tensor.matmul(ps[7][:, 256 + RD * s_:256 + RD * (s_ + 1)], r_sc[:, s_, 320:448], v, start=True, stop=True)
                    m.then_inc(*S.tick("akv"))
                    prep_pe(it + 1)

                inverse_pe(pe, S, s_rwkv, it, lambda s_: r_sc[:, s_, 0:P], {0: lambda: pe.wait_ge(*s_rwkv.dve.at("bonus", it)), 1: values})
                pe.wait_ge(*s_rwkv.act.at("akv", it))
                for d in range(2):
                    pe.wait_ge(*s_rwkv.dve.at(f"xt{LEVELS - 1}{d}", it))
                    for hh in range(2):
                        s_ = 2 * d + hh
                        m = nc.tensor.matmul(ps[6 + d][:, P * hh:P * (hh + 1)], i_xt[:, s_, :], r_rhs[:, s_, :], start=True, stop=True)
                    m.then_inc(*S.tick(f"w{d}"))
                for d in range(2):
                    pe.wait_ge(*s_rwkv.act.at(f"w{d}", it))
                    for hh in range(2):
                        m = nc.tensor.matmul(ps[d][RD * hh:RD * (hh + 1), 0:192], r_w[:, 2 * d + hh, 0:RD], r_sc[:, 2 * d + hh, P:P + 192], start=True, stop=True)
                    m.then_inc(*S.tick(f"c{d}"))
                keep_clock(6, 4)
                pe.wait_ge(*s_rwkv.dve.at("t1", it))
                for d in range(2):
                    for hh in range(2):
                        s_ = 2 * d + hh
                        v = r_v[:, d, RD * hh:RD * (hh + 1)]
                        rows = slice(RD * hh, RD * (hh + 1))
                        yo = ps[(2, 5)[hh]][:, RD * d:RD * (d + 1)]
                        nc.tensor.matmul(yo, r_sc[:, s_, P:2 * P], r_w[:, s_, RD:P], start=True, stop=False)
                        nc.tensor.matmul(yo, r_sc[:, s_, 448:576], v, start=False, stop=False)
                        m = nc.tensor.matmul(yo, r_q1[rows, d, :], r_zin[rows, d, :], start=False, stop=True)
                m.then_inc(*S.tick("y"))
                for d in range(2):
                    for hh in range(2):
                        s_ = 2 * d + hh
                        v = r_v[:, d, RD * hh:RD * (hh + 1)]
                        rows = slice(RD * hh, RD * (hh + 1))
                        zo = ps[3 + hh][rows, RD * d:RD * (d + 1)]
                        nc.tensor.matmul(zo, r_sc[:, s_, 256:320], r_w[:, s_, RD:P], start=True, stop=False)
                        nc.tensor.matmul(zo, r_ktm[:, s_, :], v, start=False, stop=False)
                        m = nc.tensor.matmul(zo, r_t1[rows, d, :], r_zin[rows, d, :], start=False, stop=True)
                m.then_inc(*S.tick("t2"))
                keep_clock(0, 8)

            with pe.Fori(0, FT) as ft:
                rwkv_pe(ft, ft, (0, 0))
            Z = s_zs.pe
            pe.wait_ge(*s_rwkv.dve.at("last", FT - 1))
            for n in range(8):
                m = nc.tensor.transpose(ps[n // 4][0:RD, P * (n % 4):P * (n % 4 + 1)], zst[:, RD * n:RD * (n + 1)], ident)
            m.then_inc(*Z.tick("out"))
            pe.wait_ge(rstate_in, 16)
            pe.wait_ge(*s_zs.act.at("znat"))
            for n in range(8):
                m = nc.tensor.transpose(ps[0][:, RD * n:RD * (n + 1)], znat[0:RD, P * n:P * (n + 1)], ident[0:RD, 0:RD])
            m.then_inc(*Z.tick("in"))
            pe.wait_ge(*s_zs.act.at("zst"))
            with pe.Fori(1, NT) as n:
                with pe.Fori(0, FT) as ft:
                    rwkv_pe(n * FT + ft, ft, (n, NT - n))
            S = s_tail.pe
            pe.sem_inc(*S.open())
            pe.wait_ge(cst_in, 16 * 9)

            pe.sem_inc(*s_mix.pe.open())

            def mix_pe(it):
                s_mix.pe.begin(it)
                pe.wait_ge(*s_mix.dve.at("sgl", it))
                nc.tensor.matmul(ps[0][:, :], t_sgl, g2w, start=True, stop=True).then_inc(*s_mix.pe.tick("gate"))

            def tail_pe(it, more):
                S.begin(it)
                pe.wait_ge(*s_mix.dve.at("o", it))
                for b in range(2):
                    for k in range(4):
                        m = nc.tensor.transpose(ps[1 + b][:, P * k:P * (k + 1)], o_tm[:, P * (4 * b + k):P * (4 * b + k + 1)], ident)
                    m.then_inc(*S.tick(f"oT{b}"))
                if more:
                    mix_pe(it + 1)
                pe.wait_ge(*s_tail.dve.at("x2", it, 1))
                pe.wait_ge(*s_tail.act.at("oT1", it))
                for b in range(2):
                    for k in range(KD):
                        m = nc.tensor.matmul(ps[3 + b][:, :], oT[:, k, :], wout[:, k, 512 * b:512 * (b + 1)], start=k == 0, stop=k == KD - 1)
                    m.then_inc(*S.tick(f"mix{b}"))
                pe.wait_ge(*s_tail.dve.at("h2", it))
                for b in range(2):
                    for k in range(4):
                        m = nc.tensor.transpose(ps[5 + b][:, P * k:P * (k + 1)], h2[:, P * (4 * b + k):P * (4 * b + k + 1)], ident)
                    m.then_inc(*S.tick(f"h2T{b}"))
                pe.wait_ge(*s_tail.act.at("h2T1", it))
                for k in range(KD):
                    m = nc.tensor.matmul(ps[7][:, 0:GROUPS + NE], h2T[:, k, :], rw_[:, k, :], start=k == 0, stop=k == KD - 1)
                m.then_inc(*S.tick("logits"))

            mix_pe(0)
            pe.wait_ge(wout_in, 16)
            tail_pe(0, True)
            with pe.Fori(1, NT - 1) as t:
                tail_pe(t, True)
            tail_pe(NT - 1, False)
            S = s_route.pe
            pe.wait_ge(*s_tail.dve.at("last", NT - 1))
            for t in range(NT):
                for q in range(t + 1):
                    m = nc.tensor.matmul(ps[0][:, NE * t:NE * (t + 1)], tab[:, T_MASK:T_MASK + P] if q == t else ones, ohs[:, q, :], start=q == 0, stop=q == t)
            for q in range(NT):
                m = nc.tensor.matmul(ps[0][:, NE * NT:NE * (NT + 1)], ones, ohs[:, q, :], start=q == 0, stop=q == NT - 1)
            m.then_inc(*S.tick("rank"))
            pe.wait_ge(*s_route.dve.at("eb"))
            n_blocks = pe.value_load(eb_i[0:1, NB:NB + 1], min_val=0, max_val=NB)
            S = s_moe.pe
            pe.sem_inc(*S.open())
            with pe.Fori(0, NB // 2) as j:
                S.begin(j)
                for u in range(2):
                    with pe.If(j * 2 + u < n_blocks):
                        wg, wu, wd = e_w[u]
                        pe.wait_ge(rows_in[u], j * 16 + 16)
                        pe.wait_ge(*s_moe.dve.at(f"xT{u}", j, 1))
                        pe.sem_inc(waited, 1)
                        for k in range(KD):
                            m = nc.tensor.transpose(ps[u][:, BT * k:BT * (k + 1)], e_x[u][:, P * k:P * (k + 1)], ident[0:BT, 0:BT])
                        m.then_inc(*S.tick(f"xT{u}"))
                        pe.wait_ge(*s_moe.dve.at(f"xT{u}", j))
                        pe.wait_ge(gu_in[u], j * 32 + 32)
                        pe.wait_ge(*s_moe.dve.at(f"h{1 - u}", j, 1 - u))
                        for w_, bank in ((wg, 2), (wu, 3)):
                            for k in range(KD):
                                for h in range(2):
                                    m = nc.tensor.matmul(ps[bank][BT * h:BT * (h + 1), 0:256], e_xT[u][:, k, :], w_[:, k, 256 * h:256 * (h + 1)], start=k == 0, stop=k == KD - 1)
                            m.then_inc(*S.tick(f"{'gate' if bank == 2 else 'up'}{u}"))
                        pe.wait_ge(*s_moe.dve.at(f"h{u}", j))
                        for c in range(2):
                            m = nc.tensor.transpose(ps[4][:, P * c:P * (c + 1)], e_h[u][:, P * c:P * (c + 1)], ident)
                        m.then_inc(*S.tick(f"hT{u}"))
                        pe.wait_ge(*s_moe.dve.at(f"hT{u}", j))
                        pe.wait_ge(dn_in[u], j * 16 + 16)
                        pe.wait_ge(*s_moe.dve.at(f"y{1 - u}", j, 1 - u))
                        for n in range(4):
                            for h in range(2):
                                m = nc.tensor.matmul(ps[5][BT * h:BT * (h + 1), :], e_hT[u][:, n % 2, n // 2, :], wd[:, n, 512 * h:512 * (h + 1)], start=n == 0, stop=n == 3)
                        m.then_inc(*S.tick(f"down{u}"))
                    pe.end_ifs()

        @block.gpsimd
        def _(pool):
            nc.gpsimd.memset(zeros, 0.0).then_inc(zeros_ready, 1)
            nc.gpsimd.memset(bonus[:, :, :], 0.0).then_inc(zeroed, 1)
            nc.gpsimd.memset(l2_eps, 1e-6).then_inc(eps_ready, 1)
            pool.wait_ge(*s_tm.pe.at(f"t{3 * NT - 1}"))
            nc.gpsimd.memset(hTf[:, 0:1024], 0.0).then_inc(zeroed, 1)
            nc.gpsimd.memset(hTf[:, 2560:5120], 0.0).then_inc(zeroed, 1)
            S = s_gdn.pool
            pool.sem_inc(*S.open())
            pool.wait_ge(*s_l2.dve.at("out", 7))

            Q = s_gp.pool
            pool.sem_inc(*Q.open())
            fmf, gtf = flat(fm[:, :, :]), gtmp[:, :, :, :].rearrange("p a b c -> p (a b c)")

            def prep_copies(it, hp, tiles):
                Q.begin(it)
                pool.wait_ge(*Q.so_far())
                pool.wait_ge(*s_gdn.pe.at("vtm", it, 1))
                pool.wait_ge(*s_gdn.pool.at("qd", it, 1))
                pool.sem_inc(waited, 1)
                for d in range(2):
                    col = tiles[d] * P
                    for base, dst in ((FM_K2, g_kq[:, 2 * d:2 * d + 2, 0:P]), (FM_Q2, g_kq[:, 2 * d:2 * d + 2, P:2 * P]), (FM_V2, pair(g_vf, d))):
                        for hh in range(2):
                            nc.gpsimd.tensor_copy(dst[:, hh], fmf[:, bass.ds((base + hh) * TOK + hp * (2 * TOK) + col, P)]).then_inc(*Q.tick())
                    for hh in range(2):
                        nc.gpsimd.tensor_copy(g_gb[:, 2 * d + hh, :], gtf[:, bass.ds((2 * NT) * 8 + tiles[d] * 8 + hp * 2 + 4 * d + hh, 1)].to_broadcast([P, P])).then_inc(*Q.tick("copies"))

            def gdn_pool(it, hp, tiles):
                S.begin(it)
                nhp, ntiles = next_of(pool, it, tiles, 2)
                pool.wait_ge(*S.so_far())
                pool.wait_ge(*s_gp.pool.at("copies", it))
                pool.wait_ge(*s_gdn.act.at("eg", it))
                pool.wait_ge(*s_gdn.dve.at("t1", it, 1))
                pool.sem_inc(waited, 1)
                for d in range(2):
                    last = P - 1 if d == 0 else 0
                    nc.gpsimd.tensor_copy(g_egl[:, 2 * d:2 * d + 2], pair(g_eg, d)[:, :, last]).then_inc(*S.tick())
                pool.wait_ge(*S.so_far())
                nc.gpsimd.tensor_tensor(g_eg, g_eg, g_kq[:, :, P:2 * P], ALU.mult).then_inc(*S.tick("qd"))
                prep_copies(it + 1, nhp, ntiles)

            prep_copies(0, 0, (0, 0))
            with pool.Fori(0, 2) as hp:
                gdn_pool(hp, hp, (0, 0))
            with pool.Fori(1, NT) as n:
                with pool.Fori(0, 2) as hp:
                    gdn_pool(n * 2 + hp, hp, (n, NT - n))
            pool.wait_ge(*s_gdn.dve.at("state", 2 * NT - 1))
            pool.wait_ge(*s_gdn.pe.at("t2", 2 * NT - 1))
            pool.wait_ge(*s_gp.pool.at("copies", 2 * NT))
            nc.gpsimd.memset(y_r, 0.0).then_inc(rzero, 1)
            nc.gpsimd.memset(zst, 0.0).then_inc(rzero, 1)
            S = s_rwkv.pool
            pool.sem_inc(*S.open())
            pool.wait_ge(lora_in, 64)
            pool.wait_ge(*s_kk.dve.at("out"))

            Q = s_rp.pool
            pool.sem_inc(*Q.open())

            def prep_pool_copies(it, ft, tiles):
                Q.begin(it)
                pool.wait_ge(*s_rp.act.at("eu", it, 1))
                pool.wait_ge(*s_rp.pool.at("rr", it, 1))
                pool.wait_ge(*s_rp.pe.at("u", it, 1))
                pool.sem_inc(waited, 1)
                nc.gpsimd.tensor_copy(r_par, rpar[:, :, :].rearrange("p f n -> p (f n)")[:, bass.ds(ft * 8, 8)]).then_inc(*Q.tick())
                for d in range(2):
                    nc.gpsimd.tensor_copy(r_lora[:, d, :], lora[:, bass.ds(ft * P + RW * d, P)]).then_inc(*Q.tick())
                    nc.gpsimd.tensor_copy(r_lw[:, d, :], fmf[:, bass.ds(tiles[d] * P + FM_LORA * TOK, P)]).then_inc(*Q.tick("copies"))

            def prep_pool(it, ft, tiles):
                pool.wait_ge(*s_rp.dve.at("gates", it))
                pool.wait_ge(*s_rp.dve.at("bk", it, 1))
                pool.wait_ge(*s_rwkv.pe.at("atm", it, 1))
                pool.wait_ge(*Q.so_far())
                pool.sem_inc(waited, 1)
                nc.gpsimd.tensor_scalar(r_kd, r_eu[:, 2:4, :], r_par[:, 5:6], r_par[:, 6:7], ALU.mult, ALU.add).then_inc(*Q.tick())
                for d in range(2):
                    nc.gpsimd.tensor_tensor(r_kka[:, d, :], r_eu[:, 2 + d, :], fmf[:, bass.ds(ft * TOK + tiles[d] * P + FM_Q2 * TOK, P)], ALU.mult).then_inc(*Q.tick("kka"))
                pool.wait_ge(*Q.so_far())
                for d in range(2):
                    nc.gpsimd.tensor_tensor(r_kd[:, d, :], r_kd[:, d, :], fmf[:, bass.ds(ft * TOK + tiles[d] * P + FM_K * TOK, P)], ALU.mult).then_inc(*Q.tick("kd"))
                pool.wait_ge(*Q.so_far())
                pool.sem_inc(waited, 1)
                nc.gpsimd.tensor_scalar(r_rr, r_kd, r_par[:, 7:8], 1.0, ALU.mult, ALU.mult).then_inc(*Q.tick())
                pool.wait_ge(*Q.so_far())
                for d in range(2):
                    nc.gpsimd.tensor_tensor(r_rr[:, d, :], r_rr[:, d, :], fmf[:, bass.ds(ft * TOK + tiles[d] * P + FM_R * TOK, P)], ALU.mult).then_inc(*Q.tick("rr"))

            def rwkv_pool(it, ft, tiles):
                S.begin(it)
                nft, ntiles = next_of(pool, it, tiles)
                prep_pool_copies(it + 1, nft, ntiles)
                pool.wait_ge(*s_rwkv.pe.at("t2", it, 1))
                pool.wait_ge(*S.so_far())
                pool.sem_inc(waited, 1)
                for d in range(2):
                    nc.gpsimd.tensor_copy(r_v[:, d, :], v_tm[:, :, :].rearrange("p t n -> p (t n)")[:, bass.ds(tiles[d] * RW + ft * P, P)]).then_inc(*S.tick("v"))
                pool.wait_ge(*s_rwkv.dve.at("last", it, 1))
                pool.wait_ge(*s_rp.dve.at("bk", it))
                pool.sem_inc(waited, 1)
                nc.gpsimd.tensor_copy(r_keep, r_ar[:, :, P:2 * P]).then_inc(*S.tick("keep"))
                prep_pool(it + 1, nft, ntiles)

            prep_pool_copies(0, 0, (0, 0))
            prep_pool(0, 0, (0, 0))
            with pool.Fori(0, FT) as ft:
                rwkv_pool(ft, ft, (0, 0))
            with pool.Fori(1, NT) as n:
                with pool.Fori(0, FT) as ft:
                    rwkv_pool(n * FT + ft, ft, (n, NT - n))
            S = s_route.pool
            pool.wait_ge(*s_conv.act.at("out1", 5))
            nc.gpsimd.memset(zi, 0).then_inc(*S.tick("zi"))
            nc.gpsimd.iota(tid, pattern=[[P, NT]], base=0, channel_multiplier=1).then_inc(*S.tick("tid"))
            pool.wait_ge(tz_out, 32)
            pool.wait_ge(*S.so_far())
            pool.wait_ge(*s_route.dve.at("slots"))
            for t in range(NT):
                for k in range(2):
                    nc.gpsimd.indirect_dma_start(out=tokd, out_offset=bass.IndirectOffsetOnAxis(ap=slot_i[:, t, k:k + 1], axis=0),
                                                 in_=tid[:, t:t + 1], in_offset=None).then_inc(tok_out, 16)
            pool.wait_ge(tok_in, 16)
            pool.wait_ge(h2_out, 16 * NT)
            pool.wait_ge(*s_route.dve.at("eb"))
            n_blocks = pool.value_load(eb_i[0:1, NB:NB + 1], min_val=0, max_val=NB)
            S = s_moe.pool
            pool.sem_inc(*S.open())
            with pool.Fori(0, NB // 2) as j:
                S.begin(j)
                for u in range(2):
                    with pool.If(j * 2 + u < n_blocks):
                        pool.wait_ge(*s_moe.pe.at(f"xT{u}", j, 1))
                        pool.sem_inc(waited, 1)
                        nc.gpsimd.tensor_copy(idx_u[:, u:u + 1], tok_i[:, bass.ds(j * 2 + u, 1)]).then_inc(*S.tick(f"idx{u}"))
                        pool.wait_ge(*S.so_far())
                        pool.sem_inc(waited, 1)
                        nc.gpsimd.indirect_dma_start(out=e_x[u], out_offset=None, in_=h2d,
                                                     in_offset=bass.IndirectOffsetOnAxis(ap=idx_u[:, u:u + 1], axis=0)).then_inc(rows_in[u], 16)
                    pool.end_ifs()
            pool.wait_ge(yd_zeroed, 16)
            for u in range(2):
                n_u = pool.snap((n_blocks + (1 - u)) // 2)
                pool.wait_ge(y_out[u], n_u * 32 + 32)
                pool.sem_inc(waited, 1)
            for t in range(NT):
                for k in range(2):
                    if t >= 1:
                        pool.wait_ge(*s_fin.dve.at(f"sum{t - 1}"))
                    nc.gpsimd.indirect_dma_start(out=comb(k), out_offset=None, in_=yd,
                                                 in_offset=bass.IndirectOffsetOnAxis(ap=slot_i[:, t, k:k + 1], axis=0)).then_inc(comb_in[k], 16)

        @block.scalar
        def _(act):
            S = s_norm.act
            act.wait_ge(c_in, 32)
            nc.scalar.activation(cexp, craw, ACT.Exp, scale=-1.0).then_inc(*S.tick("cexp"))
            S = s_ada.act
            act.sem_inc(*S.open())
            for j0, j1, home in ((0, 2, moda), (2, A_USES, modk)):
                with act.Fori(j0, j1) as j:
                    S.begin(j)
                    for u in range(2):
                        for c in range(2):
                            act.wait_ge(*s_ada.pe.at(f"bc{u}{c}", j))
                            dst = home[:, c].rearrange("p s n -> p (s n)")[:, bass.ds((j - j0) * 2 * COLS + COLS * u, COLS)]
                            nc.scalar.copy(dst, ps[2 + 2 * u + c][:, :]).then_inc(*S.tick(f"bc{u}{c}"))
                if j0 == 0:
                    act.wait_ge(x_in, 32)
                    for t in range(NT):
                        nc.scalar.activation(flat(hT[:, :, :])[:, D * t:D * (t + 1)], x[:, t, :], ACT.Square, accum_out=ssq[:, t:t + 1]).then_inc(*s_norm.act.tick(f"ssq{t}"))
            S = s_norm.act
            act.wait_ge(*s_norm.dve.at("var"))
            nc.scalar.activation(std, std, ACT.Sqrt).then_inc(*S.tick("std"))
            for t in range(NT):
                for b in range(2):
                    act.wait_ge(*s_norm.pe.at(f"hT{t}{b}"))
                    nc.scalar.copy(hT[:, 4 * b:4 * b + 4, P * t:P * (t + 1)], ps[b][:, :].rearrange("p (k n) -> p k n", k=4)
                                   ).then_inc(*S.tick(f"hT{t}{b}"))
            S = s_fm.act
            act.sem_inc(*S.open())
            with act.Fori(0, 2) as j:
                S.begin(j)
                for job in range(8):
                    act.wait_ge(*s_fm.pe.at(f"p{job}", j))
                    nc.scalar.copy(flat(fm[:, :, :])[:, bass.ds(j * 8 * TOK + job * TOK, HALF)], ps[2 * (job % 2)][:, 0:HALF]).then_inc(*S.tick(f"a{job}"))
            def prep_act():
                S = s_prep.act
                act.wait_ge(*s_tm.act.at(f"t{NT - 1}"))
                nc.scalar.activation(gtmp[:, 0], ba[:, :, 0:8], ACT.Exp, scale=-1.0).then_inc(*S.tick("ebeta"))
                act.wait_ge(*s_prep.dve.at("xa"))
                nc.scalar.activation(gtmp[:, 1], gtmp[:, 2], ACT.Abs).then_inc(*S.tick())
                act.wait_ge(*S.so_far())
                nc.scalar.activation(gtmp[:, 1], gtmp[:, 1], ACT.Exp, scale=-1.0).then_inc(*S.tick())
                act.wait_ge(*S.so_far())
                nc.scalar.activation(gtmp[:, 1], gtmp[:, 1], ACT.Ln, bias=1.0).then_inc(*S.tick("ln"))
                act.wait_ge(par_in, 16 * 12)
                nc.scalar.activation(par[:, 48:56], par[:, 48:56], ACT.Exp).then_inc(*S.tick("alog"))
                nc.scalar.activation(fm[0:64, FM_LORA, :], fm[0:64, FM_LORA, :], ACT.Tanh).then_inc(*S.tick("tanh"))

            S = s_conv.act
            act.sem_inc(*S.open())
            for j in range(6):
                S.begin(j)
                for u in range(2):
                    act.wait_ge(*s_conv.dve.at(f"cv{u}", j))
                    nc.scalar.activation(fm[:, FM_Q2 + 2 * j + u, :], scr[:, u, :], ACT.Silu).then_inc(*S.tick(f"out{u}"))
                act.wait_ge(*s_tm.pe.at(f"p{j}"))
                for g in range(2):
                    nc.scalar.copy(fm[:, FM_V2 + j, HALF * g:HALF * (g + 1)], ps[2 * (j % 2) + g][:, 0:HALF]).then_inc(*s_tm.act.tick(f"c{j}"))

            def norm_square(S, T, it, src):
                S.begin(it)
                act.wait_ge(*S.so_far())
                act.wait_ge(*T.dve.at("out", it, 1))
                act.wait_ge(*T.pe.at("ss", it, 1))
                nc.scalar.activation(scr[:, 0, :], src, ACT.Square).then_inc(*S.tick("sq"))

            def norm_root(S, T, it):
                act.wait_ge(*T.pe.at("ss", it))
                for g in range(2):
                    nc.scalar.activation(scr[:, 1, HALF * g:HALF * (g + 1)], ps[g][:, 0:HALF], ACT.Ln, bias=l2_eps).then_inc(*S.tick("ln"))
                act.wait_ge(*S.so_far())
                nc.scalar.activation(scr[:, 1, :], scr[:, 1, :], ACT.Exp, scale=-0.5).then_inc(*S.tick("rs"))

            S = s_l2.act
            act.sem_inc(*S.open())
            act.wait_ge(eps_ready, 1)
            act.wait_ge(*s_conv.act.at("out1", 5))
            for q in range(3 * NT):
                n, t = divmod(q, NT)
                if 0 <= q - 6 < 8:
                    norm_square(S, s_l2, q - 6, fm[:, FM_Q2 + q - 6, :])
                act.wait_ge(*s_tm.pe.at(f"t{q}"))
                dst = (ba, v_tm, z_tm)[n][:, t, :]
                nc.scalar.copy(dst, ps[4 + q % 4][:, 0:dst.shape[-1]]).then_inc(*s_tm.act.tick(f"t{q}"))
                if 0 <= q - 6 < 8:
                    norm_root(S, s_l2, q - 6)
                if q == NT:
                    prep_act()
            S = s_prep.act
            act.wait_ge(*s_prep.pe.at("G"))
            Gp = ps[7][:, 0:64].rearrange("p (d n) -> p d n", d=2)[:, :, 0:20].rearrange("p d (t h) -> p d t h", t=NT)
            for d in range(2):
                nc.scalar.copy(gs[:, d, :, :, 0], Gp[:, d]).then_inc(*S.tick())
                nc.scalar.activation(gs[:, d, :, :, 1], Gp[:, d], ACT.Exp).then_inc(*S.tick("eg0" if d == 0 else "negeg"))
            act.wait_ge(*s_tm.act.so_far())
            nc.scalar.activation(fm[:, FM_LORA + 1, :], fm[:, FM_LORA + 1, :], ACT.Sigmoid).then_inc(*s_route.act.tick("sgl"))
            nc.scalar.activation(z_tm[:, :, :], z_tm[:, :, :], ACT.Silu).then_inc(*s_route.act.tick("silz"))
            S = s_gdn.act
            act.sem_inc(*S.open())

            def gdn_act(it, hp, tiles):
                S.begin(it)
                act.wait_ge(*S.so_far())
                act.wait_ge(*s_gdn.pool.at("qd", it, 1))
                act.wait_ge(*s_gdn.pe.at("t2", it, 1))
                act.wait_ge(*s_gdn.dve.at("dif", it))
                nc.scalar.activation(g_et, g_et, ACT.Exp).then_inc(*S.tick("et"))
                nc.scalar.activation(g_eg, ps[0][:, :].rearrange("p (s n) -> p s n", n=P), ACT.Exp).then_inc(*S.tick("eg"))
                act.wait_ge(*s_gdn.pe.at("ktm", it))
                for s_ in range(4):
                    nc.scalar.mul(g_rhs[:, s_, 0:P], ps[3][:, P * s_:P * (s_ + 1)], g_sc[:, s_, 1:2]).then_inc(*S.tick())
                act.wait_ge(*s_gdn.dve.at("etm", it))
                for s_ in range(4):
                    last = P - 1 if s_ < 2 else 0
                    nc.scalar.mul(g_qk[:, s_, P:2 * P], ps[3][:, P * s_:P * (s_ + 1)], g_et[:, s_, last:last + 1]).then_inc(*S.tick())
                act.wait_ge(*s_gdn.pe.at("vtm", it))
                nc.scalar.copy(g_rhs[:, :, P:2 * P], ps[4][:, :].rearrange("p (s n) -> p s n", n=P)).then_inc(*S.tick("vtm"))
                inverse_act(act, S, s_gdn, it)
                for d in range(2):
                    act.wait_ge(*s_gdn.pe.at(f"w{d}", it))
                    for hh in range(2):
                        s_ = 2 * d + hh
                        nc.scalar.mul(g_w[:, s_, :], ps[6 + d][:, 256 * hh:256 * (hh + 1)], g_sc[:, s_, 3:4]).then_inc(*S.tick(f"w{d}"))

            with act.Fori(0, 2) as hp:
                gdn_act(hp, hp, (0, 0))
            with act.Fori(1, NT) as n:
                with act.Fori(0, 2) as hp:
                    gdn_act(n * 2 + hp, hp, (n, NT - n))
            def kk_square(j):
                act.wait_ge(*s_kk.dve.at(f"raw{j}"))
                nc.scalar.activation(scr[:, j % 2, :], fm[:, FM_Q2 + j, :], ACT.Square).then_inc(*s_kk.act.tick(f"sq{j}"))

            kk_square(0)
            kk_square(1)
            for j in range(FT):
                act.wait_ge(*s_kk.pe.at(f"ss{j}"))
                for g in range(2):
                    nc.scalar.activation(kk_root[:, j, HALF * g:HALF * (g + 1)], ps[2 * (j % 2) + g][:, 0:HALF], ACT.Ln, bias=l2_eps).then_inc(*s_kk.act.tick(f"ln{j}"))
                if j + 2 < FT:
                    kk_square(j + 2)
            act.wait_ge(*s_kk.act.so_far())
            nc.scalar.activation(kk_root, kk_root, ACT.Exp, scale=-0.5).then_inc(*s_kk.act.tick("rs"))
            S = s_rwkv.act
            act.sem_inc(*S.open())

            Q = s_rp.act
            act.sem_inc(*Q.open())

            def prep_act_gates(it):
                Q.begin(it)
                act.wait_ge(*s_rp.dve.at("pq", it, 1))
                act.wait_ge(*s_rp.pool.at("kka", it, 1))
                act.wait_ge(*s_rp.pool.at("copies", it))
                act.wait_ge(*s_rp.pe.at("u", it))
                for kind in range(2):
                    for d in range(2):
                        n = 2 * kind + d
                        nc.scalar.activation(r_eu[:, n, :], ps[6 + kind][:, P * d:P * (d + 1)], ACT.Exp, scale=-1.0, bias=r_par[:, n:n + 1]).then_inc(*Q.tick("eu"))

            def prep_act_factors(it):
                act.wait_ge(*s_rp.dve.at("pq", it))
                act.wait_ge(*s_rp.dve.at("bk", it, 1))
                for n, (src, sign) in enumerate(((2, -1), (1, 1), (0, -1), (3, 1), (0, 1), (3, -1))):
                    nc.scalar.activation(r_ex[:, n, :], r_pq[:, src, :], ACT.Exp, scale=sign * DECAY).then_inc(*Q.tick(f"ex{n}"))
                act.wait_ge(*s_rwkv.dve.at("hc", it, 1))
                nc.scalar.activation(r_h, r_ht, ACT.Exp, scale=-DECAY).then_inc(*Q.tick("h"))

            def rwkv_act(it, ft, tiles):
                S.begin(it)
                act.wait_ge(*S.so_far())
                act.wait_ge(*s_rwkv.dve.at("last", it, 1))
                act.wait_ge(*s_rwkv.pe.at("bktm", it))
                act.wait_ge(*s_rwkv.pe.at("t2", it, 1))
                for d in range(2):
                    nc.scalar.copy(r_sc[:, 2 * d:2 * d + 2, 256:320], ps[6][:, P * d:P * (d + 1)].rearrange("p (s n) -> p s n", s=2)).then_inc(*S.tick())
                nc.scalar.copy(r_ktm, ps[6][:, 256:512].rearrange("p (s n) -> p s n", n=RD)).then_inc(*S.tick())
                act.wait_ge(*s_rwkv.pe.at("atm", it))
                nc.scalar.copy(r_rhs[:, :, 0:RD], ps[7][:, 0:256].rearrange("p (s n) -> p s n", n=RD)).then_inc(*S.tick("tm"))

                def values():
                    prep_act_gates(it + 1)
                    act.wait_ge(*s_rwkv.pe.at("akv", it))
                    nc.scalar.copy(r_rhs[:, :, RD:P], ps[7][:, 256:512].rearrange("p (s n) -> p s n", n=RD)).then_inc(*S.tick("akv"))
                inverse_act(act, S, s_rwkv, it, {2: values, 5: lambda: prep_act_factors(it + 1)})
                for d in range(2):
                    act.wait_ge(*s_rwkv.pe.at(f"w{d}", it))
                    nc.scalar.copy(pair(r_w, d), ps[6 + d][:, 0:256].rearrange("p (s n) -> p s n", s=2)).then_inc(*S.tick(f"w{d}"))

            act.wait_ge(par_in, 16 * 12)
            prep_act_gates(0)
            prep_act_factors(0)
            with act.Fori(0, FT) as ft:
                rwkv_act(ft, ft, (0, 0))
            Z = s_zs.act
            act.wait_ge(*s_zs.pe.at("out"))
            for b in range(2):
                nc.scalar.copy(znat[0:RD, 512 * b:512 * (b + 1)], ps[b][0:RD, :]).then_inc(*Z.tick("znat"))
            act.wait_ge(*s_zs.pe.at("in"))
            nc.scalar.copy(zst, ps[0][:, :]).then_inc(*Z.tick("zst"))
            with act.Fori(1, NT) as n:
                with act.Fori(0, FT) as ft:
                    rwkv_act(n * FT + ft, ft, (n, NT - n))
            act.wait_ge(yd_zeroed, 16)
            S = s_tail.act
            act.sem_inc(*S.open())

            act.sem_inc(*s_mix.act.open())

            def mix_act(it):
                Q = s_mix.act
                Q.begin(it)
                act.wait_ge(*s_mix.dve.at("yc", it))
                nc.scalar.activation(tb, ta, ACT.Square).then_inc(*Q.tick("ysq"))
                act.wait_ge(*s_mix.dve.at("var", it))
                nc.scalar.activation(t_st[:, 16:28], t_st[:, 16:28], ACT.Sqrt).then_inc(*Q.tick("sd"))

            def tail_act(it, more):
                S.begin(it)
                act.wait_ge(*S.so_far())
                for b in range(2):
                    act.wait_ge(*s_tail.pe.at(f"oT{b}", it))
                    nc.scalar.copy(oT[:, 4 * b:4 * b + 4, :], ps[1 + b][:, :].rearrange("p (k n) -> p k n", n=P)).then_inc(*S.tick(f"oT{b}"))
                if more:
                    mix_act(it + 1)
                act.wait_ge(*s_tail.dve.at("x2", it))
                nc.scalar.activation(oT.rearrange("p k n -> p (k n)"), xf[:, bass.ds(it * D, D)], ACT.Square, accum_out=t_st[:, 32:33]).then_inc(*S.tick("ssq"))
                act.wait_ge(*s_tail.dve.at("var2", it))
                nc.scalar.activation(t_st[:, 33:34], t_st[:, 33:34], ACT.Sqrt).then_inc(*S.tick("sd2"))
                for b in range(2):
                    act.wait_ge(*s_tail.pe.at(f"h2T{b}", it))
                    nc.scalar.copy(h2T[:, 4 * b:4 * b + 4, :], ps[5 + b][:, :].rearrange("p (k n) -> p k n", n=P)).then_inc(*S.tick(f"h2T{b}"))
                act.wait_ge(*s_tail.dve.at("gmax", it))
                nc.scalar.activation(lt_[:, 0:4], lg[:, 0:4], ACT.Exp, bias=lt_[:, 4:5], accum_out=lt_[:, 5:6]).then_inc(*S.tick("gsum"))
                act.wait_ge(*s_tail.dve.at("e2", it))
                nc.scalar.activation(lt_[:, 6:7], lt_[:, 6:7], ACT.Exp).then_inc(*S.tick("e2"))

            xf = x[:, :, :].rearrange("p t n -> p (t n)")
            mix_act(0)
            tail_act(0, True)
            with act.Fori(1, NT - 1) as t:
                tail_act(t, True)
            tail_act(NT - 1, False)
            act.wait_ge(tok_out, 16 * 2 * NT)
            act.dma_start(tok_i, tokd.rearrange("(b s) o -> s (b o)", s=BT)).then_inc(tok_in, 16)
            act.wait_ge(*s_route.dve.at("eb"))
            n_blocks = act.value_load(eb_i[0:1, NB:NB + 1], min_val=0, max_val=NB)
            S = s_moe.act
            act.sem_inc(*S.open())
            with act.Fori(0, NB // 2) as j:
                S.begin(j)
                for u in range(2):
                    with act.If(j * 2 + u < n_blocks):
                        act.wait_ge(*s_moe.pe.at(f"gate{u}", j))
                        nc.scalar.activation(e_h[u], ps[2][:, 0:256], ACT.Silu).then_inc(*S.tick(f"silu{u}"))
                        act.wait_ge(*s_moe.dve.at(f"y{u}", j))
                        for h in range(2):
                            act.dma_start(yd[bass.ds((j * 2 + u) * BT, BT), 512 * h:512 * (h + 1)], e_y[u][BT * h:BT * (h + 1), :]).then_inc(y_out[u], 16)
                    act.end_ifs()
            S = s_fin.act
            for t in range(NT):
                act.wait_ge(*s_fin.dve.at(f"x{t}"))
                nc.scalar.activation(comb(0), x[:, t, :], ACT.Square, accum_out=ssq[:, t:t + 1]).then_inc(*S.tick(f"ssq{t}"))
                act.wait_ge(*s_fin.dve.at(f"var{t}"))
                nc.scalar.activation(std[:, t:t + 1], std[:, t:t + 1], ACT.Sqrt).then_inc(*S.tick(f"sd{t}"))

        @block.vector
        def _(dve):
            S = s_norm.dve
            dve.wait_ge(*s_norm.act.at("cexp"))
            nc.vector.tensor_scalar(cexp, cexp, 1.0, None, ALU.add).then_inc(*S.tick())
            dve.wait_ge(*S.so_far())
            nc.vector.reciprocal(cexp, cexp).then_inc(*S.tick())
            dve.wait_ge(*S.so_far())
            nc.vector.tensor_tensor(silc.rearrange("p k c -> p c k"), craw, cexp, ALU.mult).then_inc(*S.tick("silc"))
            S = s_ada.dve
            dve.sem_inc(*S.open())
            dve.wait_ge(bias_in, 16)
            with dve.Fori(0, A_USES) as j:
                S.begin(j)
                for u in range(2):
                    dve.wait_ge(ring_used[u], j + 1)
                    row = modrow[:, bass.ds(j * 2 * COLS + COLS * u, COLS)]
                    nc.vector.tensor_tensor(row, row, ps[u][0:2, :], ALU.add).then_inc(*S.tick(f"row{u}"))
            S = s_norm.dve
            dve.wait_ge(*s_norm.act.at(f"ssq{NT - 1}"))
            nc.vector.tensor_scalar(std, ssq, 1.0 / D, NORM_EPS, ALU.mult, ALU.add).then_inc(*S.tick("var"))
            dve.wait_ge(*s_norm.act.at("std"))
            nc.vector.reciprocal(rstd, std).then_inc(*S.tick())
            dve.wait_ge(*s_ada.act.at("bc11", A_USES - 1))
            dve.wait_ge(gain_in, 16)
            for c in range(2):
                nc.vector.scalar_tensor_tensor(moda[:, c, 1, :], moda[:, c, 1, :], 1.0, bias_row[:, :], ALU.add, ALU.mult).then_inc(*S.tick())
            dve.wait_ge(*S.so_far())
            for t in range(NT):
                c = min(t, 1)
                if t >= 2:
                    dve.wait_ge(*s_norm.pe.at(f"hT{t - 2}1"))
                hr = hrow if t % 2 == 0 else hrow2
                nc.vector.scalar_tensor_tensor(hr, x[:, t, :], rstd[:, t:t + 1], moda[:, c, 1, :], ALU.mult, ALU.mult).then_inc(*S.tick())
                dve.wait_ge(*S.so_far())
                nc.vector.tensor_tensor(hr, hr, moda[:, c, 0, :], ALU.add).then_inc(*S.tick(f"h{t}"))
            S = s_fm.dve
            dve.sem_inc(*S.open())
            with dve.Fori(0, 2) as j:
                S.begin(j)
                for job in range(8):
                    dve.wait_ge(*s_fm.pe.at(f"p{job}", j))
                    nc.vector.tensor_copy(flat(fm[:, :, :])[:, bass.ds(j * 8 * TOK + job * TOK + HALF, HALF)], ps[2 * (job % 2) + 1][:, 0:HALF]).then_inc(*S.tick(f"d{job}"))
            fmd = flat(fm[:, :, :])
            S = s_conv.dve
            dve.sem_inc(*S.open())
            dve.wait_ge(par_in, 16 * 12)
            cwf = cw[:, :, :].rearrange("p a b -> p (a b)")
            dve.wait_ge(*s_fm.act.at("a7", 1))
            dve.wait_ge(*s_fm.dve.at("d7", 1))

            def conv_dve(j):
                S.begin(j)
                for u in range(2):
                    src = fmd[:, bass.ds((j * 2 + u) * TOK + FM_Q2 * TOK, TOK)]
                    rows = src.rearrange("p (r c) -> p r c", c=ROW)
                    cv = scr[:, u, :]
                    cvr = cv.rearrange("p (r c) -> p r c", c=ROW)
                    taps = hst[:, 4 * u:4 * u + 3]
                    dve.wait_ge(*S.so_far())
                    dve.wait_ge(*s_conv.act.at(f"out{u}", j, 1))
                    dve.wait_ge(*S.at(f"cv{u}", j, 1))
                    dve.sem_inc(waited, 1)
                    nc.vector.tensor_copy(taps, cwf[:, bass.ds((j * 2 + u) * 4, 3)]).then_inc(*S.tick())
                    dve.wait_ge(*S.so_far())
                    nc.vector.tensor_scalar(cv, src, taps[:, 1:2], None, ALU.mult).then_inc(*S.tick())
                    dve.wait_ge(*S.so_far())
                    nc.vector.scalar_tensor_tensor(cvr[:, :, 1:], rows[:, :, :-1], taps[:, 0:1], cvr[:, :, 1:], ALU.mult, ALU.add).then_inc(*S.tick())
                    dve.wait_ge(*S.so_far())
                    nc.vector.scalar_tensor_tensor(cvr[:, :, :-1], rows[:, :, 1:], taps[:, 2:3], cvr[:, :, :-1], ALU.mult, ALU.add).then_inc(*S.tick())
                    dve.wait_ge(*S.so_far())
                    nc.vector.scalar_tensor_tensor(cv[:, ROW:ROW + 1], rows[:, 0, ROW - 1:ROW], taps[:, 0:1], cv[:, ROW:ROW + 1], ALU.mult, ALU.add).then_inc(*S.tick())
                    nc.vector.scalar_tensor_tensor(cv[:, ROW - 1:ROW], rows[:, 1, 0:1], taps[:, 2:3], cv[:, ROW - 1:ROW], ALU.mult, ALU.add).then_inc(*S.tick(f"cv{u}"))

            with dve.Fori(0, 4) as j:
                conv_dve(j)
            dve.wait_ge(*s_tm.act.at("c3"))
            with dve.Fori(4, 6) as j:
                conv_dve(j)
            S = s_prep.dve
            dve.wait_ge(*s_tm.act.at(f"t{NT - 1}"))
            dtb = par[:, 56:64].unsqueeze(1).to_broadcast([P, NT, 8])
            nc.vector.tensor_tensor(gtmp[:, 2], ba[:, :, 8:16], dtb, ALU.add).then_inc(*S.tick("xa"))
            dve.wait_ge(*s_prep.act.at("ebeta"))
            nc.vector.tensor_scalar(gtmp[:, 0], gtmp[:, 0], 1.0, None, ALU.add).then_inc(*S.tick())
            dve.wait_ge(*s_prep.act.at("ln"))
            nc.vector.tensor_scalar(gtmp[:, 2], gtmp[:, 2], 0.0, None, ALU.max).then_inc(*S.tick())
            dve.wait_ge(*S.so_far())
            nc.vector.tensor_tensor(gtmp[:, 2], gtmp[:, 2], gtmp[:, 1], ALU.add).then_inc(*S.tick())
            nc.vector.reciprocal(gtmp[:, 3], gtmp[:, 0]).then_inc(*S.tick())
            dve.wait_ge(*s_prep.act.at("alog"))
            dve.wait_ge(*S.so_far())
            nc.vector.scalar_tensor_tensor(gtmp[:, 2], gtmp[:, 2], -1.0, par[:, 48:56].unsqueeze(1).to_broadcast([P, NT, 8]), ALU.mult, ALU.mult).then_inc(*S.tick("g"))
            for d in range(2):
                nc.vector.tensor_scalar(gs[:, d, :, :, 2], gtmp[:, 3, :, 4 * d:4 * d + 4], -1.0, None, ALU.mult).then_inc(*S.tick())
                nc.vector.tensor_copy(gs[:, d, :, :, 3], gtmp[:, 3, :, 4 * d:4 * d + 4]).then_inc(*S.tick())
            S = s_l2.dve
            dve.sem_inc(*S.open())
            dve.wait_ge(*s_conv.act.at("out1", 5))
            for g0 in range(2):
                with dve.Fori(4 * g0, 4 * g0 + 4) as j:
                    S.begin(j)
                    src = fmd[:, bass.ds(j * TOK + FM_Q2 * TOK, TOK)]
                    dve.wait_ge(*s_l2.act.at("rs", j))
                    nc.vector.scalar_tensor_tensor(src, src, GD ** -0.5 if g0 == 0 else 1.0, scr[:, 1, :], ALU.mult, ALU.mult).then_inc(*S.tick("out"))
            S = s_prep.dve
            dve.wait_ge(*s_prep.act.at("negeg"))
            for d in range(2):
                nc.vector.tensor_scalar(gs[:, d, :, :, 1], gs[:, d, :, :, 1], -1.0, None, ALU.mult).then_inc(*S.tick("gs"))
            S = s_gdn.dve
            dve.sem_inc(*S.open())
            dve.wait_ge(*s_prep.dve.at("gs"))
            gsf = gs[:, :, :, :, :].rearrange("p d t h n -> p (d t h n)")

            def gdn_dve(it, hp, tiles):
                S.begin(it)
                dve.wait_ge(*S.so_far())
                dve.wait_ge(*s_gdn.act.at("w1", it, 1))
                for d in range(2):
                    nc.vector.tensor_copy(g_sc[:, 2 * d:2 * d + 2, :].rearrange("p s n -> p (s n)"),
                                          gsf[:, bass.ds((tiles[d] + NT * d) * (4 * GH) + hp * 8, 8)]).then_inc(*S.tick())
                dve.wait_ge(*S.so_far())
                dve.wait_ge(*s_gdn.pe.at("grow", it))
                for s_ in range(4):
                    nc.vector.tensor_scalar(g_et[:, s_, :], ps[0][:, P * s_:P * (s_ + 1)], g_sc[:, s_, 0:1], 0.0, ALU.subtract, ALU.min).then_inc(*S.tick("dif"))
                dve.wait_ge(*s_gdn.act.at("et", it))
                for d in range(2):
                    nc.vector.tensor_tensor(pair(g_et, d), pair(g_et, d), two(incl(d)), ALU.mult).then_inc(*S.tick("etm"))
                dve.wait_ge(*S.so_far())
                dve.wait_ge(*s_gdn.pe.at("scores", it))
                for s_ in range(4):
                    nc.vector.scalar_tensor_tensor(g_lt[:, s_, :], ps[1 + s_ // 2][:, 256 * (s_ % 2):256 * (s_ % 2) + P], g_sc[:, s_, 2:3], g_et[:, s_, :], ALU.mult, ALU.mult).then_inc(*S.tick())
                for d in range(2):
                    nc.vector.tensor_tensor(g_qk[:, 2 * d:2 * d + 2, 0:P], ps[1 + d][:, :].rearrange("p (s n) -> p s n", s=2)[:, :, P:2 * P], pair(g_et, d), ALU.mult).then_inc(*S.tick("qk"))
                dve.wait_ge(*S.so_far())
                for d in range(2):
                    inverse_dve_start(dve, S, d, pair(g_lt, d))
                inverse_dve(dve, S, s_gdn, it)
                dve.wait_ge(*s_gdn.pool.at("qd", it))
                for d in range(2):
                    dve.wait_ge(*s_gdn.pe.at(f"c{d}", it))
                    cp = ps[d][:, :].rearrange("p (s n) -> p s n", s=2)
                    nc.vector.tensor_tensor(pair(g_q1, d), cp[:, :, 0:P], pair(g_eg, d), ALU.add).then_inc(*S.tick("q1"))
                    for hh in range(2):
                        s_ = 2 * d + hh
                        nc.vector.scalar_tensor_tensor(g_t1[:, s_, :], ident, g_egl[:, s_:s_ + 1], cp[:, hh, P:2 * P], ALU.mult, ALU.add).then_inc(*S.tick("t1"))
                dve.wait_ge(*s_gdn.pe.at("y", it))
                for d in range(2):
                    yv = y_gf[:, bass.ds(tiles[d] * 512 + hp * 256, 256)]
                    nc.vector.tensor_tensor(yv, yv, ps[2][:, 256 * d:256 * (d + 1)], ALU.add).then_inc(*S.tick())
                    dve.wait_ge(*S.so_far())
                dve.wait_ge(*s_gdn.pe.at("t2", it))
                for d in range(2):
                    nc.vector.tensor_copy(g_state[:, d, bass.ds(hp * 256, 256)], ps[3][:, 256 * d:256 * (d + 1)]).then_inc(*S.tick("state"))

            y_gf = hTf[:, 2560:5120]
            dve.wait_ge(zeroed, 3)
            with dve.Fori(0, 2) as hp:
                gdn_dve(hp, hp, (0, 0))
            dve.wait_ge(state_in, 32)
            with dve.Fori(1, NT) as n:
                with dve.Fori(0, 2) as hp:
                    gdn_dve(n * 2 + hp, hp, (n, NT - n))
            dve.wait_ge(yd_zeroed, 16)
            S = s_kk.dve
            dve.wait_ge(*s_gdn.pe.at("t2", 2 * NT - 1))
            dve.wait_ge(*s_gp.pool.at("copies", 2 * NT))
            dve.wait_ge(*s_l2.dve.at("out", 7))
            nc.vector.tensor_scalar(rpar[:, :, 6], rpar[:, :, 5], -1.0, 1.0, ALU.mult, ALU.add).then_inc(waited, 1)
            nc.vector.tensor_scalar(rpar[:, :, 0:4], rpar[:, :, 0:4], -1.0, None, ALU.mult).then_inc(waited, 1)
            for j in range(FT):
                nc.vector.tensor_scalar(fm[:, FM_Q2 + j, :], fm[:, FM_K + j, :], rpar[:, j, 4:5], None, ALU.mult).then_inc(*S.tick(f"raw{j}"))
            dve.wait_ge(*s_kk.act.at("rs"))
            nc.vector.tensor_tensor(fm[:, FM_Q2:FM_Q2 + FT, :], fm[:, FM_Q2:FM_Q2 + FT, :], kk_root, ALU.mult).then_inc(*S.tick("out"))
            dve.wait_ge(*S.so_far())
            S = s_rwkv.dve
            dve.sem_inc(*S.open())
            dve.wait_ge(rzero, 2)
            bonusf = bonus[:, :, :].rearrange("p t h -> p (t h)")

            Q = s_rp.dve
            dve.sem_inc(*Q.open())

            def prep_dve_start(it):
                Q.begin(it)
                dve.wait_ge(*s_rp.act.at("eu", it))
                nc.vector.tensor_scalar(r_eu, r_eu, 1.0, None, ALU.add).then_inc(*Q.tick())
                dve.wait_ge(*Q.so_far())

            def prep_dve_gates(n):
                nc.vector.reciprocal(r_eu[:, n, :], r_eu[:, n, :]).then_inc(*Q.tick("gates"))

            def prep_dve_sums(it):
                dve.wait_ge(*Q.so_far())
                dve.wait_ge(*s_rp.act.at("h", it, 1))
                for d in range(2):
                    nc.vector.tensor_tensor_scan(r_cs[:, d, :], ones, r_eu[:, d, :], 0.0, ALU.mult, ALU.add).then_inc(*Q.tick())
                dve.wait_ge(*Q.so_far())
                nc.vector.tensor_scalar(r_ht, r_cs[:, :, P - 1], 0.5, None, ALU.mult).then_inc(*Q.tick())
                dve.wait_ge(*Q.so_far())
                for d in range(2):
                    nc.vector.tensor_scalar(r_pq[:, d, :], r_cs[:, d, :], r_ht[:, d:d + 1], None, ALU.subtract).then_inc(*Q.tick())
                dve.wait_ge(*Q.so_far())
                nc.vector.tensor_tensor(r_pq[:, 2:4, :], r_pq[:, 0:2, :], r_eu[:, 0:2, :], ALU.subtract).then_inc(*Q.tick("pq"))

            def prep_dve_products(it, ft, tiles):
                dve.wait_ge(*s_rwkv.pe.at("atm", it, 1))
                dve.wait_ge(*s_rwkv.pool.at("keep", it, 1))
                dve.wait_ge(*s_rp.act.at("ex3", it))
                dve.sem_inc(waited, 1)
                for d in range(2):
                    kkn = fmd[:, bass.ds(ft * TOK + tiles[d] * P + FM_Q2 * TOK, P)]
                    rr_ = fmd[:, bass.ds(ft * TOK + tiles[d] * P + FM_R * TOK, P)]
                    nc.vector.tensor_tensor(r_ar[:, d, 0:P], kkn, r_ex[:, d, :], ALU.mult).then_inc(*Q.tick())
                    nc.vector.tensor_tensor(r_ar[:, d, P:2 * P], rr_, r_ex[:, 2 + d, :], ALU.mult).then_inc(*Q.tick())
                dve.wait_ge(*s_rp.act.at("h", it))
                dve.wait_ge(*s_rp.pool.at("kd", it))
                nc.vector.scalar_tensor_tensor(r_bk[:, 0:2, :], r_kka, -1.0, r_ex[:, 4:6, :], ALU.mult, ALU.mult).then_inc(*Q.tick())
                nc.vector.tensor_tensor(r_bk[:, 2:4, :], r_kd, r_ex[:, 4:6, :], ALU.mult).then_inc(*Q.tick("bk"))

            def rwkv_dve(it, ft, tiles):
                S.begin(it)
                nft, ntiles = next_of(dve, it, tiles)
                dve.wait_ge(*S.so_far())
                dve.wait_ge(*s_rp.act.at("h", it))
                nc.vector.tensor_copy(r_hc, r_h).then_inc(*S.tick("hc"))
                dve.wait_ge(*S.so_far())
                for d in range(2):
                    dve.wait_ge(*s_rwkv.pe.at(f"scores{d}", it))
                    for hh in range(2):
                        s_ = 2 * d + hh
                        nc.vector.tensor_tensor(r_sc[:, s_, :].rearrange("p (a b) -> p a b", b=320)[:, :, 0:256], ps[2 + s_][:, :].rearrange("p (a b) -> p a b", a=2),
                                                tab[:, T_MASK + 512 * d:T_MASK + 512 * (d + 1)].rearrange("p (a b) -> p a b", a=2), ALU.mult).then_inc(*S.tick("sc"))
                    dve.wait_ge(*S.so_far())
                    inverse_dve_start(dve, S, d, r_sc[:, 2 * d:2 * d + 2, 0:P])
                dve.wait_ge(*s_rwkv.act.at("tm", it))
                for d in range(2):
                    bv = bonusf[:, bass.ds(tiles[d] * RH + ft * 2, 2)]
                    nc.vector.tensor_tensor(bv, bv, ps[1][:, 256 + 2 * d:258 + 2 * d], ALU.add).then_inc(*S.tick("bonus"))
                    nc.vector.tensor_scalar(r_zin[:, d, :], zst[:, bass.ds(ft * RD + 256 * d, RD)], r_hc[:, d:d + 1], None, ALU.mult).then_inc(*S.tick())
                    dve.wait_ge(*S.so_far())
                    dve.sem_inc(waited, 1)
                def first():
                    prep_dve_start(it + 1)
                    prep_dve_gates(0)

                def last():
                    prep_dve_gates(3)
                    prep_dve_sums(it + 1)
                inverse_dve(dve, S, s_rwkv, it, {2: first, 3: lambda: (prep_dve_gates(1), prep_dve_gates(2)), 4: last,
                                                 6: lambda: prep_dve_products(it + 1, nft, ntiles)})
                dve.wait_ge(*s_rwkv.pool.at("keep", it))
                for d in range(2):
                    dve.wait_ge(*s_rwkv.pe.at(f"c{d}", it))
                    nc.vector.tensor_tensor(r_q1[:, d, :], ps[d][:, 0:P], r_keep[:, d, :], ALU.add).then_inc(*S.tick())
                    nc.vector.tensor_tensor(r_t1[:, d, :], ps[d][:, P:P + RD], tab[:, T_EYE:T_EYE + RD], ALU.add).then_inc(*S.tick("t1"))
                dve.wait_ge(*s_rwkv.pe.at("y", it))
                for d in range(2):
                    for hh in range(2):
                        yv = y_r[:, bass.ds(tiles[d] * RW + ft * P + RD * hh, RD)]
                        nc.vector.tensor_tensor(yv, yv, ps[(2, 5)[hh]][:, RD * d:RD * (d + 1)], ALU.add).then_inc(*S.tick())
                    dve.wait_ge(*S.so_far())
                dve.wait_ge(*s_rwkv.pe.at("t2", it))
                for hh in range(2):
                    rows = slice(RD * hh, RD * (hh + 1))
                    for d in range(2):
                        nc.vector.tensor_scalar(r_zn[rows, d, :], ps[3 + hh][rows, RD * d:RD * (d + 1)], r_hc[rows, d:d + 1], None, ALU.mult).then_inc(*S.tick())
                dve.wait_ge(*S.so_far())
                dve.sem_inc(waited, 1)
                for d in range(2):
                    nc.vector.tensor_copy(zst[:, bass.ds(ft * RD + 256 * d, RD)], r_zn[:, d, :]).then_inc(*S.tick("last"))

            prep_dve_start(0)
            for q in range(4):
                prep_dve_gates(q)
            prep_dve_sums(0)
            prep_dve_products(0, 0, (0, 0))
            with dve.Fori(0, FT) as ft:
                rwkv_dve(ft, ft, (0, 0))
            dve.wait_ge(*s_zs.act.at("zst"))
            with dve.Fori(1, NT) as n:
                with dve.Fori(0, FT) as ft:
                    rwkv_dve(n * FT + ft, ft, (n, NT - n))
            S = s_tail.dve
            dve.sem_inc(*S.open())
            dve.wait_ge(cst_in, 16 * 9)
            dve.wait_ge(*s_route.act.at("silz"))
            for c in range(2):
                nc.vector.scalar_tensor_tensor(modk[:, c, 2, :], modk[:, c, 2, :], 1.0, bias_row[:, :], ALU.add, ALU.mult).then_inc(*s_route.dve.tick("gain2"))
            dve.wait_ge(*s_route.dve.so_far())
            xd, zd, vd = x[:, :, :].rearrange("p t n -> p (t n)"), z_tm[:, :, :].rearrange("p t n -> p (t n)"), v_tm[:, :, :].rearrange("p t n -> p (t n)")
            b3 = lambda ap, n: ap.unsqueeze(2).to_broadcast([P, ap.shape[-1], n])
            ohd, ohsd, gad = scr[:, 0, :], scr[:, 1, 0:NT * NE], scr[:, 1, 2 * NT * NE:2 * NT * NE + 2 * NT]

            dve.sem_inc(*s_mix.dve.open())

            def mix_dve(it):
                Q = s_mix.dve
                Q.begin(it)

                def then(ins, name=None):
                    ins.then_inc(*Q.tick(name))
                    dve.wait_ge(*Q.so_far())
                then(nc.vector.tensor_copy(t_sgl, fmd[:, bass.ds(it * P + (FM_LORA + 1) * TOK, P)]), "sgl")
                y3 = y_r[:, bass.ds(it * RW, RW)].rearrange("p (h n) -> p h n", n=RD)
                ta3, tb3 = ta.rearrange("p (h n) -> p h n", n=RD), tb.rearrange("p (h n) -> p h n", n=RD)
                then(nc.vector.tensor_reduce(t_st[:, 0:8], y3, AX.X, ALU.add))
                then(nc.vector.tensor_scalar(t_st[:, 0:8], t_st[:, 0:8], 1.0 / RD, None, ALU.mult))
                then(nc.vector.tensor_tensor(ta3, y3, b3(t_st[:, 0:8], RD), ALU.subtract), "yc")
                dve.wait_ge(*s_mix.act.at("ysq", it))
                then(nc.vector.tensor_reduce(t_st[:, 8:16], tb3, AX.X, ALU.add))
                then(nc.vector.tensor_scalar(t_st[:, 16:24], t_st[:, 8:16], 1.0 / RD, LNX_EPS, ALU.mult, ALU.add))
                yg = y_gf[:, bass.ds(it * 512, 512)]
                then(nc.vector.tensor_tensor(tb, yg, yg, ALU.mult))
                then(nc.vector.tensor_reduce(t_st[:, 8:12], tb.rearrange("p (h n) -> p h n", n=GD), AX.X, ALU.add))
                then(nc.vector.tensor_scalar(t_st[:, 24:28], t_st[:, 8:12], 1.0 / GD, NORM_EPS, ALU.mult, ALU.add), "var")
                dve.wait_ge(*s_mix.act.at("sd", it))
                then(nc.vector.reciprocal(t_st[:, 16:28], t_st[:, 16:28]))
                then(nc.vector.tensor_tensor(ta3, ta3, b3(t_st[:, 16:24], RD), ALU.mult))
                then(nc.vector.tensor_tensor(ta, ta, lnx_g, ALU.mult))
                then(nc.vector.tensor_tensor(ta, ta, lnx_b, ALU.add))
                then(nc.vector.tensor_copy(t_st[:, 8:16], bonusf[:, bass.ds(it * RH, RH)]))
                then(nc.vector.tensor_tensor(tb3, vd[:, bass.ds(it * RW, RW)].rearrange("p (h n) -> p h n", n=RD), b3(t_st[:, 8:16], RD), ALU.mult))
                then(nc.vector.tensor_tensor(ta, ta, tb, ALU.add))
                dve.wait_ge(*s_mix.pe.at("gate", it))
                dve.wait_ge(*s_tail.pe.at("oT1", it, 1))
                then(nc.vector.tensor_tensor(o_tm[:, 0:RW], ta, ps[0][:, :], ALU.mult), "gn")
                then(nc.vector.tensor_tensor(tb.rearrange("p (h n) -> p h n", n=GD), yg.rearrange("p (h n) -> p h n", n=GD), b3(t_st[:, 24:28], GD), ALU.mult))
                then(nc.vector.tensor_tensor(tb.rearrange("p (h n) -> p h n", n=GD), tb.rearrange("p (h n) -> p h n", n=GD), gng.unsqueeze(1).to_broadcast([P, GH, GD]), ALU.mult))
                then(nc.vector.tensor_tensor(o_tm[:, RW:D], tb, zd[:, bass.ds(it * RW, RW)], ALU.mult), "o")

            def tail_dve(it, c, more=True):
                S.begin(it)
                if more:
                    mix_dve(it + 1)
                dve.wait_ge(*S.so_far())
                dve.sem_inc(waited, 1)

                def then(ins, name=None):
                    ins.then_inc(*S.tick(name))
                    dve.wait_ge(*S.so_far())
                for b in range(2):
                    dve.wait_ge(*s_tail.pe.at(f"mix{b}", it))
                    then(nc.vector.tensor_tensor(ta, ps[3 + b][:, :], modk[:, c, 0, 512 * b:512 * (b + 1)], ALU.mult))
                    xb = xd[:, bass.ds(it * D + 512 * b, 512)]
                    then(nc.vector.tensor_tensor(xb, xb, ta, ALU.add), "x2")
                dve.wait_ge(*s_tail.act.at("ssq", it))
                then(nc.vector.tensor_scalar(t_st[:, 33:34], t_st[:, 32:33], 1.0 / D, NORM_EPS, ALU.mult, ALU.add), "var2")
                dve.wait_ge(*s_tail.act.at("sd2", it))
                then(nc.vector.reciprocal(t_st[:, 34:35], t_st[:, 33:34]))
                if c:
                    dve.wait_ge(h2_out, it * 16)
                then(nc.vector.scalar_tensor_tensor(h2, xd[:, bass.ds(it * D, D)], t_st[:, 34:35], modk[:, c, 2, :], ALU.mult, ALU.mult))
                then(nc.vector.tensor_tensor(h2, h2, modk[:, c, 1, :], ALU.add), "h2")
                dve.wait_ge(*s_tail.pe.at("logits", it))
                then(nc.vector.memset(lg[:, 0:8], -BIG))
                then(nc.vector.tensor_tensor(lg[:, 0:4], ps[7][:, 0:GROUPS], rtb[:, 0:GROUPS], ALU.add))
                then(nc.vector.tensor_tensor(el, ps[7][:, GROUPS:GROUPS + NE], rtb[:, GROUPS:], ALU.add))
                dve.sem_inc(waited, 1)
                then(nc.vector.max(m8, lg[:, 0:8]))
                dve.sem_inc(waited, 1)
                then(nc.vector.max_index(mi8.bitcast(mybir.dt.uint32), m8, lg[:, 0:8]))
                then(nc.vector.tensor_scalar(lt_[:, 4:5], m8[:, 0:1], -1.0, None, ALU.mult), "gmax")
                then(nc.vector.tensor_copy(lt_[:, 7:8], mi8[:, 0:1]))
                then(nc.vector.tensor_scalar(lt_[:, 8:12], tab[:, T_IOTA:T_IOTA + GROUPS], lt_[:, 7:8], None, ALU.is_equal))
                then(nc.vector.tensor_scalar(lt_[:, 12:16], lt_[:, 8:12], BIG, -BIG, ALU.mult, ALU.add))
                el3, el23 = el.rearrange("p (g n) -> p g n", n=PER_GROUP), el2.rearrange("p (g n) -> p g n", n=PER_GROUP)
                then(nc.vector.tensor_tensor(el23, el3, b3(lt_[:, 8:12], PER_GROUP), ALU.mult))
                then(nc.vector.tensor_tensor(el23, el23, b3(lt_[:, 12:16], PER_GROUP), ALU.add))
                dve.sem_inc(waited, 1)
                then(nc.vector.max(m8, el2))
                dve.sem_inc(waited, 1)
                then(nc.vector.max_index(mi8.bitcast(mybir.dt.uint32), m8, el2))
                dve.wait_ge(*s_tail.act.at("gsum", it))
                then(nc.vector.tensor_tensor(lt_[:, 6:7], m8[:, 1:2], m8[:, 0:1], ALU.subtract), "e2")
                then(nc.vector.tensor_copy(lt_[:, 8:10], mi8[:, 0:2]))
                for k in range(2):
                    then(nc.vector.tensor_scalar(ohd[:, bass.ds(it * NE + NT * NE * k, NE)], tab[:, T_BIOTA:T_BIOTA + NE], lt_[:, 8 + k:9 + k], None, ALU.is_equal))
                then(nc.vector.tensor_tensor(ohsd[:, bass.ds(it * NE, NE)], ohd[:, bass.ds(it * NE, NE)], ohd[:, bass.ds(it * NE + NT * NE, NE)], ALU.add))
                dve.wait_ge(*s_tail.act.at("e2", it))
                then(nc.vector.tensor_scalar(lt_[:, 10:11], lt_[:, 6:7], 1.0, lt_[:, 5:6], ALU.add, ALU.mult))
                then(nc.vector.reciprocal(lt_[:, 10:11], lt_[:, 10:11]))
                then(nc.vector.tensor_tensor(lt_[:, 11:12], lt_[:, 10:11], lt_[:, 6:7], ALU.mult))
                dve.sem_inc(waited, 1)
                then(nc.vector.tensor_copy(gad[:, bass.ds(it * 2, 2)], lt_[:, 10:12]), "last")

            mix_dve(0)
            tail_dve(0, 0)
            with dve.Fori(1, NT - 1) as t:
                tail_dve(t, 1)
            tail_dve(NT - 1, 1, False)
            S = s_route.dve

            def then(ins, name=None):
                ins.then_inc(*S.tick(name))
                dve.wait_ge(*S.so_far())
            dve.wait_ge(*s_route.pe.at("rank"))
            then(nc.vector.tensor_copy(cnt, ps[0][:, NE * NT:NE * (NT + 1)]))
            big = oT.rearrange("p k n -> p (k n)")[:, 0:NE * 10].rearrange("p (e m) -> p e m", m=10)
            then(nc.vector.tensor_tensor(big, b3(cnt, 10), tab[:, T_THR:T_THR + 10].unsqueeze(1).to_broadcast([P, NE, 10]), ALU.is_gt))
            then(nc.vector.tensor_reduce(nblk, big, AX.X, ALU.add))
            then(nc.vector.tensor_tensor_scan(pend, ones[:, 0:NE], nblk, 0.0, ALU.mult, ALU.add))
            then(nc.vector.tensor_tensor(base, pend, nblk, ALU.subtract))
            then(nc.vector.tensor_scalar(base, base, float(BT), None, ALU.mult))
            then(nc.vector.tensor_tensor(slotm, ps[0][:, 0:NE * NT].rearrange("p (t e) -> p t e", e=NE), base.unsqueeze(1).to_broadcast([P, NT, NE]), ALU.add))
            for k in range(2):
                then(nc.vector.tensor_tensor(oh[:, k], oh[:, k], slotm, ALU.mult))
                then(nc.vector.tensor_reduce(slot_f[:, :, k], oh[:, k], AX.X, ALU.add))
            then(nc.vector.tensor_copy(slot_i, slot_f), "slots")
            big2 = tl[:, 0:NB * NE].rearrange("p (b e) -> p b e", e=NE)
            then(nc.vector.tensor_tensor(big2, pend.unsqueeze(1).to_broadcast([P, NB, NE]), b3(tab[:, T_BIOTA:T_BIOTA + NB], NE), ALU.is_le))
            then(nc.vector.tensor_reduce(ebf, big2, AX.X, ALU.add))
            then(nc.vector.tensor_scalar(ebf, ebf, float(NE - 1), None, ALU.min))
            then(nc.vector.tensor_copy(eb_i[:, NB:NB + 1], pend[:, NE - 1:NE]))
            then(nc.vector.tensor_copy(eb_i[:, 0:NB], ebf), "eb")
            n_blocks = dve.value_load(eb_i[0:1, NB:NB + 1], min_val=0, max_val=NB)
            S = s_moe.dve
            dve.sem_inc(*S.open())
            for u in range(2):
                dve.sem_inc(y_out[u], 32)
            with dve.Fori(0, NB // 2) as j:
                S.begin(j)
                for u in range(2):
                    with dve.If(j * 2 + u < n_blocks):
                        dve.wait_ge(*s_moe.pe.at(f"xT{u}", j))
                        dve.sem_inc(waited, 1)
                        nc.vector.tensor_copy(e_xT[u], ps[u][:, :].rearrange("p (k n) -> p k n", n=BT)).then_inc(*S.tick(f"xT{u}"))
                        dve.wait_ge(*s_moe.act.at(f"silu{u}", j))
                        dve.wait_ge(*s_moe.pe.at(f"up{u}", j))
                        nc.vector.tensor_tensor(e_h[u], e_h[u], ps[3][:, 0:256], ALU.mult).then_inc(*S.tick(f"h{u}"))
                        dve.wait_ge(*s_moe.pe.at(f"hT{u}", j))
                        dve.sem_inc(waited, 1)
                        nc.vector.tensor_copy(e_hT[u], ps[4][:, 0:256].rearrange("p (c h n) -> p c h n", c=2, h=2)).then_inc(*S.tick(f"hT{u}"))
                        dve.wait_ge(*s_moe.pe.at(f"down{u}", j))
                        dve.wait_ge(y_out[u], j * 32 + 32)
                        dve.sem_inc(waited, 1)
                        nc.vector.tensor_copy(e_y[u], ps[5][:, :]).then_inc(*S.tick(f"y{u}"))
                    dve.end_ifs()
            S = s_fin.dve
            dve.wait_ge(fin_in, 16)
            for t in range(NT):
                c = min(t, 1)
                for k in range(2):
                    dve.wait_ge(comb_in[k], 16 * (t + 1))
                then(nc.vector.tensor_scalar(comb(0), comb(0), gates[:, t, 0:1], None, ALU.mult))
                then(nc.vector.scalar_tensor_tensor(comb(2), comb(1), gates[:, t, 1:2], comb(0), ALU.mult, ALU.add))
                then(nc.vector.tensor_tensor(comb(2), comb(2), modk[:, c, 3, :], ALU.mult))
                then(nc.vector.tensor_tensor(x[:, t, :], x[:, t, :], comb(2), ALU.add), f"x{t}")
                dve.wait_ge(*s_fin.act.at(f"ssq{t}"))
                then(nc.vector.tensor_scalar(std[:, t:t + 1], ssq[:, t:t + 1], 1.0 / D, NORM_EPS, ALU.mult, ALU.add), f"var{t}")
                S.book[f"sum{t}"] = S.n
                dve.wait_ge(*s_fin.act.at(f"sd{t}"))
                then(nc.vector.reciprocal(rstd[:, t:t + 1], std[:, t:t + 1]))
                then(nc.vector.scalar_tensor_tensor(x[:, t, :], x[:, t, :], rstd[:, t:t + 1], bias_row[:, :], ALU.mult, ALU.mult), f"out{t}")


INS = ['x_prompt', 'x_sample', 'state_rwkv', 'state_gdn', 'c', 'c_ctx', 'ada_w', 'ada_b', 'norm1_g', 'norm2_g',
       'w_in', 'w_out', 'rwkv_w0', 'rwkv_w2', 'rwkv_a0', 'rwkv_a2', 'rwkv_g2', 'rwkv_k_k', 'rwkv_k_a', 'rwkv_r_k',
       'rwkv_lnx_g', 'rwkv_lnx_b', 'gdn_conv', 'gdn_a_log', 'gdn_dt_bias', 'gdn_norm_g', 'router_group_w',
       'router_group_b', 'router_expert_w', 'router_expert_b', 'expert_gate', 'expert_up', 'expert_down', 'final_norm_g']
OUTS = [('y_prompt', (1, CTX, D)), ('y_sample', (1, LAT, D)), ('new_rwkv', (1, 1, 2, RH, RD, RD)), ('new_gdn', (1, 1, 2, GH, GD, GD))]


def kernel(**inputs):
    import concourse.bacc as bacc
    from concourse.bass_utils import run_bass_kernel_spmd

    arrays = {f"in_{n}": np.ascontiguousarray(inputs[n]) for n in INS}
    arrays["in_tables"] = shape_tables()
    book = {}
    for _ in range(2):
        nc = bacc.Bacc("TRN2", target_bir_lowering=False, num_devices=1)
        A = {n[3:]: nc.dram_tensor(n, a.shape, mybir.dt.from_np(a.dtype), kind="ExternalInput").ap() for n, a in arrays.items()}
        O = {n: nc.dram_tensor(f"out_{n}", shape, F32, kind="ExternalOutput").ap() for n, shape in OUTS}
        program(nc, A, O, book)
    got = run_bass_kernel_spmd(nc, [arrays], core_ids=[0]).results[0]
    return tuple(got[f"out_{n}"] for n, _ in OUTS)
```
